# Optimizing a Trainium2 kernel written in Bass

```python
import jax
import jax.numpy as jnp
from jax import lax
import numpy as np

D_MODEL = 1024
BATCH = 1
SEQ = 256
DEPTH = 2

CTX_LEN = 256
GRID_W = 64
NORM_EPS = 1e-6
N_BRANCHES = 3

GLA_HEADS = 4
GLA_DK = D_MODEL // (2 * GLA_HEADS)
GLA_DV = D_MODEL // GLA_HEADS
GLA_QK = GLA_HEADS * GLA_DK
GLA_V = GLA_HEADS * GLA_DV
GLA_RANK = 16
GLA_TEMP = 16.0
GLA_CHUNK = 64

HEAD_DIM = 128
ATT_Q_HEADS = D_MODEL // HEAD_DIM
ATT_KV_HEADS = ATT_Q_HEADS // 4
ATT_GROUP = ATT_Q_HEADS // ATT_KV_HEADS
ATT_Q = ATT_Q_HEADS * HEAD_DIM
ATT_KV = ATT_KV_HEADS * HEAD_DIM
ROPE_THETA = 10000.0
Q_BLOCK = 128

LRU_WIDTH = D_MODEL
LRU_BLOCKS = 8
LRU_BW = LRU_WIDTH // LRU_BLOCKS
LRU_C = 8.0
LRU_CONV = 4
LRU_CONV_LEFT = 2

D_FF = 2816
FFN_CONV = 3
FFN_CONV_LEFT = 1

IN_SPLITS = (GLA_QK, GLA_QK, GLA_V, GLA_V, GLA_RANK, GLA_RANK,
             ATT_Q, ATT_KV, ATT_KV, LRU_WIDTH, LRU_WIDTH, N_BRANCHES * D_MODEL)
D_IN = 2 * GLA_QK + 2 * GLA_V + 2 * GLA_RANK + ATT_Q + 2 * ATT_KV + 2 * LRU_WIDTH + N_BRANCHES * D_MODEL

kernel_name = "hybrid_gla_gqa_rglru_flow_block"

def rms_norm(x, g):
    xf = x.astype(jnp.float32)
    y = xf * lax.rsqrt(jnp.mean(jnp.square(xf), axis=-1, keepdims=True) + NORM_EPS)
    return (y * g.astype(jnp.float32)).astype(x.dtype)

def modulate(x, shift, scale):
    return x * (1 + scale) + shift

def depthwise_conv(x, w, b, left):
    k = w.shape[0]
    y = lax.conv_general_dilated(
        x, w[:, None, :].astype(x.dtype), window_strides=(1,), padding=[(left, k - 1 - left)],
        dimension_numbers=('NWC', 'WIO', 'NWC'), feature_group_count=x.shape[-1])
    return y + b.astype(x.dtype)

def split_proj(p):
    idx = np.cumsum(IN_SPLITS)[:-1].tolist()
    return jnp.split(p, idx, axis=-1)

def axial_rope_tables(rows):
    row = jnp.repeat(jnp.arange(rows), GRID_W)
    col = jnp.tile(jnp.arange(GRID_W), rows)
    axis_dim = HEAD_DIM // 2
    inv_freq = 1.0 / (ROPE_THETA ** (jnp.arange(0, axis_dim, 2, dtype=jnp.float32) / axis_dim))
    ang = jnp.stack([row, col], axis=-1).astype(jnp.float32)[:, :, None] * inv_freq
    return jnp.cos(ang), jnp.sin(ang)

def apply_rope(x, cos, sin):
    shp = x.shape
    xr = x.astype(jnp.float32).reshape(shp[:-1] + (2, 2, HEAD_DIM // 4))
    x1, x2 = xr[..., 0, :], xr[..., 1, :]
    out = jnp.stack([x1 * cos - x2 * sin, x1 * sin + x2 * cos], axis=-2)
    return out.reshape(shp).astype(x.dtype)

def gla_chunked(q, k, v, log_a, s0):
    b_, h_, n_, _ = q.shape
    dv = v.shape[-1]
    nc = n_ // GLA_CHUNK

    def chunks(t):
        return jnp.moveaxis(t.reshape(b_, h_, nc, GLA_CHUNK, t.shape[-1]), 2, 0)

    q, k, v, log_a = chunks(q), chunks(k), chunks(v), chunks(log_a)
    cum = jnp.cumsum(log_a, axis=-2)
    total = cum[..., -1:, :]
    q_dec = q * jnp.exp(cum)
    k_inv = k * jnp.exp(-cum)
    k_end = k * jnp.exp(total - cum)
    lower_tri = jnp.tril(jnp.ones((GLA_CHUNK, GLA_CHUNK), dtype=bool))

    def step(s, inp):
        qd, ki, ke, vc, tot = inp
        att = jnp.where(lower_tri, jnp.einsum('bhtd,bhsd->bhts', qd, ki), 0.0)
        o = jnp.einsum('bhts,bhsv->bhtv', att, vc) + jnp.einsum('bhtd,bhdv->bhtv', qd, s)
        s = jnp.exp(tot[..., 0, :])[..., None] * s + jnp.einsum('bhsd,bhsv->bhdv', ke, vc)
        return s, o

    s_last, o = lax.scan(step, s0, (q_dec, k_inv, k_end, v, total))
    o = jnp.moveaxis(o, 0, 2).reshape(b_, h_, n_, dv)
    return o, s_last

def gla_output(o, r, g_norm):
    b, h, n, dv = o.shape
    o = rms_norm(jnp.swapaxes(o, 1, 2), g_norm.reshape(h, dv)).reshape(b, n, h * dv)
    return o.astype(r.dtype) * jax.nn.silu(r)

def gla_branch(pc, pl, w_dec, b_dec, g_norm, need_ctx):
    def prep(p):
        q, k, v, r, lr_f, lr_b = p
        b, n, _ = q.shape

        def heads(t, d):
            return jnp.swapaxes(t.reshape(b, n, GLA_HEADS, d), 1, 2).astype(jnp.float32)

        log_a = [heads(jax.nn.log_sigmoid((lr @ w_dec[d] + b_dec[d]).astype(jnp.float32)) / GLA_TEMP, GLA_DK)
                 for d, lr in enumerate((lr_f, lr_b))]
        return heads(q, GLA_DK) * GLA_DK ** -0.5, heads(k, GLA_DK), heads(v, GLA_DV), log_a, r

    qc, kc, vc, lac, rc = prep(pc)
    ql, kl, vl, lal, rl = prep(pl)
    s0 = jnp.zeros(qc.shape[:2] + (GLA_DK, GLA_DV), jnp.float32)
    o_lat, o_ctx = 0.0, 0.0
    for d in range(2):
        f = (lambda t: t) if d == 0 else (lambda t: jnp.flip(t, axis=2))
        oc, sc = gla_chunked(f(qc), f(kc), f(vc), f(lac[d]), s0)
        ol, _ = gla_chunked(f(ql), f(kl), f(vl), f(lal[d]), sc)
        o_lat = o_lat + f(ol)
        o_ctx = o_ctx + f(oc)
    out_l = gla_output(o_lat, rl, g_norm)
    out_c = gla_output(o_ctx, rc, g_norm) if need_ctx else None
    return out_l, out_c

def gqa_attend(q, k, v):
    s = jnp.einsum('bkgqd,bksd->bkgqs', q, k, preferred_element_type=jnp.float32) * HEAD_DIM ** -0.5
    p = jax.nn.softmax(s, axis=-1)
    return jnp.einsum('bkgqs,bksd->bkgqd', p.astype(v.dtype), v)

def merge_heads(o):
    b, h, n, d = o.shape
    return jnp.swapaxes(o, 1, 2).reshape(b, n, h * d)

def attention_branch(pc, pl, g_q, g_k, cos, sin, need_ctx):
    def heads(t, h):
        b, n, _ = t.shape
        return jnp.swapaxes(t.reshape(b, n, h, HEAD_DIM), 1, 2)

    def prep(p):
        q, k, v = p
        return (rms_norm(heads(q, ATT_Q_HEADS), g_q), rms_norm(heads(k, ATT_KV_HEADS), g_k),
                heads(v, ATT_KV_HEADS))

    qc, kc, vc = prep(pc)
    ql, kl, vl = prep(pl)
    ql = apply_rope(ql, cos, sin)
    kl = apply_rope(kl, cos, sin)
    k_all = jnp.concatenate([kc, kl], axis=2)
    v_all = jnp.concatenate([vc, vl], axis=2)
    b, _, n, _ = ql.shape
    qb = ql.reshape(b, ATT_KV_HEADS, ATT_GROUP, n // Q_BLOCK, Q_BLOCK, HEAD_DIM)
    qb = jnp.moveaxis(qb, 3, 0)
    ol = lax.map(lambda q: gqa_attend(q, k_all, v_all), qb)
    ol = jnp.moveaxis(ol, 0, 3).reshape(b, ATT_Q_HEADS, n, HEAD_DIM)
    out_l = merge_heads(ol)
    out_c = None
    if need_ctx:
        nc = qc.shape[2]
        oc = gqa_attend(qc.reshape(b, ATT_KV_HEADS, ATT_GROUP, nc, HEAD_DIM), kc, vc)
        out_c = merge_heads(oc.reshape(b, ATT_Q_HEADS, nc, HEAD_DIM))
    return out_l, out_c

def lru_coeffs(x, w_gates, b_gates, lam):
    b, n, w = x.shape
    xb = x.reshape(b, n, LRU_BLOCKS, LRU_BW)
    z = jnp.einsum('bnhi,ghij->gbnhj', xb, w_gates).reshape(2, b, n, w) + b_gates[:, None, None, :]
    gate_r = jax.nn.sigmoid(z[0].astype(jnp.float32))
    gate_i = jax.nn.sigmoid(z[1].astype(jnp.float32))
    log_a = -LRU_C * gate_r * jax.nn.softplus(-lam.astype(jnp.float32))
    u = jnp.sqrt(-jnp.expm1(2.0 * log_a)) * (gate_i * x.astype(jnp.float32))
    return jnp.exp(log_a), u

def lru_scan(a, u, h0):
    def step(h, au):
        h = au[0] * h + au[1]
        return h, h

    h_last, hs = lax.scan(step, h0, (jnp.swapaxes(a, 0, 1), jnp.swapaxes(u, 0, 1)))
    return jnp.swapaxes(hs, 0, 1), h_last

def rglru_branch(pc, pl, conv_w, conv_b, w_gates, b_gates, lam, need_ctx):
    xc = depthwise_conv(pc[0], conv_w, conv_b, LRU_CONV_LEFT)
    xl = depthwise_conv(pl[0], conv_w, conv_b, LRU_CONV_LEFT)
    h0 = jnp.zeros((xc.shape[0], LRU_WIDTH), jnp.float32)
    h_lat, h_ctx = 0.0, 0.0
    for d in range(2):
        f = (lambda t: t) if d == 0 else (lambda t: jnp.flip(t, axis=1))
        hc, hc_last = lru_scan(*lru_coeffs(f(xc), w_gates[d], b_gates[d], lam[d]), h0)
        hl, _ = lru_scan(*lru_coeffs(f(xl), w_gates[d], b_gates[d], lam[d]), hc_last)
        h_lat = h_lat + f(hl)
        h_ctx = h_ctx + f(hc)
    yl = pl[1]
    out_l = (h_lat * jax.nn.gelu(yl.astype(jnp.float32))).astype(yl.dtype)
    out_c = None
    if need_ctx:
        yc = pc[1]
        out_c = (h_ctx * jax.nn.gelu(yc.astype(jnp.float32))).astype(yc.dtype)
    return out_l, out_c

def merge_branches(branches, gate_logits, w_branch, w_out):
    gates = jnp.split(jax.nn.sigmoid(gate_logits.astype(jnp.float32)).astype(gate_logits.dtype), N_BRANCHES, axis=-1)
    mixed = gates[0] * (branches[0] @ w_branch[0])
    for i in range(1, N_BRANCHES):
        mixed = mixed + gates[i] * (branches[i] @ w_branch[i])
    return mixed @ w_out

def conv_ffn(h, w_up, conv_w, conv_b, w_down):
    u = depthwise_conv(h @ w_up, conv_w, conv_b, FFN_CONV_LEFT)
    g, v = jnp.split(u, 2, axis=-1)
    return (jax.nn.silu(g) * v) @ w_down

def setup_inputs(seed: int = 0) -> dict:
    key = jax.random.key(seed)
    ks = jax.random.split(key, 24)
    f32 = jnp.float32

    def nrm(k, shape, fan_in, gain=1.0):
        return jax.random.normal(k, shape, f32) * (gain * fan_in ** -0.5)

    def small(k, shape, s=0.02):
        return s * jax.random.normal(k, shape, f32)

    u = jax.random.uniform(ks[17], (DEPTH, 2, LRU_WIDTH), f32, 0.9, 0.999)
    s = u ** (1.0 / LRU_C)
    return {
        'x': jax.random.normal(ks[0], (BATCH, SEQ, D_MODEL), f32),
        'c': jax.random.normal(ks[1], (BATCH, D_MODEL), f32),
        'ctx': jax.random.normal(ks[2], (BATCH, CTX_LEN, D_MODEL), f32),
        'c_ctx': jax.random.normal(ks[3], (D_MODEL,), f32),
        'w_ada': nrm(ks[4], (DEPTH, D_MODEL, 6 * D_MODEL), D_MODEL, 0.5),
        'b_ada': small(ks[5], (DEPTH, 6 * D_MODEL)),
        'norm_gains': 1.0 + small(ks[6], (DEPTH, 4, D_MODEL), 0.05),
        'w_in': nrm(ks[7], (DEPTH, D_MODEL, D_IN), D_MODEL),
        'gla_w_decay': nrm(ks[8], (DEPTH, 2, GLA_RANK, GLA_QK), GLA_RANK),
        'gla_b_decay': small(ks[9], (DEPTH, 2, GLA_QK), 0.1),
        'gla_norm_g': 1.0 + small(ks[10], (DEPTH, GLA_V), 0.05),
        'att_q_norm_g': 1.0 + small(ks[11], (DEPTH, HEAD_DIM), 0.05),
        'att_k_norm_g': 1.0 + small(ks[12], (DEPTH, HEAD_DIM), 0.05),
        'lru_conv_w': nrm(ks[13], (DEPTH, LRU_CONV, LRU_WIDTH), LRU_CONV),
        'lru_conv_b': small(ks[14], (DEPTH, LRU_WIDTH)),
        'lru_w_gates': nrm(ks[15], (DEPTH, 2, 2, LRU_BLOCKS, LRU_BW, LRU_BW), LRU_BW),
        'lru_b_gates': small(ks[16], (DEPTH, 2, 2, LRU_WIDTH)),
        'lru_lambda': jnp.log(s) - jnp.log1p(-s),
        'w_branch': nrm(ks[18], (DEPTH, N_BRANCHES, D_MODEL, D_MODEL), D_MODEL),
        'w_out': nrm(ks[19], (DEPTH, D_MODEL, D_MODEL), D_MODEL),
        'ffn_w_up': nrm(ks[20], (DEPTH, D_MODEL, 2 * D_FF), D_MODEL),
        'ffn_conv_w': nrm(ks[21], (DEPTH, FFN_CONV, 2 * D_FF), FFN_CONV),
        'ffn_conv_b': small(ks[22], (DEPTH, 2 * D_FF)),
        'ffn_w_down': nrm(ks[23], (DEPTH, D_FF, D_MODEL), D_FF),
    }

def reference(x, c, ctx, c_ctx, w_ada, b_ada, norm_gains, w_in, gla_w_decay, gla_b_decay, gla_norm_g,
              att_q_norm_g, att_k_norm_g, lru_conv_w, lru_conv_b, lru_w_gates, lru_b_gates, lru_lambda,
              w_branch, w_out, ffn_w_up, ffn_conv_w, ffn_conv_b, ffn_w_down):
    rows = x.shape[1] // GRID_W
    cos, sin = axial_rope_tables(rows)
    for l in range(DEPTH):
        need_ctx = l < DEPTH - 1
        mod_l = jnp.split((jax.nn.silu(c) @ w_ada[l] + b_ada[l])[:, None, :], 6, axis=-1)
        mod_c = jnp.split(jax.nn.silu(c_ctx) @ w_ada[l] + b_ada[l], 6, axis=-1)
        g_pre_mix, g_post_mix, g_pre_ffn, g_post_ffn = norm_gains[l]

        h_l = modulate(rms_norm(x, g_pre_mix), mod_l[0], mod_l[1])
        h_c = modulate(rms_norm(ctx, g_pre_mix), mod_c[0], mod_c[1])
        p_l = split_proj(h_l @ w_in[l])
        p_c = split_proj(h_c @ w_in[l])
        gla_l, gla_c = gla_branch(p_c[0:6], p_l[0:6], gla_w_decay[l], gla_b_decay[l], gla_norm_g[l], need_ctx)
        att_l, att_c = attention_branch(p_c[6:9], p_l[6:9], att_q_norm_g[l], att_k_norm_g[l], cos, sin, need_ctx)
        lru_l, lru_c = rglru_branch(p_c[9:11], p_l[9:11], lru_conv_w[l], lru_conv_b[l], lru_w_gates[l],
                                    lru_b_gates[l], lru_lambda[l], need_ctx)
        y_l = merge_branches((gla_l, att_l, lru_l), p_l[11], w_branch[l], w_out[l])
        x = x + mod_l[2] * rms_norm(y_l, g_post_mix)
        if need_ctx:
            y_c = merge_branches((gla_c, att_c, lru_c), p_c[11], w_branch[l], w_out[l])
            ctx = ctx + mod_c[2] * rms_norm(y_c, g_post_mix)

        h_l = modulate(rms_norm(x, g_pre_ffn), mod_l[3], mod_l[4])
        x = x + mod_l[5] * rms_norm(conv_ffn(h_l, ffn_w_up[l], ffn_conv_w[l], ffn_conv_b[l], ffn_w_down[l]), g_post_ffn)
        if need_ctx:
            h_c = modulate(rms_norm(ctx, g_pre_ffn), mod_c[3], mod_c[4])
            ctx = ctx + mod_c[5] * rms_norm(conv_ffn(h_c, ffn_w_up[l], ffn_conv_w[l], ffn_conv_b[l], ffn_w_down[l]), g_post_ffn)
    return x


_drawn_inputs = setup_inputs


def setup_inputs(seed=0):
    import zlib

    import numpy as np

    out = dict(_drawn_inputs(seed))
    spreads = {}
    factors = {'gla_b_decay': 8.0,
     'gla_norm_g': 7.97,
     'att_q_norm_g': 8.0,
     'att_k_norm_g': 8.0,
     'lru_b_gates': 8.0,
     'ffn_conv_b': 5.448}
    for name, (base, spread) in spreads.items():
        noise = np.random.default_rng([zlib.crc32(name.encode()), seed]).standard_normal(out[name].shape)
        drawn = base * np.exp(spread * noise) if base else spread * noise
        out[name] = jnp.asarray(drawn.astype(out[name].dtype))
    for name, factor in factors.items():
        out[name] = (out[name] * factor).astype(out[name].dtype)
    return out
```

```python
from contextlib import ExitStack

import numpy as np

import concourse.bass as bass
from concourse import mybir

F32 = mybir.dt.float32
F32R = mybir.dt.float32r
I32 = mybir.dt.int32
ALU = mybir.AluOpType
ACT = mybir.ActivationFunctionType
AX_X = mybir.AxisListType.X

P = 128
D_MODEL, SEQ, CTX, DEPTH, GRID_W = 1024, 256, 256, 2, 64
TOK = CTX + SEQ
KT = D_MODEL // P
EPS = 1e-6
HEADS, DK, DV, RANK, TEMP, CHUNK = 4, 128, 256, 16, 16.0, 64
NCH = TOK // CHUNK
AQ, AKV, HD = 8, 2, 128
BLOCKS = 8
D_FF = 2816
FT = D_FF // P
UK, UC = 4, 256
RAW = 4
PLAIN = 2

GLA_QK_PAIRS, GLA_V_PAIRS, R_PAIRS = 4, 4, 4
ATT_Q_PAIRS = 4
DOWN_UNITS = -(-FT // UK)
DOWN_LAST = FT - UK * (DOWN_UNITS - 1)
SPLIT_UNITS = 2 * (GLA_QK_PAIRS + GLA_V_PAIRS + R_PAIRS + 8 + ATT_Q_PAIRS + 2 + 8 + 4 + 4 + 8 + 4 + FT) + 4 * DOWN_UNITS
ADA_UNITS = 6 * D_MODEL // UC * 2
GATE_UNITS = BLOCKS // 2
PLAIN_UNITS = ADA_UNITS + GATE_UNITS

PCOLS = {}
_at = 0
for _n, _w in (("b_ada", 48), ("gains", 32), ("b_dec", 8), ("g_gla", 8), ("g_qk", 10), ("cw", 32), ("cb", 8),
               ("b_gate", 32), ("lam", 16), ("fw", 3 * 2 * FT), ("fb", 2 * FT)):
    PCOLS[_n] = (_at, _at + _w)
    _at += _w
NPAR = _at

CONSTS, READY = 20, 3


class Chain:

    def __init__(self, eng, sem):
        self.eng, self.sem, self.base, self.k, self.i, self.stride = eng, sem, 0, 0, None, 0

    def link(self, ins):
        ins.then_inc(self.sem, 1)
        self.k += 1
        at = self.base + self.k
        self.eng.wait_ge(self.sem, at if self.i is None else self.i * self.stride + at)

    def enter(self, i, stride):
        self.base, self.k, self.i, self.stride = self.base + self.k, 0, i, stride

    def leave(self, times):
        assert self.k == self.stride, (self.k, self.stride)
        self.base, self.k, self.i = self.base + times * self.stride, 0, None


def build(nc, xt, cvec, weights, plain, w_lr, w_dec, params, rope, out):
    with ExitStack() as ctx:
        def sb(name, shape, dt=F32):
            return ctx.enter_context(nc.sbuf_tensor(name, shape, dt))

        def sem(name):
            return ctx.enter_context(nc.semaphore(name))

        ident = sb("ident", [P, P])
        ones = sb("ones", [P, P])
        swap = sb("swap", [P, P])
        cs = sb("cs", [P, 2, SEQ])
        scanmask = sb("scanmask", [P, NCH, CHUNK])
        keep = sb("keep", [P, 2, P])
        par = sb("par", [P, DEPTH, NPAR])
        cin = sb("cin", [P, KT, 2])
        csil = sb("csil", [P, KT, 2])
        mod = sb("mod", [P, ADA_UNITS // 2, 2, 2])
        gmod = sb("gmod", [P, 4, KT, 2])
        hbias = sb("hbias", [P, 32])
        sp = sb("sp", [P, 3, 16])
        wdec = sb("wdec", [2 * RANK, 2, HEADS * DK])
        wdh = sb("wdh", [2 * RANK, 2, DK])
        rstd = sb("rstd", [P, TOK])
        one, eps = sb("one", [P, 1]), sb("eps", [P, 1])
        mx = sb("mx", [P, 4, 2])
        nb = sb("nb", [P, 4, 2])
        sums = sb("sums", [P, 4, 2])
        rsum = sb("rsum", [P, 4, 2])

        SLOT = 4 * TOK
        base = -(-nc.sbuf_base // 64) * 64
        slots = (nc.sbuf_usable_end - base) // SLOT
        ctx.enter_context(nc.sbuf_tensor("arena", [P, slots * TOK], F32, align_bytes=64))

        def at(name, slot, shape, dt=F32, extra=0):
            size = 4 * int(np.prod(shape[1:]))
            assert slot * SLOT + extra + size <= slots * SLOT, (name, slot, size, slots)
            return nc.alloc_sbuf_tensor_at(name, shape, dt, offset=base + slot * SLOT + extra)

        def tiles(name, slot, n, dt=F32):
            return at(name, slot, [P, n, TOK], dt)

        X, H, WR, WS, PL = 0, 8, 24, 32, 40
        M = 44
        B = M + 8
        A = B + 16
        T = A + 16
        x = tiles("x", X, KT)
        hh, hl = tiles("hh", H, KT, F32R), tiles("hl", H + KT, KT, F32R)
        wraw = [at(f"wraw{i}", WR + 2 * i, [P, UK, UC]) for i in range(RAW)]
        whi = [at(f"whi{i}", WS + 2 * i, [P, UK, UC], F32R) for i in range(2)]
        wlo = [at(f"wlo{i}", WS + 4 + 2 * i, [P, UK, UC], F32R) for i in range(2)]
        wpl = [at(f"wpl{i}", PL + 2 * i, [P, UK, UC]) for i in range(PLAIN)]
        mixed = tiles("mixed", M, KT)
        bh, bl = tiles("bh", B, KT, F32R), tiles("bl", B + KT, KT, F32R)
        sq, nt = tiles("sq", B, KT), tiles("nt", B + KT, KT)
        gqk = at("gqk", A, [P, HEADS, 2, TOK])
        gv = at("gv", A + 8, [P, TOK // P, HEADS * DV])
        go = at("go", T + 0, [P, 2, TOK])
        gl_l = tiles("gl_l", B, 2)
        gl_m = tiles("gl_m", B + 2, 2)
        gl_c = tiles("gl_c", B + 4, 2)
        gl_ep = tiles("gl_ep", B + 6, 2)
        gl_ki = tiles("gl_ki", B + 8, 2)
        gl_ke = tiles("gl_ke", B + 10, 2)
        gl_qd = tiles("gl_qd", B + 12, 2)
        lr = at("lr", B + 14, [2 * RANK, TOK])
        state = at("state", M, [P, 2, NCH, DV])
        attm = tiles("attm", T + 2, 2)
        vh = at("vh", T + 4, [P, TOK // P, DV])
        keT = at("keT", T + 6, [P, 2, TOK // P, P])
        gstat = tiles("gstat", T + 8, 1)
        lrw = at("lrw", B, [P, KT, 2 * RANK])
        lrh = at("lrh", B + 2, [P, KT, P], F32R)
        lrl = at("lrl", B + 4, [P, KT, P], F32R)
        ev = [tiles(f"ev{i}", T + 4 * i, 2) for i in range(2)]
        evp = [tiles(f"evp{i}", T + 2 + 4 * i, 2) for i in range(2)]
        aqk = tiles("aqk", A, AQ + AKV)
        av = at("av", A + AQ + AKV, [P, TOK // P, AKV * HD])
        astat = tiles("astat", B, AQ + AKV)
        asq = [tiles(f"asq{i}", T + i, 1) for i in range(2)]
        arot = [at(f"arot{i}", T + 2 + i, [P, 2, SEQ]) for i in range(2)]
        qcur = [tiles(f"qcur{i}", A + 12 + i, 1) for i in range(2)]
        prob = [tiles(f"prob{i}", T + 2 * i, 2) for i in range(2)]
        probT = [at(f"probT{i}", T + 4 + 2 * i, [P, TOK // P, SEQ]) for i in range(2)]
        xc, hsum = tiles("xc", A, BLOCKS), tiles("hsum", A + 8, BLOCKS)
        l_tr, l_ti, l_a, l_th = (tiles(n, B + 4 * i, 4) for i, n in enumerate(("l_tr", "l_ti", "l_a", "l_th")))
        l_a2 = tiles("l_a2", T, 4)
        l_h = tiles("l_h", T + 4, 2)
        mh, ml = tiles("mh", A, KT, F32R), tiles("ml", A + KT, KT, F32R)
        fh, fl = tiles("fh", M, FT, F32R), tiles("fl", M + FT, FT, F32R)
        fa = [tiles(f"fa{i}", M + 2 * FT + 3 * i, 2) for i in range(2)]
        fs = [tiles(f"fs{i}", M + 2 * FT + 2 + 3 * i, 1) for i in range(2)]
        y2 = tiles("y2", H, KT)

        ps = ctx.enter_context(nc.psum_tensor("ps", [P, 8, 512], F32))
        PAIR = [ps[:, 0:2], ps[:, 2:4]]
        KEEP = keep[:].bitcast(I32)
        MOD = mod[:].rearrange("p a f s -> p (a f) s")

        s_in, s_par = sem("x_loaded"), sem("params_loaded")
        s_const, s_ready = sem("pool_consts_made"), sem("vector_consts_made")
        raw_full = [sem(f"raw_full{i}") for i in range(RAW)]
        plain_full = [sem(f"plain_full{i}") for i in range(PLAIN)]
        s_hi, s_lo, s_used = sem("w_hi_made"), sem("w_lo_made"), sem("w_unit_used")
        plain_used = sem("plain_unit_used")
        taken = [sem("pair0_taken"), sem("pair1_taken")]
        s_csil, s_mod = sem("cond_silu_made"), sem("mod_made")
        s_sq, s_stat, s_rstd = sem("squares_made"), sem("stat_done"), sem("rstd_made")
        s_nt, s_hhi, s_h = sem("scaled_made"), sem("h_hi_made"), sem("h_made")
        s_x = sem("x_updated")
        s_sp, s_c4 = sem("softplus_parts_made"), sem("softplus_made")
        s_lrw, s_wdec = sem("lr_weights_loaded"), sem("decay_weights_loaded")
        s_lrz, s_lrh, s_lrl = sem("lr_pad_zeroed"), sem("lr_hi_made"), sem("lr_lo_made")
        s_lrp, s_lr = sem("lr_done"), sem("lr_copied")
        s_wdz = sem("decay_weights_zeroed")
        s_vh, s_gz, s_ga, s_gl = sem("head_slices_copied"), sem("decay_logits_done"), sem("abs_made"), sem("ln_made")
        s_gc, s_ge, s_go = sem("cum_made"), sem("decay_exps_made"), sem("decayed_qk_made")
        s_keT, s_keTc, s_att, s_attm = sem("keT_done"), sem("keT_copied"), sem("gla_att_done"), sem("gla_att_masked")
        s_kv, s_state, s_o = sem("kv_done"), sem("states_made"), sem("gla_o_done")
        s_osq, s_ostat, s_orstd, s_on = sem("o_squares"), sem("o_stat"), sem("o_rstd"), sem("o_normed")
        s_eva, s_evp, s_evh, s_b = sem("evac_act"), sem("evac_product"), sem("evac_hi"), sem("split_pairs_made")
        s_asq, s_asd, s_aln = sem("att_squares"), sem("att_stat_done"), sem("att_ln_made")
        s_arstd, s_anorm, s_arot, s_arope = sem("att_rstd"), sem("att_normed"), sem("att_swapped"), sem("att_roped")
        s_qc, s_sc, s_nb, s_ex = sem("q_copied"), sem("scores_done"), sem("neg_max_made"), sem("probs_exped")
        s_pn, s_pt, s_ptc, s_av = sem("probs_normed"), sem("probs_transposed"), sem("probsT_copied"), sem("att_out_done")
        s_ahi, s_alo = sem("att_hi"), sem("att_lo")
        s_lz, s_ltz, s_lt, s_la2 = sem("lru_logits_done"), sem("lru_logits_taken"), sem("lru_exps_made"), sem("lru_squares")
        s_lv, s_ls, s_lh = sem("lru_v_made"), sem("lru_sqrt_made"), sem("lru_h_made")
        s_fa, s_fs = sem("ffn_centre_tap"), sem("ffn_silu")
        s_c_act, s_c_dve = sem("act_chain"), sem("dve_chain")
        s_out = sem("out_stored")

        block = ctx.enter_context(nc.Block())

        def pcol(l, name):
            a, b = PCOLS[name]
            return par[:, l, a:b]

        def c0_of(l):
            return 0 if l < DEPTH - 1 else CTX

        def segs_of(c0):
            return [s for s in range(2) if (s + 1) * CTX > c0]

        stages = [("gqk", 4, 2), ("gv", 4, 2), ("r", 4, 2), ("br0", 8, 2), ("aq", 4, 2), ("akv", 2, 2), ("br1", 8, 2),
                  ("lx", 4, 2), ("y", 4, 2), ("br2", 8, 2), ("out", 4, 2), ("up", FT, 2), ("down", 4, DOWN_UNITS)]
        pairs_of = {n: c for n, c, _ in stages}
        units_of = {n: m for n, _, m in stages}
        order = [(l, n) for l in range(DEPTH) for n, _, _ in stages]
        first_unit, first_pair = {}, {}
        u = q = 0
        for l, name in order:
            first_unit[l, name], first_pair[l, name] = u, q
            u, q = u + pairs_of[name] * units_of[name], q + pairs_of[name]
        assert u == DEPTH * SPLIT_UNITS and all(v % 4 == 0 for v in first_unit.values())

        def before(group, l, name):
            n = order.index((l, name))
            return sum(pairs_of[s] // (2 if s[:2] == "br" else 1) for _, s in order[:n] if s in group)

        PRODUCTS = ("r", "y", "br2", "up")
        CENTRES = ("lx", "up")

        def wait_taken(eng, l, name):
            n = (first_pair[l, name] + pairs_of[name]) // 2
            for j in range(2):
                eng.wait_ge(taken[j], n + 1)

        CHUNK_ORDER = [list(range(NCH)), [3, 2, 1, 0, 7, 6, 5, 4]]
        KV_BANK = (6, 2)
        HSCALE = HD ** -0.5

        def att_items(l):
            return 16 * l, len(segs_of(c0_of(l)))

        @block.sync
        def _(sp_):
            def load_split(first, n):
                with sp_.Fori(0, n // RAW) as i:
                    for s in range(RAW):
                        sp_.wait_ge(s_lo, i * RAW + (first - RAW + s + 1))
                        sp_.dma_start(wraw[s][:], weights[i * RAW + (first + s)]).then_inc(raw_full[s], 16)

            def load_plain(first, n):
                if first == 0:
                    for s in range(PLAIN):
                        sp_.dma_start(wpl[s][:], plain[s]).then_inc(plain_full[s], 16)
                    first, n = PLAIN, n - PLAIN
                with sp_.Fori(0, n // PLAIN) as i:
                    for s in range(PLAIN):
                        sp_.wait_ge(plain_used, i * PLAIN + (first - PLAIN + s + 1))
                        sp_.dma_start(wpl[s][:], plain[i * PLAIN + (first + s)]).then_inc(plain_full[s], 16)

            sp_.dma_start(x[:], xt).then_inc(s_in, 16)
            for s in range(RAW):
                sp_.dma_start(wraw[s][:], weights[s]).then_inc(raw_full[s], 16)
            for l in range(DEPTH):
                load_plain(l * PLAIN_UNITS, ADA_UNITS)
                load_split(first_unit[l, "gqk"] + RAW, first_unit[l, "y"] - first_unit[l, "gqk"])
                load_plain(l * PLAIN_UNITS + ADA_UNITS, GATE_UNITS)
                load_split(first_unit[l, "y"] + RAW,
                           (l + 1) * SPLIT_UNITS - first_unit[l, "y"] - (RAW if l == DEPTH - 1 else 0))
            sp_.wait_ge(s_x, KT * 2 * DEPTH)
            sp_.dma_start(out, x[:, :, CTX:TOK]).then_inc(s_out, 16)
            sp_.wait_ge(s_out, 16)

        @block.gpsimd
        def _(pool):
            pool.dma_start(par[:], params).then_inc(s_par, 16)
            pool.dma_start(cin[:], cvec).then_inc(s_par, 16)
            pool.dma_start(cs[:], rope).then_inc(s_par, 16)
            nc.gpsimd.memset(ident[:], 0.0).then_inc(s_const, 1)
            nc.gpsimd.memset(swap[:], 0.0).then_inc(s_const, 1)
            nc.gpsimd.memset(keep[:], 1.0).then_inc(s_const, 1)
            made = 3

            def select(v, op, fill, base, pattern, mult):
                nonlocal made
                pool.wait_ge(s_const, made)
                nc.gpsimd.affine_select(out=v, in_=v, compare_op=op, fill=fill, base=base, pattern=pattern,
                                        channel_multiplier=mult).then_inc(s_const, 1)
                made += 1

            select(ident[:], ALU.not_equal, 1.0, 0, [[-1, P]], 1)
            for off, fill in ((32, -1.0), (-32, 1.0)):
                for axis in range(2):
                    m0 = 64 * axis + (0 if off > 0 else 32)
                    select(swap[:, m0:m0 + 32], ALU.not_equal, fill, -(m0 + off), [[-1, 32]], 1)
            for d, sign in enumerate((1, -1)):
                for c in range(P // CHUNK):
                    v = keep[:, d, c * CHUNK:(c + 1) * CHUNK]
                    select(v, ALU.is_ge, 0.0, -c * CHUNK, [[0, CHUNK]], 1)
                    select(v, ALU.is_ge, 0.0, (c + 1) * CHUNK - 1, [[0, CHUNK]], -1)
                    select(v, ALU.is_ge, 0.0, sign * c * CHUNK, [[sign, CHUNK]], -sign)
            assert made == CONSTS
            for l in range(DEPTH):
                if l:
                    pool.wait_ge(s_vh, HEADS * l)
                nc.gpsimd.memset(wdec[:], 0.0).then_inc(s_wdz, 1)
                pool.wait_ge(s_wdz, l + 1)
                for d in range(2):
                    pool.dma_start(wdec[d * RANK:(d + 1) * RANK, d, :], w_dec[l, d]).then_inc(s_wdec, 16)
                pool.wait_ge(s_hhi, KT * (2 * l + 1))
                pool.dma_start(lrw[:], w_lr[l]).then_inc(s_lrw, 16)
                pool.wait_ge(s_wdec, 32 * (l + 1))
                wait_taken(pool, l, "gv")
                with pool.Fori(0, HEADS) as i:
                    pool.wait_ge(s_on, i + (HEADS * l + 1))
                    nc.gpsimd.tensor_copy(wdh[:], wdec[:, :, bass.ds(i * DK, DK)]).then_inc(s_vh, 1)
                    nc.gpsimd.tensor_copy(vh[:], gv[:, :, bass.ds(i * DV, DV)]).then_inc(s_vh, 1)
                pool.wait_ge(s_arope, (l + 1) * (AQ + AKV))
                n0, ng = att_items(l)
                c0 = c0_of(l)
                for kv in range(AKV):
                    with pool.Fori(0, 2) as i:
                        for j in range(2):
                            pool.wait_ge(s_alo, i * (2 * ng) + (4 + n0 + ng * (4 * kv + j - 1)))
                            nc.gpsimd.tensor_copy(qcur[j][:, 0, c0:], aqk[:, i * 2 + (4 * kv + j), c0:]).then_inc(s_qc, 1)
                with pool.Fori(0, BLOCKS // 2) as i:
                    pool.wait_ge(s_lt, i + (BLOCKS // 2 * l + 1))
                    nc.gpsimd.tensor_tensor(l_a2[:], l_a[:], l_a[:], ALU.mult).then_inc(s_la2, 1)

        @block.scalar
        def _(act):
            chain = Chain(act, s_c_act)
            link = chain.link
            A_ = nc.scalar.activation

            def hi(b4, off):
                act.wait_ge(raw_full[off % RAW], b4 * 16 + (16 * (off // RAW) + 16))
                act.wait_ge(s_used, b4 * 4 + (off - 1))
                A_(whi[off % 2][:], wraw[off % RAW][:], ACT.Copy).then_inc(s_hi, 1)

            def pairs(l, name, evac, stride=0):
                m, n, last = units_of[name], pairs_of[name], (l, name) == order[-1]
                b, turns = first_unit[l, name] // 4, pairs_of[name] // 2

                def turn(i, b4, final):
                    for j in range(2):
                        for o in range(2 + m * j, m * (j + 1) + 2):
                            if not (final and o >= 2 * m):
                                hi(b4, o)
                        act.wait_ge(s_used, b4 * 4 + m * (j + 1))
                        evac(i, j)

                with act.Fori(0, turns - last) as i:
                    chain.enter(i, stride)
                    turn(i, i * (m // 2) + b, False)
                    chain.leave(turns - last)
                if last:
                    turn(turns - 1, b + (turns - 1) * (m // 2), True)

            def norm_stats(n, src, ready, c0):
                for j in range(4):
                    ready(2 * j + 2)
                    A_(sq[:, 2 * j:2 * j + 2, c0:], src[:, 2 * j:2 * j + 2, c0:], ACT.Square).then_inc(s_sq, 1)
                act.wait_ge(s_stat, n + 1)
                link(A_(rstd[:, c0:], ps[:, 6, c0:], ACT.Ln, scale=1.0 / D_MODEL, bias=eps[:]))
                A_(rstd[:, c0:], rstd[:, c0:], ACT.Exp, scale=-0.5).then_inc(s_rstd, 1)

            def make_h(n, shift, segs):
                for k in range(KT):
                    act.wait_ge(s_nt, KT * n + k + 1)
                    for s in segs:
                        c = slice(s * CTX, (s + 1) * CTX)
                        ins = A_(hh[:, k, c], nt[:, k, c], ACT.Identity, bias=MOD[:, 8 * shift + k, s:s + 1])
                    ins.then_inc(s_hhi, 1)

            act.wait_ge(s_par, 48)
            act.wait_ge(s_ready, READY)
            A_(csil[:], cin[:], ACT.Silu).then_inc(s_csil, 1)
            for s in range(2):
                act.wait_ge(raw_full[s], 16)
                A_(whi[s][:], wraw[s][:], ACT.Copy).then_inc(s_hi, 1)
            act.wait_ge(s_in, 16)
            for l in range(DEPTH):
                c0, segs = c0_of(l), segs_of(c0_of(l))
                if l:
                    act.wait_ge(s_lh, BLOCKS // 2 * l)
                link(A_(sp[:, 0], pcol(l, "lam"), ACT.Abs))
                link(A_(sp[:, 0], sp[:, 0], ACT.Exp, scale=-1.0))
                link(A_(sp[:, 0], sp[:, 0], ACT.Ln, bias=one[:]))
                A_(sp[:, 1], pcol(l, "lam"), ACT.Relu, scale=-1.0).then_inc(s_sp, 1)
                norm_stats(4 * l, x, (lambda k: act.wait_ge(s_x, KT * (2 * l - 1) + k)) if l else (lambda k: None), 0)
                act.wait_ge(s_mod, l + 1)
                make_h(2 * l, 0, (0, 1))

                def copy_gqk(i, j):
                    A_(gqk[:, i * 2 + j, 0, c0:], PAIR[j][:, 0, c0:], ACT.Copy)
                    A_(gqk[:, i * 2 + j, 1, :], PAIR[j][:, 1, :], ACT.Copy).then_inc(taken[j], 1)

                def copy_gv(i, j):
                    A_(gv[:, :, bass.ds(i * 512 + 256 * j, 256)], PAIR[j].rearrange("p a (b c) -> p (a b) c", c=256),
                       ACT.Copy).then_inc(taken[j], 1)

                pairs(l, "gqk", copy_gqk)
                pairs(l, "gv", copy_gv)

                act.wait_ge(s_lrw, 16 * (l + 1))
                act.wait_ge(s_lrz, 2 * (l + 1))
                A_(lrh[:, :, 0:2 * RANK], lrw[:], ACT.Copy).then_inc(s_lrh, 1)
                act.wait_ge(s_lrp, l + 1)
                A_(lr[:], ps[0:2 * RANK, 7, :], ACT.Copy).then_inc(s_lr, 1)

                with act.Fori(0, HEADS) as i:
                    chain.enter(i, 2)
                    n = i + HEADS * l
                    act.wait_ge(s_gz, n + 1)
                    for d in range(2):
                        ins = A_(gl_l[:, d], ps[:, d], ACT.Abs, bias=pcol(l, "b_dec")[:, bass.ds(i * 2 + d, 1)])
                    ins.then_inc(s_ga, 1)
                    act.wait_ge(s_ga, n + 1)
                    link(A_(gl_l[:], gl_l[:], ACT.Exp, scale=-1.0))
                    A_(gl_l[:], gl_l[:], ACT.Ln, bias=one[:]).then_inc(s_gl, 1)
                    act.wait_ge(s_gc, n + 1)
                    A_(gl_ke[:], gl_ke[:], ACT.Exp, scale=1.0 / TEMP).then_inc(s_ge, 1)
                    A_(gl_ep[:], gl_c[:], ACT.Exp, scale=1.0 / TEMP).then_inc(s_ge, 1)
                    A_(gl_ki[:], gl_c[:], ACT.Exp, scale=-1.0 / TEMP).then_inc(s_ge, 1)
                    act.wait_ge(s_keT, n + 1)
                    A_(keT[:].rearrange("p d t k -> p d (t k)"), ps[:, 2:4], ACT.Copy).then_inc(s_keTc, 1)
                    act.wait_ge(s_o, n + 1)
                    A_(go[:, :, c0:], ps[:, 4:6, c0:], ACT.Square).then_inc(s_osq, 1)
                    act.wait_ge(s_ostat, n + 1)
                    link(A_(gstat[:, 0, c0:], ps[:, 0, c0:], ACT.Ln, scale=1.0 / DV, bias=eps[:]))
                    A_(gstat[:, 0, c0:], gstat[:, 0, c0:], ACT.Exp, scale=-0.5).then_inc(s_orstd, 1)
                    chain.leave(HEADS)

                def product(name, func):
                    n0 = before(PRODUCTS, l, name)

                    def evac(i, j):
                        act.wait_ge(s_evp, i * 2 + (n0 + j - 1)) if n0 + j - 1 > 0 else None
                        A_(ev[j][:, :, c0:], PAIR[j][:, :, c0:], func).then_inc(taken[j], 1)
                        act.wait_ge(s_evp, i * 2 + (n0 + j + 1))
                        A_(bh[:, bass.ds(i * 4 + 2 * j, 2), c0:], evp[j][:, :, c0:], ACT.Copy).then_inc(s_evh, 1)
                    return evac

                def gate(name):
                    def evac(i, j):
                        if j == 0:
                            act.wait_ge(taken[1], i + (first_pair[l, name] // 2 + 1))
                            A_(ev[0][:, :, c0:], PAIR[0][:, :, c0:], ACT.Tanh, scale=0.5).then_inc(taken[0], 1)
                        elif name == "br2":
                            act.wait_ge(s_evp, i + (before(PRODUCTS, l, name) + 1))
                            A_(mh[:, bass.ds(i * 2, 2), c0:], mixed[:, bass.ds(i * 2, 2), c0:], ACT.Copy, scale=0.5)\
                                .then_inc(s_evh, 1)
                    return evac

                pairs(l, "r", product("r", ACT.Silu))
                pairs(l, "br0", gate("br0"))

                def copy_aq(i, j):
                    A_(aqk[:, bass.ds(i * 4 + 2 * j, 2), c0:], PAIR[j][:, :, c0:], ACT.Copy).then_inc(taken[j], 1)

                def copy_akv(i, j):
                    if j == 0:
                        A_(aqk[:, AQ:], PAIR[0], ACT.Copy).then_inc(taken[0], 1)
                    else:
                        A_(av[:], PAIR[1].rearrange("p a (b c) -> p (a b) c", c=256), ACT.Copy).then_inc(taken[1], 1)

                pairs(l, "aq", copy_aq)
                pairs(l, "akv", copy_akv)

                wait_taken(act, l, "akv")
                t0 = (AQ + AKV) * l

                def att_stats(i, t, c):
                    for j in range(2):
                        act.wait_ge(s_asd, i * 2 + (t0 + t + j - 1)) if t0 + t + j > 1 else None
                        A_(asq[j][:, 0, c:], aqk[:, i * 2 + (t + j), c:], ACT.Square).then_inc(s_asq, 1)
                    for j in range(2):
                        act.wait_ge(s_asd, i * 2 + (t0 + t + j + 1))
                        A_(astat[:, i * 2 + (t + j), c:], ps[:, 4 + j, c:], ACT.Ln, scale=1.0 / HD, bias=eps[:])\
                            .then_inc(s_aln, 1)
                with act.Fori(0, AQ // 2) as i:
                    att_stats(i, 0, c0)
                att_stats(0, AQ, 0)
                act.wait_ge(s_aln, t0 + AQ + AKV)
                A_(astat[:, 0:AQ, c0:], astat[:, 0:AQ, c0:], ACT.Exp, scale=-0.5).then_inc(s_arstd, 1)
                A_(astat[:, AQ:], astat[:, AQ:], ACT.Exp, scale=-0.5).then_inc(s_arstd, 1)

                n0, ng = att_items(l)
                for kv in range(AKV):
                    with act.Fori(0, 2) as i:
                        def item(k):
                            return i * (2 * ng) + (n0 + 4 * ng * kv + k + 1)

                        def exps(k):
                            g, b = segs[k % ng], k % 2
                            act.wait_ge(s_nb, item(k))
                            for t in range(2):
                                ins = A_(prob[b][:, t, 0:(g + 1) * CTX], PAIR[b][:, t, 0:(g + 1) * CTX], ACT.Exp,
                                         scale=HSCALE, bias=nb[:, b, t:t + 1], accum_out=sums[:, b, t:t + 1])
                            ins.then_inc(s_ex, 1)

                        exps(0)
                        for k in range(2 * ng):
                            g, b = segs[k % ng], k % 2
                            if k + 1 < 2 * ng:
                                exps(k + 1)
                            act.wait_ge(s_pt, item(k))
                            A_(probT[b][:, 0:2 * g + 2], ps[:, 4:6].rearrange("p a (b c) -> p (a b) c", c=SEQ)[:, 0:2 * g + 2],
                               ACT.Copy).then_inc(s_ptc, 1)
                            act.wait_ge(s_av, item(k))
                            A_(bh[:, i * 2 + (4 * kv + k // ng), g * CTX:(g + 1) * CTX], ps[:, 6 + b, 0:SEQ], ACT.Copy)\
                                .then_inc(s_ahi, 1)

                pairs(l, "br1", gate("br1"))

                def centre(name, dst, w, bias, c, tile):
                    def evac(i, j):
                        for f in range(2):
                            ins = A_(dst(i, j, f)[:, c:], PAIR[j][:, f, c:], ACT.Identity,
                                     scale=pcol(l, w)[:, bass.ds(tile(i, j, f), 1)],
                                     bias=pcol(l, bias)[:, bass.ds(tile(i, j, f), 1)] if w != "cw" else
                                     pcol(l, bias)[:, bass.ds(i * 4 + (2 * j + f), 1)])
                        ins.then_inc(s_eva, 1)
                    return evac

                pairs(l, "lx", centre("lx", lambda i, j, f: xc[:, i * 4 + (2 * j + f)], "cw", "cb", 0,
                                      lambda i, j, f: i * 4 + (2 * KT + 2 * j + f)))

                act.wait_ge(s_c4, l + 1)
                with act.Fori(0, BLOCKS // 2) as i:
                    for c in range(4):
                        act.wait_ge(s_lz, i * 4 + (16 * l + c + 1))
                        if c == 0:
                            act.wait_ge(s_lh, i + (4 * l + 1))
                        for g, buf in enumerate((l_tr, l_ti)):
                            ins = A_(buf[:, c], PAIR[c % 2][:, g], ACT.Tanh, scale=0.5,
                                     bias=hbias[:, bass.ds(i * 8 + (2 * c + g), 1)])
                        ins.then_inc(s_ltz, 1)
                    act.wait_ge(s_ltz, i * 4 + (16 * l + 2 + 4))
                    for c in range(4):
                        k4 = sp[:, 2, bass.ds(i * 4 + c, 1)]
                        A_(l_a[:, c], l_tr[:, c], ACT.Exp, scale=k4, bias=k4)
                        ins = A_(l_th[:, c], l_tr[:, c], ACT.Tanh, scale=k4, bias=k4)
                    ins.then_inc(s_lt, 1)
                    act.wait_ge(s_lv, i + (4 * l + 1))
                    A_(l_tr[:], l_a2[:], ACT.Sqrt, scale=-0.25).then_inc(s_ls, 1)

                act.wait_ge(s_ls, BLOCKS // 2 * (l + 1))
                pairs(l, "y", product("y", ACT.Gelu_apprx_tanh))
                pairs(l, "br2", gate("br2"))

                def copy_out(i, j):
                    A_(mixed[:, bass.ds(i * 4 + 2 * j, 2), c0:], PAIR[j][:, :, c0:], ACT.Copy).then_inc(taken[j], 1)

                pairs(l, "out", copy_out)

                def taken_tiles(name):
                    q0 = (first_pair[l, name]) // 2
                    return lambda k: act.wait_ge(taken[(k // 2 - 1) % 2], q0 + (k // 2 - 1) // 2 + 2)

                norm_stats(4 * l + 1, mixed, taken_tiles("out"), c0)
                norm_stats(4 * l + 2, x, lambda k: act.wait_ge(s_x, KT * 2 * l + k), c0)
                make_h(2 * l + 1, 3, segs)

                n_p = before(PRODUCTS, l, "up")
                tap = centre("up", lambda i, j, f: fa[j][:, f], "fw", "fb", c0, None)

                def up(i, j):
                    for f in range(2):
                        t = i * 4 + (2 * j + f)
                        ins = A_(fa[j][:, f, c0:], PAIR[j][:, f, c0:], ACT.Identity,
                                 scale=pcol(l, "fw")[:, bass.ds(t + 2 * FT, 1)], bias=pcol(l, "fb")[:, bass.ds(t, 1)])
                    ins.then_inc(s_eva, 1)
                    act.wait_ge(taken[j], i + (first_pair[l, "up"] // 2 + 2))
                    A_(fs[j][:, 0, c0:], fa[j][:, 0, c0:], ACT.Silu).then_inc(s_fs, 1)
                    act.wait_ge(s_evp, i * 2 + (n_p + j + 1))
                    A_(fh[:, i * 2 + j, c0:], fa[j][:, 1, c0:], ACT.Copy).then_inc(s_evh, 1)

                pairs(l, "up", up)

                def copy_down(i, j):
                    A_(y2[:, bass.ds(i * 4 + 2 * j, 2), c0:] if not isinstance(i, int) else
                       y2[:, i * 4 + 2 * j:i * 4 + 2 * j + 2, c0:], PAIR[j][:, :, c0:], ACT.Copy).then_inc(taken[j], 1)

                pairs(l, "down", copy_down)
                norm_stats(4 * l + 3, y2, taken_tiles("down"), c0)

        @block.vector
        def _(dve):
            chain = Chain(dve, s_c_dve)
            link = chain.link
            V = nc.vector

            def lo(b4, off):
                dve.wait_ge(s_hi, b4 * 4 + (off + 1))
                V.tensor_tensor(wlo[off % 2][:], wraw[off % RAW][:], whi[off % 2][:].bitcast(F32), ALU.subtract)\
                    .then_inc(s_lo, 1)

            def pairs(l, name, evac, stride=0):
                m, last = units_of[name], (l, name) == order[-1]
                b, turns = first_unit[l, name] // 4, pairs_of[name] // 2

                def turn(i, b4, final):
                    for j in range(2):
                        for o in range(2 + m * j, m * (j + 1) + 2):
                            if not (final and o >= 2 * m):
                                lo(b4, o)
                        if evac:
                            evac(i, j)

                with dve.Fori(0, turns - last) as i:
                    chain.enter(i, stride)
                    turn(i, i * (m // 2) + b, False)
                    chain.leave(turns - last)
                if last:
                    turn(turns - 1, b + (turns - 1) * (m // 2), True)

            def split_h(n, gain, shift, segs):
                c0 = segs[0] * CTX
                dve.wait_ge(s_rstd, n_stat[n] + 1)
                for k0 in range(0, KT, 2):
                    for k in (k0, k0 + 1):
                        for s in segs:
                            c = slice(s * CTX, (s + 1) * CTX)
                            ins = V.scalar_tensor_tensor(nt[:, k, c], x[:, k, c], gmod[:, gain, k, s:s + 1], rstd[:, c],
                                                         ALU.mult, ALU.mult)
                        ins.then_inc(s_nt, 1)
                    for k in (k0, k0 + 1):
                        dve.wait_ge(s_hhi, KT * n + k + 1)
                        for s in segs:
                            c = slice(s * CTX, (s + 1) * CTX)
                            ins = V.scalar_tensor_tensor(hl[:, k, c], nt[:, k, c], MOD[:, 8 * shift + k, s:s + 1],
                                                         hh[:, k, c].bitcast(F32), ALU.add, ALU.subtract)
                        ins.then_inc(s_h, 1)

            def residual(n, src, gain, segs):
                dve.wait_ge(s_rstd, n + 1)
                for k in range(KT):
                    for s in segs:
                        c = slice(s * CTX, (s + 1) * CTX)
                        link(V.scalar_tensor_tensor(src[:, k, c], src[:, k, c], gmod[:, gain, k, s:s + 1], rstd[:, c],
                                                    ALU.mult, ALU.mult))
                    c = slice(segs[0] * CTX, TOK)
                    V.tensor_tensor(x[:, k, c], x[:, k, c], src[:, k, c], ALU.add).then_inc(s_x, 1)

            n_stat = {0: 0, 1: 2, 2: 4, 3: 6}
            V.memset(ones[:], 1.0).then_inc(s_ready, 1)
            V.memset(one[:], 1.0).then_inc(s_ready, 1)
            V.memset(eps[:], EPS).then_inc(s_ready, 1)
            link(V.memset(scanmask[:], 1.0))
            link(V.memset(scanmask[:, :, 0:1], 0.0))
            for s, k in ((taken[0], 1), (taken[1], 1), (s_ltz, 2), (s_on, 1), (s_lh, 1), (s_alo, 4)):
                dve.sem_inc(s, k)
            for s in range(2):
                dve.wait_ge(s_hi, s + 1)
                V.tensor_tensor(wlo[s][:], wraw[s][:], whi[s][:].bitcast(F32), ALU.subtract).then_inc(s_lo, 1)
            dve.wait_ge(s_par, 48)
            dve.wait_ge(s_const, CONSTS)
            dve.wait_ge(s_in, 16)
            for l in range(DEPTH):
                c0, segs = c0_of(l), segs_of(c0_of(l))
                W = TOK - c0
                dve.wait_ge(plain_used, l * PLAIN_UNITS + ADA_UNITS)
                for f in range(2):
                    link(V.tensor_tensor(mod[:, :, f, :], ps[:, 4 + f, 0:ADA_UNITS].rearrange("p (a s) -> p a s", s=2),
                                         pcol(l, "b_ada").rearrange("p (a f) -> p a f", f=2)[:, :, f, None]
                                         .broadcast_to([P, ADA_UNITS // 2, 2]), ALU.add))
                for n, (m, plus) in enumerate(((1, 1.0), (2, 0.0), (4, 1.0), (5, 0.0))):
                    link(V.scalar_tensor_tensor(gmod[:, n], MOD[:, 8 * m:8 * m + 8], plus,
                                                pcol(l, "gains")[:, 8 * n:8 * n + 8, None].broadcast_to([P, KT, 2]),
                                                ALU.add, ALU.mult))
                link(V.tensor_scalar(hbias[:], pcol(l, "b_gate"), 0.5, None, ALU.mult))
                dve.wait_ge(s_sp, l + 1)
                link(V.tensor_tensor(sp[:, 0], sp[:, 0], sp[:, 1], ALU.add))
                V.tensor_scalar(sp[:, 2], sp[:, 0], -4.0, None, ALU.mult).then_inc(s_c4, 1)
                V.memset(attm[:], 0.0).then_inc(s_mod, 1)
                split_h(2 * l, 0, 0, (0, 1))
                pairs(l, "gqk", None)
                pairs(l, "gv", None)

                dve.wait_ge(s_lrw, 16 * (l + 1))
                V.memset(lrh[:].bitcast(F32), 0.0).then_inc(s_lrz, 1)
                V.memset(lrl[:].bitcast(F32), 0.0).then_inc(s_lrz, 1)
                dve.wait_ge(s_lrh, l + 1)
                V.tensor_tensor(lrl[:, :, 0:2 * RANK], lrw[:], lrh[:, :, 0:2 * RANK].bitcast(F32), ALU.subtract)\
                    .then_inc(s_lrl, 1)

                def chunks(v):
                    return v.rearrange("p (n c) -> p n c", c=CHUNK)

                with dve.Fori(0, HEADS) as i:
                    chain.enter(i, 9)
                    n = i + HEADS * l
                    dve.wait_ge(s_ga, n + 1)
                    for d in range(2):
                        ins = V.tensor_scalar(gl_m[:, d], ps[:, d], pcol(l, "b_dec")[:, bass.ds(i * 2 + d, 1)], 0.0,
                                              ALU.add, ALU.min)
                    link(ins)
                    dve.wait_ge(s_gl, n + 1)
                    link(V.tensor_tensor(gl_m[:], gl_m[:], gl_l[:], ALU.subtract))
                    mask = scanmask[:].rearrange("p n c -> p (n c)")
                    V.tensor_tensor_scan(gl_c[:, 0], mask, gl_m[:, 0], 0.0, ALU.mult, ALU.add)
                    link(V.tensor_tensor_scan(gl_c[:, 1, ::-1], mask, gl_m[:, 1, ::-1], 0.0, ALU.mult, ALU.add))
                    for d, end in enumerate((CHUNK - 1, 0)):
                        v = chunks(gl_c[:, d])
                        ins = V.tensor_tensor(chunks(gl_ke[:, d]), v[:, :, end:end + 1].broadcast_to([P, NCH, CHUNK]), v,
                                              ALU.subtract)
                    ins.then_inc(s_gc, 1)
                    q = gqk[:, i, 0:1, c0:].broadcast_to([P, 2, W])
                    k = gqk[:, i, 1:2, :].broadcast_to([P, 2, TOK])
                    dve.wait_ge(s_ge, n * 3 + 1)
                    V.tensor_tensor(gl_ke[:], gl_ke[:], k, ALU.mult).then_inc(s_go, 1)
                    dve.wait_ge(s_ge, n * 3 + 2)
                    V.scalar_tensor_tensor(gl_qd[:, :, c0:], q, DK ** -0.5, gl_ep[:, :, c0:], ALU.mult, ALU.mult)\
                        .then_inc(s_go, 1)
                    dve.wait_ge(s_ge, n * 3 + 3)
                    V.tensor_tensor(gl_ki[:, :, c0:], gl_ki[:, :, c0:], k[:, :, c0:], ALU.mult).then_inc(s_go, 1)
                    dve.wait_ge(s_const, CONSTS)
                    dve.wait_ge(s_att, n + 1)
                    for d in range(2):
                        v = slice(c0 // P, TOK // P)
                        V.copy_predicated(attm[:, d].rearrange("p (t c) -> p t c", c=P)[:, v],
                                          KEEP[:, d:d + 1].broadcast_to([P, (TOK - c0) // P, P]),
                                          ps[:, d].rearrange("p (t c) -> p t c", c=P)[:, v]).then_inc(s_attm, 1)
                    for d in range(2):
                        for e in range(4):
                            dve.wait_ge(s_kv, n * 8 + (4 * d + e + 1))
                            for p in range(2 * e, min(2 * e + 2, NCH - 1)):
                                c = CHUNK_ORDER[d][p]
                                kv_ = ps[:, KV_BANK[e % 2] + c % 2, 0:DV]
                                end = c * CHUNK + (0 if d else CHUNK - 1)
                                if p == 0:
                                    ins = V.tensor_copy(state[:, d, 1], kv_)
                                else:
                                    ins = V.scalar_tensor_tensor(state[:, d, p + 1], state[:, d, p],
                                                                 gl_ep[:, d, end:end + 1], kv_, ALU.mult, ALU.add)
                                if p % 2 or p == NCH - 2:
                                    ins.then_inc(s_state, 1)
                                    dve.wait_ge(s_state, n * 8 + (4 * d + e + 1))
                                else:
                                    link(ins)
                    dve.wait_ge(s_orstd, n + 1)
                    for t in range(2):
                        ins = V.scalar_tensor_tensor(gqk[:, i, t, c0:], ps[:, 4 + t, c0:],
                                                     pcol(l, "g_gla")[:, bass.ds(i * 2 + t, 1)], gstat[:, 0, c0:],
                                                     ALU.mult, ALU.mult)
                    ins.then_inc(s_on, 1)
                    chain.leave(HEADS)

                def product(name, other):
                    n0, q0 = before(PRODUCTS, l, name), first_pair[l, name]

                    def evac(i, j):
                        dve.wait_ge(taken[j], i + (q0 // 2 + 2))
                        V.tensor_tensor(evp[j][:, :, c0:], ev[j][:, :, c0:], other(i, j), ALU.mult).then_inc(s_evp, 1)
                        dve.wait_ge(s_evh, i * 2 + (n0 + j + 1))
                        t = bass.ds(i * 4 + 2 * j, 2)
                        V.tensor_tensor(bl[:, t, c0:], evp[j][:, :, c0:], bh[:, t, c0:].bitcast(F32), ALU.subtract)\
                            .then_inc(s_b, 1)
                    return evac

                def gate(name):
                    def evac(i, j):
                        if j == 0:
                            return
                        tiles_ = bass.ds(i * 2, 2)
                        b4 = i + first_unit[l, name] // 4
                        dve.wait_ge(s_used, b4 * 4 + 4)
                        dve.wait_ge(taken[0], i + (first_pair[l, name] // 2 + 2))
                        dst = mixed[:, tiles_, c0:] if name == "br0" else evp[0][:, :, c0:]
                        V.scalar_tensor_tensor(dst, ev[0][:, :, c0:], 1.0, PAIR[1][:, :, c0:], ALU.add, ALU.mult)\
                            .then_inc(taken[1], 1)
                        if name == "br0":
                            return
                        dve.wait_ge(taken[1], i + (first_pair[l, name] // 2 + 2))
                        ins = V.tensor_tensor(mixed[:, tiles_, c0:], mixed[:, tiles_, c0:], evp[0][:, :, c0:], ALU.add)
                        if name == "br2":
                            ins.then_inc(s_evp, 1)
                            dve.wait_ge(s_evh, i + (before(PRODUCTS, l, name) + 1))
                            V.scalar_tensor_tensor(ml[:, tiles_, c0:], mixed[:, tiles_, c0:], 0.5,
                                                   mh[:, tiles_, c0:].bitcast(F32), ALU.mult, ALU.subtract)\
                                .then_inc(s_b, 1)
                    return evac

                pairs(l, "r", product("r", lambda i, j: gqk[:, i * 2 + j, :, c0:]))
                pairs(l, "br0", gate("br0"))
                pairs(l, "aq", None)
                pairs(l, "akv", None)

                t0 = (AQ + AKV) * l

                def att_norm(i, t, c):
                    for j in range(2):
                        v = aqk[:, i * 2 + (t + j), c:]
                        V.scalar_tensor_tensor(v, v, pcol(l, "g_qk")[:, bass.ds(i * 2 + (t + j), 1)],
                                               astat[:, i * 2 + (t + j), c:], ALU.mult, ALU.mult).then_inc(s_anorm, 1)
                    for j in range(2):
                        v = aqk[:, i * 2 + (t + j), CTX:]
                        dve.wait_ge(s_anorm, i * 2 + (t0 + t + j + 1))
                        V.tensor_tensor(arot[j][:, 1], v, cs[:, 0], ALU.mult)
                        dve.wait_ge(s_arot, i * 2 + (t0 + t + j + 1))
                        link(V.tensor_tensor(arot[j][:, 0], ps[:, 4 + j, 0:SEQ], cs[:, 1], ALU.mult))
                        V.tensor_tensor(v, arot[j][:, 0], arot[j][:, 1], ALU.add).then_inc(s_arope, 1)
                dve.wait_ge(s_arstd, 2 * l + 2)
                with dve.Fori(0, AQ // 2) as i:
                    chain.enter(i, 2)
                    att_norm(i, 0, c0)
                    chain.leave(AQ // 2)
                att_norm(0, AQ, 0)

                n0, ng = att_items(l)
                for kv in range(AKV):
                    with dve.Fori(0, 2) as i:
                        chain.enter(i, 4 * ng)

                        def item(k):
                            return i * (2 * ng) + (n0 + 4 * ng * kv + k + 1)

                        def row_max(k):
                            g, b = segs[k % ng], k % 2
                            dve.wait_ge(s_sc, item(k))
                            link(V.tensor_reduce(mx[:, b], PAIR[b][:, :, 0:(g + 1) * CTX], AX_X, ALU.max))
                            V.tensor_scalar(nb[:, b], mx[:, b], -HSCALE, None, ALU.mult).then_inc(s_nb, 1)

                        row_max(0)
                        for k in range(2 * ng):
                            g, b = segs[k % ng], k % 2
                            if k + 1 < 2 * ng:
                                row_max(k + 1)
                            dve.wait_ge(s_ex, item(k))
                            link(V.reciprocal(rsum[:, b], sums[:, b]))
                            for t in range(2):
                                v = prob[b][:, t, 0:(g + 1) * CTX]
                                ins = V.tensor_scalar(v, v, rsum[:, b, t:t + 1], None, ALU.mult)
                            ins.then_inc(s_pn, 1)
                            dve.wait_ge(s_ahi, item(k))
                            hd, c = i * 2 + (4 * kv + k // ng), slice(g * CTX, (g + 1) * CTX)
                            V.tensor_tensor(bl[:, hd, c], ps[:, 6 + b, 0:SEQ], bh[:, hd, c].bitcast(F32), ALU.subtract)\
                                .then_inc(s_alo, 1)
                        chain.leave(2)

                pairs(l, "br1", gate("br1"))

                def seg(v, c):
                    return v.rearrange("p (s t) -> p s t", t=CTX)[:, c // CTX:]

                def taps(name, dst, taps_, c, tile, n0, q0):
                    def evac(i, j):
                        dve.wait_ge(s_eva, i * 2 + (n0 + j + 1))
                        for n, (k, sh) in enumerate(taps_):
                            for f in range(2):
                                o, v = seg(dst(i, j, f), c), seg(PAIR[j][:, f], c)
                                a, b = (slice(-sh, None), slice(0, sh)) if sh < 0 else (slice(0, CTX - sh), slice(sh, CTX))
                                a, b = (slice(-sh, CTX), slice(0, CTX + sh)) if sh < 0 else (a, b)
                                ins = V.scalar_tensor_tensor(o[:, :, a], v[:, :, b], tile(i, j, f, k), o[:, :, a],
                                                             ALU.mult, ALU.add)
                            if n < len(taps_) - 1:
                                link(ins)
                        ins.then_inc(taken[j], 1)
                    return evac

                pairs(l, "lx", taps("lx", lambda i, j, f: xc[:, i * 4 + (2 * j + f)], ((0, -2), (1, -1), (3, 1)), 0,
                                    lambda i, j, f, k: pcol(l, "cw")[:, bass.ds(i * 4 + (KT * k + 2 * j + f), 1)],
                                    before(CENTRES, l, "lx"), first_pair[l, "lx"]), stride=4)

                wait_taken(dve, l, "lx")
                with dve.Fori(0, BLOCKS // 2) as i:
                    chain.enter(i, 7)
                    n = i + BLOCKS // 2 * l
                    dve.wait_ge(s_la2, n + 1)
                    V.scalar_tensor_tensor(l_a2[:], l_a2[:], 1.0, l_th[:], ALU.add, ALU.mult).then_inc(s_lv, 1)
                    for b in range(2):
                        v = l_ti[:, 2 * b:2 * b + 2]
                        ins = V.scalar_tensor_tensor(v, v, 1.0, xc[:, i * 2 + b, None].broadcast_to([P, 2, TOK]),
                                                     ALU.add, ALU.mult)
                    link(ins)
                    dve.wait_ge(s_ls, n + 1)
                    link(V.tensor_tensor(l_ti[:], l_ti[:], l_tr[:], ALU.mult))
                    for b in range(2):
                        f, r = 2 * b, 2 * b + 1
                        V.tensor_tensor_scan(l_h[:, 0], l_a[:, f], l_ti[:, f], 0.0, ALU.mult, ALU.add)
                        rev = slice(CTX - 1, None, -1)
                        link(V.tensor_tensor_scan(l_h[:, 1, 0:CTX][:, ::-1], l_a[:, r, 0:CTX][:, ::-1],
                                                  l_ti[:, r, 0:CTX][:, ::-1], 0.0, ALU.mult, ALU.add))
                        link(V.tensor_tensor_scan(l_h[:, 1, CTX:][:, ::-1], l_a[:, r, CTX:][:, ::-1],
                                                  l_ti[:, r, CTX:][:, ::-1], l_h[:, 1, 0:1], ALU.mult, ALU.add))
                        ins = V.tensor_tensor(hsum[:, i * 2 + b, c0:], l_h[:, 0, c0:], l_h[:, 1, c0:], ALU.add)
                        if b == 0:
                            link(ins)
                    ins.then_inc(s_lh, 1)
                    chain.leave(BLOCKS // 2)
                dve.wait_ge(s_lh, 1 + BLOCKS // 2 * (l + 1))

                pairs(l, "y", product("y", lambda i, j: hsum[:, bass.ds(i * 4 + 2 * j, 2), c0:]))
                pairs(l, "br2", gate("br2"))
                pairs(l, "out", None)
                residual(4 * l + 1, mixed, 1, segs)
                split_h(2 * l + 1, 2, 3, segs)

                n_p = before(PRODUCTS, l, "up")
                up_taps = taps("up", lambda i, j, f: fa[j][:, f], ((0, -1), (2, 1)), c0,
                               lambda i, j, f, k: pcol(l, "fw")[:, bass.ds(i * 4 + (2 * FT * k + 2 * j + f), 1)],
                               before(CENTRES, l, "up"), first_pair[l, "up"])

                def up(i, j):
                    up_taps(i, j)
                    dve.wait_ge(s_fs, i * 2 + (FT * l + j + 1))
                    V.tensor_tensor(fa[j][:, 1, c0:], fs[j][:, 0, c0:], fa[j][:, 1, c0:], ALU.mult).then_inc(s_evp, 1)
                    dve.wait_ge(s_evh, i * 2 + (n_p + j + 1))
                    V.tensor_tensor(fl[:, i * 2 + j, c0:], fa[j][:, 1, c0:], fh[:, i * 2 + j, c0:].bitcast(F32),
                                    ALU.subtract).then_inc(s_b, 1)

                pairs(l, "up", up, stride=2)
                pairs(l, "down", None)
                residual(4 * l + 3, y2, 3, segs)

        @block.tensor
        def _(pe):
            mm = nc.tensor.matmul

            def project(l, name, moving, feature_major=True):
                m, turns = units_of[name], pairs_of[name] // 2
                b, q2 = first_unit[l, name] // 4, first_pair[l, name] // 2
                with pe.Fori(0, turns) as i:
                    b4 = i * (m // 2) + b
                    for j in range(2):
                        pe.wait_ge(taken[j], i + (q2 + 1))
                        mh_, ml_, c = moving(i, j)
                        for h in range(m):
                            o = m * j + h
                            w_h, w_l = whi[o % 2], wlo[o % 2]
                            nk = DOWN_LAST if name == "down" and h == m - 1 else UK
                            pe.wait_ge(s_hi, b4 * 4 + (o + 1))
                            token_major = not feature_major or (name == "akv" and j == 1)
                            for part, (w, parts) in enumerate(((w_h, (mh_, ml_)), (w_l, (mh_,)))):
                                if part:
                                    pe.wait_ge(s_lo, b4 * 4 + (o + 1))
                                for r in range(4 if token_major else 2):
                                    for x_ in parts:
                                        for k in range(nk):
                                            kk = UK * h + k
                                            first = h == 0 and k == 0 and part == 0 and x_ is mh_
                                            final = h == m - 1 and k == nk - 1 and part == 1
                                            if token_major:
                                                ins = mm(PAIR[j][:, r // 2, 256 * (r % 2):256 * (r % 2 + 1)],
                                                         x_[:, kk, r * P:(r + 1) * P], w[:, k, :],
                                                         start=first and r % 2 == 0, stop=final and r % 2 == 1,
                                                         skip_group_check=True)
                                            else:
                                                c_ = c[r]
                                                ins = mm(PAIR[j][:, r, c_:], w[:, k, r * P:(r + 1) * P], x_[:, kk, c_:],
                                                         start=first, stop=final)
                            ins.then_inc(s_used, 1)

            def sum_squares(n, c0):
                for j in range(4):
                    pe.wait_ge(s_sq, 4 * n + j + 1)
                    for k in (2 * j, 2 * j + 1):
                        ins = mm(ps[:, 6, c0:], ones[:], sq[:, k, c0:], start=k == 0, stop=k == KT - 1)
                ins.then_inc(s_stat, 1)

            pe.wait_ge(s_ready, READY)
            pe.wait_ge(s_const, CONSTS)
            pe.wait_ge(s_csil, 1)
            for l in range(DEPTH):
                c0, segs = c0_of(l), segs_of(c0_of(l))
                with pe.Fori(0, ADA_UNITS // 2) as i:
                    for h in range(2):
                        pe.wait_ge(plain_full[h], i * 16 + (16 * (PLAIN_UNITS // 2 * l) + 16))
                        for f in range(2):
                            for k in range(UK):
                                ins = mm(ps[:, 4 + f, bass.ds(i * 2, 2)], wpl[h][:, k, f * P:(f + 1) * P],
                                         csil[:, UK * h + k, :], start=h == 0 and k == 0, stop=h == 1 and k == UK - 1)
                        ins.then_inc(plain_used, 1)
                sum_squares(4 * l, 0)
                pe.wait_ge(s_h, KT * (2 * l + 1))
                both = (0, 0)
                project(l, "gqk", lambda i, j: (hh, hl, (c0, 0)))
                project(l, "gv", lambda i, j: (hh, hl, None), feature_major=False)

                pe.wait_ge(s_lrh, l + 1)
                for x_ in (hh, hl):
                    for k in range(KT):
                        mm(ps[:, 7, :], lrh[:, k, :], x_[:, k, :], start=k == 0 and x_ is hh, stop=False)
                pe.wait_ge(s_lrl, l + 1)
                for k in range(KT):
                    ins = mm(ps[:, 7, :], lrl[:, k, :], hh[:, k, :], start=False, stop=k == KT - 1)
                ins.then_inc(s_lrp, 1)
                pe.wait_ge(s_lr, l + 1)

                t_first = c0 // P
                with pe.Fori(0, HEADS) as i:
                    n = i + HEADS * l
                    pe.wait_ge(s_vh, n * 2 + 2)
                    for d in range(2):
                        ins = mm(ps[:, d], wdh[:, d, :], lr[:], start=True, stop=True)
                    ins.then_inc(s_gz, 1)
                    pe.wait_ge(s_go, n * 3 + 1)
                    for d in range(2):
                        for t in range(TOK // P):
                            ins = nc.tensor.transpose(ps[:, 2 + d, t * P:(t + 1) * P], gl_ke[:, d, t * P:(t + 1) * P],
                                                      ident[:])
                    ins.then_inc(s_keT, 1)
                    pe.wait_ge(s_go, n * 3 + 3)
                    for d in range(2):
                        for t in range(t_first, TOK // P):
                            c = slice(t * P, (t + 1) * P)
                            ins = mm(ps[:, d, c], gl_ki[:, d, c], gl_qd[:, d, c], start=True, stop=True)
                    ins.then_inc(s_att, 1)
                    pe.wait_ge(s_keTc, n + 1)
                    for d in range(2):
                        for e in range(4):
                            g = 4 * d + e
                            if g >= 2:
                                pe.wait_ge(s_state, n * 8 + (g - 1))
                            for p in range(2 * e, min(2 * e + 2, NCH - 1)):
                                c = CHUNK_ORDER[d][p]
                                r = slice((c % 2) * CHUNK, (c % 2 + 1) * CHUNK)
                                ins = mm(ps[:, KV_BANK[e % 2] + c % 2, 0:DV], keT[r, d, c // 2, :],
                                         vh[r, c // 2, :], start=True, stop=True)
                            ins.then_inc(s_kv, 1)
                    pe.wait_ge(s_attm, n * 2 + 2)
                    for d in range(2):
                        for t in range(t_first, TOK // P):
                            c = slice(t * P, (t + 1) * P)
                            for v in range(2):
                                mm(ps[:, 4 + v, c], vh[:, t, v * P:(v + 1) * P], attm[:, d, c],
                                   start=d == 0 and t == t_first, stop=False, skip_group_check=True)
                    for d in range(2):
                        for p in range(1, NCH):
                            c = CHUNK_ORDER[d][p]
                            if p % 2 or p == NCH - 1:
                                pe.wait_ge(s_state, n * 8 + (4 * d + (p - 1) // 2 + 1))
                            if c * CHUNK < c0:
                                continue
                            cc = slice(c * CHUNK, (c + 1) * CHUNK)
                            for v in range(2):
                                ins = mm(ps[:, 4 + v, cc], state[:, d, p, v * P:(v + 1) * P], gl_qd[:, d, cc],
                                         start=False, stop=d == 1 and p == NCH - 1, skip_group_check=True)
                    ins.then_inc(s_o, 1)
                    pe.wait_ge(s_osq, n + 1)
                    for v in range(2):
                        ins = mm(ps[:, 0, c0:], ones[:], go[:, v, c0:], start=v == 0, stop=v == 1)
                    ins.then_inc(s_ostat, 1)

                pe.wait_ge(s_on, 1 + HEADS * (l + 1))
                project(l, "r", lambda i, j: (hh, hl, (c0, c0)))
                lat = (c0, c0)
                pe.wait_ge(s_b, before(PRODUCTS, l, "r") + R_PAIRS)
                project(l, "br0", lambda i, j: ((bh, bl, lat) if j else (hh, hl, lat)))
                project(l, "aq", lambda i, j: (hh, hl, lat))
                project(l, "akv", lambda i, j: (hh, hl, both))

                t0 = (AQ + AKV) * l
                wait_taken(pe, l, "akv")

                def att_sums(i, t, c):
                    for j in range(2):
                        n = i * 2 + (t0 + t + j + 1)
                        pe.wait_ge(s_asq, n)
                        pe.wait_ge(s_aln, n - 2) if t0 + t + j > 1 else None
                        mm(ps[:, 4 + j, c:], ones[:], asq[j][:, 0, c:], start=True, stop=True).then_inc(s_asd, 1)

                def att_swap(i, t):
                    for j in range(2):
                        n = i * 2 + (t0 + t + j + 1)
                        pe.wait_ge(s_anorm, n)
                        pe.wait_ge(s_arope, n - 2) if t0 + t + j > 1 else None
                        mm(ps[:, 4 + j, 0:SEQ], swap[:], aqk[:, i * 2 + (t + j), CTX:], start=True, stop=True)\
                            .then_inc(s_arot, 1)
                with pe.Fori(0, AQ // 2) as i:
                    att_sums(i, 0, c0)
                att_sums(0, AQ, 0)
                with pe.Fori(0, AQ // 2) as i:
                    att_swap(i, 0)
                att_swap(0, AQ)

                n0, ng = att_items(l)
                pe.wait_ge(s_arope, t0 + AQ + AKV)
                for kv in range(AKV):
                    with pe.Fori(0, 2) as i:
                        def item(k):
                            return i * (2 * ng) + (n0 + 4 * ng * kv + k + 1)

                        def scores(k):
                            g, b = segs[k % ng], k % 2
                            if k % ng == 0:
                                pe.wait_ge(s_qc, i * 2 + (AQ * l + 4 * kv + k // ng + 1))
                            for t in range(2):
                                q0 = g * CTX + t * P
                                ins = mm(PAIR[b][:, t, 0:(g + 1) * CTX], qcur[k // ng][:, 0, q0:q0 + P],
                                         aqk[:, AQ + kv, 0:(g + 1) * CTX], start=True, stop=True)
                            ins.then_inc(s_sc, 1)

                        scores(0)
                        for k in range(2 * ng):
                            g, b = segs[k % ng], k % 2
                            if k + 1 < 2 * ng:
                                scores(k + 1)
                            pe.wait_ge(s_pn, item(k))
                            for st in range(2 * g + 2):
                                for t in range(2):
                                    c = (st % 2) * SEQ + t * P
                                    ins = nc.tensor.transpose(ps[:, 4 + st // 2, c:c + P],
                                                              prob[b][:, t, st * P:(st + 1) * P], ident[:])
                            ins.then_inc(s_pt, 1)
                            pe.wait_ge(s_ptc, item(k))
                            pe.wait_ge(s_alo, item(k) + 1 + 1)
                            for st in range(2 * g + 2):
                                ins = mm(ps[:, 6 + b, 0:SEQ], av[:, st, kv * HD:(kv + 1) * HD], probT[b][:, st, :],
                                         start=st == 0, stop=st == 2 * g + 1)
                            ins.then_inc(s_av, 1)

                pe.wait_ge(s_alo, 4 + n0 + AQ * ng)
                project(l, "br1", lambda i, j: ((bh, bl, lat) if j else (hh, hl, lat)))
                project(l, "lx", lambda i, j: (hh, hl, both))

                wait_taken(pe, l, "lx")
                with pe.Fori(0, BLOCKS // 4) as i:
                    for w in range(2):
                        pe.wait_ge(plain_full[w], i * 16 + (16 * (PLAIN_UNITS // 2 * l + ADA_UNITS // 2) + 16))
                        for c in range(4):
                            b, d = c // 2, c % 2
                            pe.wait_ge(s_ltz, i * 8 + (16 * l + 4 * w + c + 1))
                            for g in range(2):
                                ins = mm(PAIR[d][:, g], wpl[w][:, 2 * d + g, b * P:(b + 1) * P],
                                         xc[:, i * 4 + (2 * w + b), :], start=True, stop=True)
                            ins.then_inc(s_lz, 1)
                        ins = mm(ps[:, 4, 0:2], wpl[w][:, 0, 0:P], wpl[w][:, 0, 0:2], start=True, stop=True)
                        ins.then_inc(plain_used, 1)

                pe.wait_ge(s_ltz, 2 + 16 * (l + 1))
                project(l, "y", lambda i, j: (hh, hl, lat))
                pe.wait_ge(s_b, before(PRODUCTS, l, "y") + 4)
                project(l, "br2", lambda i, j: ((bh, bl, lat) if j else (hh, hl, lat)))
                pe.wait_ge(s_b, before(PRODUCTS, l, "br2") + 4)
                project(l, "out", lambda i, j: (mh, ml, lat))
                sum_squares(4 * l + 1, c0)
                sum_squares(4 * l + 2, c0)
                pe.wait_ge(s_h, KT * (2 * l + 2))
                project(l, "up", lambda i, j: (hh, hl, lat))
                pe.wait_ge(s_b, before(PRODUCTS, l, "up") + FT)
                project(l, "down", lambda i, j: (fh, fl, lat))
                sum_squares(4 * l + 3, c0)



def units(w, order):
    k_tiles = -(-w.shape[0] // (P * UK)) * UK
    if w.shape[0] < P * k_tiles:
        w = np.concatenate([w, np.zeros((P * k_tiles - w.shape[0], w.shape[1]), w.dtype)])
    got = []
    for cols in order:
        v = w[:, cols].reshape(k_tiles // UK, UK, P, UC).transpose(0, 2, 1, 3)
        got.append(v)
    return np.concatenate(got)


def lay_out(inputs):
    g = {k: np.asarray(v) for k, v in inputs.items()}
    pair = lambda base: [np.arange(base + UC * i, base + UC * (i + 1)) for i in range(1000)]
    q0, k0, v0, r0, lr0 = 0, 512, 1024, 2048, 3072
    aq0, ak0, lx0, y0, gate0 = 3104, 4128, 4640, 5664, 6688
    tile = lambda base, t: np.arange(base + P * t, base + P * (t + 1))
    weights, plain, w_lr = [], [], []
    for l in range(DEPTH):
        w_in = g["w_in"][l]

        def branch(n):
            a = units(w_in, pair(gate0 + D_MODEL * n)[:4])
            b = units(g["w_branch"][l, n], pair(0)[:4])
            return np.stack([a.reshape(4, 2, P, UK, UC), b.reshape(4, 2, P, UK, UC)], 1).reshape(16, P, UK, UC)

        weights += [
            units(w_in, [np.concatenate([tile(q0, h), tile(k0, h)]) for h in range(HEADS)]),
            units(w_in, pair(v0)[:4]), units(w_in, pair(r0)[:4]), branch(0),
            units(w_in, pair(aq0)[:4]), units(w_in, pair(ak0)[:2]), branch(1),
            units(w_in, pair(lx0)[:4]), units(w_in, pair(y0)[:4]), branch(2), units(g["w_out"][l], pair(0)[:4]),
            units(g["ffn_w_up"][l], [np.concatenate([tile(0, t), tile(D_FF, t)]) for t in range(FT)]),
            units(g["ffn_w_down"][l], pair(0)[:4]),
        ]
        gates = g["lru_w_gates"][l].reshape(4, 4, 2, P, P)
        plain += [units(g["w_ada"][l], pair(0)[:24]),
                  gates.transpose(1, 3, 0, 2, 4).reshape(4, P, UK, UC)]
        w_lr.append(w_in[:, lr0:lr0 + 2 * RANK].reshape(KT, P, 2 * RANK).transpose(1, 0, 2))
    cols = lambda v: v.reshape(-1, P).T
    pieces = lambda v: np.concatenate([cols(r) for r in v], 1)
    params = []
    for l in range(DEPTH):
        fw = g["ffn_conv_w"][l].reshape(3, 2, FT, P).transpose(0, 2, 1, 3).reshape(-1, P).T
        fb = g["ffn_conv_b"][l].reshape(2, FT, P).transpose(1, 0, 2).reshape(-1, P).T
        params.append(np.concatenate([
            cols(g["b_ada"][l]), pieces(g["norm_gains"][l]),
            g["gla_b_decay"][l].reshape(2, HEADS, P).transpose(1, 0, 2).reshape(-1, P).T,
            cols(g["gla_norm_g"][l]),
            np.stack([g["att_q_norm_g"][l]] * AQ + [g["att_k_norm_g"][l]] * AKV, 1),
            pieces(g["lru_conv_w"][l]), cols(g["lru_conv_b"][l]),
            g["lru_b_gates"][l].reshape(2, 2, BLOCKS, P).transpose(2, 0, 1, 3).reshape(-1, P).T,
            g["lru_lambda"][l].reshape(2, BLOCKS, P).transpose(1, 0, 2).reshape(-1, P).T,
            fw, fb], 1))
    stream = np.concatenate([g["ctx"][0], g["x"][0]]).T.reshape(KT, P, TOK).transpose(1, 0, 2)
    cvec = np.stack([g["c_ctx"], g["c"][0]], 1).reshape(KT, P, 2).transpose(1, 0, 2)
    axis_dim = HD // 2
    inv_freq = (1.0 / 10000.0 ** (np.arange(0, axis_dim, 2, dtype=np.float32) / np.float32(axis_dim))).astype(np.float32)
    t = np.arange(SEQ)
    ang = np.concatenate([np.outer(inv_freq, p.astype(np.float32)) for p in (t // GRID_W, t // GRID_W, t % GRID_W,
                                                                            t % GRID_W)])
    rope = np.stack([np.cos(ang), np.sin(ang)], 1).astype(np.float32)
    return {
        "xt": stream, "cvec": cvec, "weights": np.concatenate(weights), "plain": np.concatenate(plain),
        "w_lr": np.stack(w_lr), "w_dec": g["gla_w_decay"], "params": np.stack(params, 1), "rope": rope,
    }


def kernel(**inputs):
    import concourse.bacc as _bacc
    from concourse.bass_utils import run_bass_kernel_spmd as _run

    nc = _bacc.Bacc("TRN2", target_bir_lowering=False, num_devices=1)
    arrays, args = {}, []
    for name, a in lay_out(inputs).items():
        a = np.ascontiguousarray(a)
        arrays[f"in_{name}"] = a
        args.append(nc.dram_tensor(f"in_{name}", a.shape, mybir.dt.from_np(a.dtype), kind="ExternalInput").ap())
    args.append(nc.dram_tensor("out_x", (P, KT, SEQ), F32, kind="ExternalOutput").ap())
    build(nc, *args)
    r = _run(nc, [arrays], core_ids=[0])
    got = np.asarray(r.results[0]["out_x"])
    return np.ascontiguousarray(got.transpose(2, 1, 0)).reshape(1, SEQ, D_MODEL)
```

```python
from contextlib import ExitStack

import numpy as np

import concourse.bass as bass
from concourse import mybir

F32 = mybir.dt.float32
F32R = mybir.dt.float32r
I32 = mybir.dt.int32
ALU = mybir.AluOpType
ACT = mybir.ActivationFunctionType
AX_X = mybir.AxisListType.X

P = 128
D_MODEL, SEQ, CTX, DEPTH, GRID_W = 1024, 256, 256, 2, 64
TOK = CTX + SEQ
KT = D_MODEL // P
EPS = 1e-6
HEADS, DK, DV, RANK, TEMP, CHUNK = 4, 128, 256, 16, 16.0, 64
NCH = TOK // CHUNK
AQ, AKV, HD = 8, 2, 128
BLOCKS = 8
D_FF = 2816
FT = D_FF // P
UK, UC = 4, 256
RAW = 4
PLAIN = 2

GLA_QK_PAIRS, GLA_V_PAIRS, R_PAIRS = 4, 4, 4
ATT_Q_PAIRS = 4
DOWN_UNITS = -(-FT // UK)
DOWN_LAST = FT - UK * (DOWN_UNITS - 1)
SPLIT_UNITS = 2 * (GLA_QK_PAIRS + GLA_V_PAIRS + R_PAIRS + 8 + ATT_Q_PAIRS + 2 + 8 + 4 + 4 + 8 + 4 + FT) + 4 * DOWN_UNITS
ADA_UNITS = 6 * D_MODEL // UC * 2
ADA_FIRST = 16
SIDE = {(0, "r"): (0, 1, 2, 3), (0, "br0"): (0, 1, 2, 3), (0, "aq"): (0, 1, 2, 3), (0, "up"): (0, 1, 2, 3),
        (0, "down"): (0, 1), (0, "br1"): (0, 2), (1, "br1"): (0, 2)}

PCOLS = {}
_at = 0
for _n, _w in (("b_ada", 48), ("gains", 32), ("b_dec", 8), ("g_gla", 8), ("g_qk", 10), ("cw", 32), ("cb", 8),
               ("b_gate", 32), ("lam", 16), ("fw", 3 * 2 * FT), ("fb", 2 * FT)):
    PCOLS[_n] = (_at, _at + _w)
    _at += _w
NPAR = _at

CONSTS, READY = 20, 3


class Chain:

    def __init__(self, eng, sem):
        self.eng, self.sem, self.base, self.k, self.i, self.stride = eng, sem, 0, 0, None, 0

    def link(self, ins):
        ins.then_inc(self.sem, 1)
        self.k += 1
        at = self.base + self.k
        self.eng.wait_ge(self.sem, at if self.i is None else self.i * self.stride + at)

    def enter(self, i, stride):
        self.base, self.k, self.i, self.stride = self.base + self.k, 0, i, stride

    def leave(self, times):
        assert self.k == self.stride, (self.k, self.stride)
        self.base, self.k, self.i = self.base + times * self.stride, 0, None


def build(nc, xt, cvec, weights, w_ada, w_gate, w_lr, w_dec, params, rope, out):
    with ExitStack() as ctx:
        def sb(name, shape, dt=F32):
            return ctx.enter_context(nc.sbuf_tensor(name, shape, dt))

        def sem(name):
            return ctx.enter_context(nc.semaphore(name))

        ident = sb("ident", [P, P])
        ones = sb("ones", [P, P])
        swap = sb("swap", [P, P])
        cs = sb("cs", [P, 2, SEQ])
        scanmask = sb("scanmask", [P, NCH, CHUNK])
        keep = sb("keep", [P, 2, P])
        par = sb("par", [P, DEPTH, NPAR])
        cin = sb("cin", [P, KT, 2])
        csil = sb("csil", [P, KT, 2])
        mod = sb("mod", [P, DEPTH, ADA_UNITS // 2, 2, 2])
        gmod = sb("gmod", [P, 4, KT, 2])
        hbias = sb("hbias", [P, 32])
        sp = sb("sp", [P, 3, 16])
        wdec = sb("wdec", [2 * RANK, 2, HEADS * DK])
        wdh = sb("wdh", [2 * RANK, 2, DK])
        rstd = sb("rstd", [P, TOK])
        g_end = sb("g_end", [P, 2, NCH])
        one, eps = sb("one", [P, 1]), sb("eps", [P, 1])
        mx = sb("mx", [P, 4, 2])
        nb = sb("nb", [P, 4, 2])
        sums = sb("sums", [P, 4, 2])
        rsum = sb("rsum", [P, 4, 2])

        SLOT = 4 * TOK
        base = -(-nc.sbuf_base // 64) * 64
        slots = (nc.sbuf_usable_end - base) // SLOT
        ctx.enter_context(nc.sbuf_tensor("arena", [P, slots * TOK], F32, align_bytes=64))

        def at(name, slot, shape, dt=F32, extra=0):
            size = 4 * int(np.prod(shape[1:]))
            assert slot * SLOT + extra + size <= slots * SLOT, (name, slot, size, slots)
            return nc.alloc_sbuf_tensor_at(name, shape, dt, offset=base + slot * SLOT + extra)

        def tiles(name, slot, n, dt=F32):
            return at(name, slot, [P, n, TOK], dt)

        X, H, WR, WS, PL = 0, 8, 24, 32, 40
        M = 44
        B = M + 8
        A = B + 16
        T = A + 16
        x = tiles("x", X, KT)
        hh, hl = tiles("hh", H, KT, F32R), tiles("hl", H + KT, KT, F32R)
        wraw = [at(f"wraw{i}", WR + 2 * i, [P, UK, UC]) for i in range(RAW)]
        whi = [at(f"whi{i}", WS + 2 * i, [P, UK, UC], F32R) for i in range(2)]
        wlo = [at(f"wlo{i}", WS + 4 + 2 * i, [P, UK, UC], F32R) for i in range(2)]
        wada = [at(f"wada{i}", PL + 2 * i, [P, UK, UC]) for i in range(PLAIN)]
        wgate = [at(f"wgate{i}", PL + 2 * i, [P, 4, P]) for i in range(PLAIN)]
        mixed = tiles("mixed", M, KT)
        bh, bl = tiles("bh", B, KT, F32R), tiles("bl", B + KT, KT, F32R)
        ada_first = [at(f"ada_first{i}", s_, [P, 4, UK, UC]) for i, s_ in enumerate((M, A, A + 8, T))]
        sq, nt = tiles("sq", B, KT), tiles("nt", B + KT, KT)
        gqk = at("gqk", A, [P, HEADS, 2, TOK])
        gv = at("gv", A + 8, [P, TOK // P, HEADS * DV])
        go = at("go", T + 0, [P, 2, TOK])
        gl_l = tiles("gl_l", B, 2)
        gl_m = tiles("gl_m", B + 2, 2)
        gl_c = tiles("gl_c", B + 4, 2)
        gl_ep = tiles("gl_ep", B + 6, 2)
        gl_ki = tiles("gl_ki", B + 8, 2)
        gl_ke = tiles("gl_ke", B + 10, 2)
        gl_qd = tiles("gl_qd", B + 12, 2)
        lr = at("lr", B + 14, [2 * RANK, TOK])
        state = at("state", M, [P, 2, NCH, DV])
        attm = tiles("attm", T + 2, 2)
        vh = at("vh", T + 4, [P, TOK // P, DV])
        keT = at("keT", T + 6, [P, 2, TOK // P, P])
        gstat = tiles("gstat", T + 8, 1)
        lrw = at("lrw", B, [P, KT, 2 * RANK])
        lrh = at("lrh", B + 2, [P, KT, P], F32R)
        lrl = at("lrl", B + 4, [P, KT, P], F32R)
        ev = [tiles(f"ev{i}", T + 4 * i, 2) for i in range(2)]
        evp = [tiles(f"evp{i}", T + 2 + 4 * i, 2) for i in range(2)]
        aqk = tiles("aqk", A, AQ + AKV)
        av = at("av", A + AQ + AKV, [P, TOK // P, AKV * HD])
        astat = tiles("astat", B, AQ + AKV)
        asq = [tiles(f"asq{i}", T + i, 1) for i in range(2)]
        arot = [at(f"arot{i}", T + 2 + i, [P, 2, SEQ]) for i in range(2)]
        qcur = [tiles(f"qcur{i}", A + 12 + i, 1) for i in range(2)]
        prob = [tiles(f"prob{i}", T + 2 * i, 2) for i in range(2)]
        probT = [at(f"probT{i}", T + 4 + 2 * i, [P, TOK // P, SEQ]) for i in range(2)]
        xc = tiles("xc", A, BLOCKS)
        l_tr, l_ti, l_a, l_th = (tiles(n, A + 8 + 2 * i, 2) for i, n in enumerate(("l_tr", "l_ti", "l_a", "l_th")))
        l_a2 = tiles("l_a2", T + 4, 2)
        l_h = tiles("l_h", T + 6, 2)
        mh, ml = tiles("mh", A, KT, F32R), tiles("ml", A + KT, KT, F32R)
        fh, fl = tiles("fh", M, FT, F32R), tiles("fl", M + FT, FT, F32R)
        fa = [tiles(f"fa{i}", M + 2 * FT + 3 * i, 2) for i in range(2)]
        fs = [tiles(f"fs{i}", M + 2 * FT + 2 + 3 * i, 1) for i in range(2)]
        y2 = tiles("y2", H, KT)

        ps = ctx.enter_context(nc.psum_tensor("ps", [P, 8, 512], F32))
        PAIR = [ps[:, 0:2], ps[:, 2:4]]
        KEEP = keep[:].bitcast(I32)
        MOD = [mod[:, l].rearrange("p a f s -> p (a f) s") for l in range(DEPTH)]

        s_in, s_par = sem("x_loaded"), sem("params_loaded")
        s_const, s_ready = sem("pool_consts_made"), sem("vector_consts_made")
        raw_full = [sem(f"raw_full{i}") for i in range(RAW)]
        plain_full = [sem(f"plain_full{i}") for i in range(PLAIN)]
        s_hi, s_lo, s_used = sem("w_hi_made"), sem("w_lo_made"), sem("w_unit_used")
        ada_full = [sem(f"ada_first_full{i}") for i in range(4)]
        plain_used, s_ada = sem("ada_unit_used"), sem("ada_columns_taken")
        taken = [sem("pair0_taken"), sem("pair1_taken")]
        s_csil, s_mod = sem("cond_silu_made"), sem("mod_made")
        s_sq, s_stat, s_rstd = sem("squares_made"), sem("stat_done"), sem("rstd_made")
        s_nt, s_hhi, s_h = sem("scaled_made"), sem("h_hi_made"), sem("h_made")
        s_x = sem("x_updated")
        s_sp, s_c4 = sem("softplus_parts_made"), sem("softplus_made")
        s_lrw, s_wdec = sem("lr_weights_loaded"), sem("decay_weights_loaded")
        s_lrz, s_lrh, s_lrl = sem("lr_pad_zeroed"), sem("lr_hi_made"), sem("lr_lo_made")
        s_lrp, s_lr = sem("lr_done"), sem("lr_copied")
        s_wdz = sem("decay_weights_zeroed")
        s_wdh, s_vh, s_gz, s_ga, s_gl = sem("head_decay_weights_copied"), sem("head_values_copied"), sem("decay_logits_done"), sem("abs_made"), sem("ln_made")
        s_gc, s_ge, s_go = sem("cum_made"), sem("decay_exps_made"), sem("decayed_qk_made")
        s_keT, s_keTc, s_att, s_attm = sem("keT_done"), sem("keT_copied"), sem("gla_att_done"), sem("gla_att_masked")
        s_kv, s_state, s_o = sem("kv_done"), sem("states_made"), sem("gla_o_done")
        s_osq, s_ostat, s_orstd, s_on = sem("o_squares"), sem("o_stat"), sem("o_rstd"), sem("o_normed")
        s_eva, s_evp, s_evh, s_b = sem("evac_act"), sem("evac_product"), sem("evac_hi"), sem("split_pairs_made")
        s_asq, s_asd, s_aln = sem("att_squares"), sem("att_stat_done"), sem("att_ln_made")
        s_arstd, s_anorm, s_arot, s_arope = sem("att_rstd"), sem("att_normed"), sem("att_swapped"), sem("att_roped")
        s_qc, s_sc, s_nb, s_ex = sem("q_copied"), sem("scores_done"), sem("neg_max_made"), sem("probs_exped")
        s_pn, s_pt, s_ptc, s_av = sem("probs_normed"), sem("probs_transposed"), sem("probsT_copied"), sem("att_out_done")
        s_ahi, s_alo = sem("att_hi"), sem("att_lo")
        s_lz, s_ltz, s_lt, s_la2 = sem("lru_logits_done"), sem("lru_logits_taken"), sem("lru_exps_made"), sem("lru_squares")
        s_lv, s_ls, s_lh = sem("lru_v_made"), sem("lru_sqrt_made"), sem("lru_h_made")
        s_fa, s_fs = sem("ffn_centre_tap"), sem("ffn_silu")
        s_c_act, s_c_dve = sem("act_chain"), sem("dve_chain")
        s_out = sem("out_stored")

        block = ctx.enter_context(nc.Block())

        def pcol(l, name):
            a, b = PCOLS[name]
            return par[:, l, a:b]

        def c0_of(l):
            return 0 if l < DEPTH - 1 else CTX

        def segs_of(c0):
            return [s for s in range(2) if (s + 1) * CTX > c0]

        stages = [("gqk", 4, 2), ("gv", 4, 2), ("r", 4, 2), ("br0", 8, 2), ("aq", 4, 2), ("akv", 2, 2), ("lx", 4, 2),
                  ("br1", 8, 2), ("y", 4, 2), ("br2", 8, 2), ("out", 4, 2), ("up", FT, 2), ("down", 4, DOWN_UNITS)]
        pairs_of = {n: c for n, c, _ in stages}
        units_of = {n: m for n, _, m in stages}
        order = [(l, n) for l in range(DEPTH) for n, _, _ in stages]
        first_unit, first_pair = {}, {}
        u = q = 0
        for l, name in order:
            first_unit[l, name], first_pair[l, name] = u, q
            u, q = u + pairs_of[name] * units_of[name], q + pairs_of[name]
        assert u == DEPTH * SPLIT_UNITS and all(v % 4 == 0 for v in first_unit.values())

        def side_before(l, name, kinds=("ada", "gate")):
            n = order.index((l, name))
            return sum(len(SIDE.get(k, ())) * pairs_of[k[1]] // 2 for k in order[:n]
                       if ("gate" if k[1] == "br1" else "ada") in kinds)

        def takes_before(l, name):
            return 1 + sum(pairs_of[n] // 2 for k, n in order[:order.index((l, name))] if (k, n) in SIDE and n != "br1")

        ADA_TAKES = takes_before(1, "gqk")

        def gla_turns(eng, chain, stride, turn):
            turn(0, False, True)
            with eng.Fori(0, HEADS - 2) as i:
                if chain:
                    chain.enter(i, stride)
                turn(i + 1, True, True)
                if chain:
                    chain.leave(HEADS - 2)
            turn(HEADS - 1, True, False)

        def ds(first, n):
            return slice(first, first + n) if isinstance(first, int) else bass.ds(first, n)

        def before(group, l, name):
            n = order.index((l, name))
            return sum(pairs_of[s] // (2 if s[:2] == "br" else 1) for _, s in order[:n] if s in group)

        PRODUCTS = ("r", "y", "br2", "up")
        CENTRES = ("lx", "up")

        def wait_taken(eng, l, name):
            n = (first_pair[l, name] + pairs_of[name]) // 2
            for j in range(2):
                eng.wait_ge(taken[j], n + 1)

        CHUNK_ORDER = [list(range(NCH)), [3, 2, 1, 0, 7, 6, 5, 4]]
        KV_BANK = (2, 6)
        HSCALE = HD ** -0.5

        def att_items(l):
            return 16 * l, len(segs_of(c0_of(l)))

        @block.sync
        def _(sp_):
            def load_stage(l, name):
                n, last = 2 * units_of[name], (l, name) == order[-1]
                turns, side = pairs_of[name] // 2, SIDE.get((l, name), ())
                u0, r0, a0 = first_unit[l, name], side_before(l, name), side_before(l, name, ("ada",))
                if side and name == "br1":
                    sp_.wait_ge(plain_used, ADA_FIRST // 2 + a0)
                elif side:
                    sp_.wait_ge(s_lz, 2 * side_before(l, name, ("gate",)) + 4)

                def turn(i, final):
                    for o in range(n):
                        s = o % RAW
                        if not (final and o >= n - RAW):
                            sp_.wait_ge(s_lo, i * n + (u0 + o + 1))
                            sp_.dma_start(wraw[s][:], weights[i * n + (u0 + RAW + o)]).then_inc(raw_full[s], 16)
                        if o not in side:
                            continue
                        k = side.index(o)
                        if name == "br1":
                            sp_.wait_ge(s_lz, i * 4 + (2 * BLOCKS * l + 2 * k + 2))
                            sp_.dma_start(wgate[k][:], w_gate[i * 2 + (BLOCKS * l + k)]).then_inc(plain_full[k], 16)
                        else:
                            sp_.wait_ge(plain_used, i * len(side) + (ADA_FIRST // 2 + a0 + k - 1))
                            sp_.dma_start(wada[k % 2][:], w_ada[i * len(side) + (ADA_FIRST + a0 + k)])\
                                .then_inc(plain_full[k % 2], 16)

                with sp_.Fori(0, turns - last) as i:
                    turn(i, False)
                if last:
                    turn(turns - 1, True)

            sp_.dma_start(x[:], xt).then_inc(s_in, 16)
            for u in range(0, ADA_FIRST, 2):
                sp_.dma_start(ada_first[u // 4][:, u % 4], w_ada[u]).then_inc(ada_full[u // 4], 16)
            for s in range(RAW):
                sp_.dma_start(wraw[s][:], weights[s]).then_inc(raw_full[s], 16)
            for l, name in order:
                load_stage(l, name)
            sp_.wait_ge(s_x, KT * 2 * DEPTH)
            sp_.dma_start(out, x[:, :, CTX:TOK]).then_inc(s_out, 16)
            sp_.wait_ge(s_out, 16)

        @block.gpsimd
        def _(pool):
            pool.dma_start(par[:], params).then_inc(s_par, 16)
            pool.dma_start(cin[:], cvec).then_inc(s_par, 16)
            pool.dma_start(cs[:], rope).then_inc(s_par, 16)
            nc.gpsimd.memset(ident[:], 0.0).then_inc(s_const, 1)
            nc.gpsimd.memset(swap[:], 0.0).then_inc(s_const, 1)
            nc.gpsimd.memset(keep[:], 1.0).then_inc(s_const, 1)
            made = 3

            def select(v, op, fill, base, pattern, mult):
                nonlocal made
                pool.wait_ge(s_const, made)
                nc.gpsimd.affine_select(out=v, in_=v, compare_op=op, fill=fill, base=base, pattern=pattern,
                                        channel_multiplier=mult).then_inc(s_const, 1)
                made += 1

            select(ident[:], ALU.not_equal, 1.0, 0, [[-1, P]], 1)
            for off, fill in ((32, -1.0), (-32, 1.0)):
                for axis in range(2):
                    m0 = 64 * axis + (0 if off > 0 else 32)
                    select(swap[:, m0:m0 + 32], ALU.not_equal, fill, -(m0 + off), [[-1, 32]], 1)
            for d, sign in enumerate((1, -1)):
                for c in range(P // CHUNK):
                    v = keep[:, d, c * CHUNK:(c + 1) * CHUNK]
                    select(v, ALU.is_ge, 0.0, -c * CHUNK, [[0, CHUNK]], 1)
                    select(v, ALU.is_ge, 0.0, (c + 1) * CHUNK - 1, [[0, CHUNK]], -1)
                    select(v, ALU.is_ge, 0.0, sign * c * CHUNK, [[sign, CHUNK]], -sign)
            assert made == CONSTS
            for l in range(DEPTH):
                if l:
                    pool.wait_ge(s_wdh, HEADS * l)
                nc.gpsimd.memset(wdec[:], 0.0).then_inc(s_wdz, 1)
                pool.wait_ge(s_wdz, l + 1)
                for d in range(2):
                    pool.dma_start(wdec[d * RANK:(d + 1) * RANK, d, :], w_dec[l, d]).then_inc(s_wdec, 16)
                pool.wait_ge(s_hhi, KT * (2 * l + 1))
                pool.dma_start(lrw[:], w_lr[l]).then_inc(s_lrw, 16)
                pool.wait_ge(s_wdec, 32 * (l + 1))
                if l:
                    pool.wait_ge(s_gz, HEADS * l)
                nc.gpsimd.tensor_copy(wdh[:], wdec[:, :, 0:DK]).then_inc(s_wdh, 1)
                wait_taken(pool, l, "gv")
                nc.gpsimd.tensor_copy(vh[:], gv[:, :, 0:DV]).then_inc(s_vh, 1)
                with pool.Fori(0, HEADS - 1) as i:
                    pool.wait_ge(s_gz, i + (HEADS * l + 1))
                    nc.gpsimd.tensor_copy(wdh[:], wdec[:, :, bass.ds(i * DK + DK, DK)]).then_inc(s_wdh, 1)
                    pool.wait_ge(s_o, i + (HEADS * l + 1))
                    nc.gpsimd.tensor_copy(vh[:], gv[:, :, bass.ds(i * DV + DV, DV)]).then_inc(s_vh, 1)
                pool.wait_ge(s_arope, (l + 1) * (AQ + AKV))
                n0, ng = att_items(l)
                c0 = c0_of(l)
                for kv in range(AKV):
                    with pool.Fori(0, 2) as i:
                        for j in range(2):
                            pool.wait_ge(s_alo, i * (2 * ng) + (4 + n0 + ng * (4 * kv + j - 1)))
                            nc.gpsimd.tensor_copy(qcur[j][:, 0, c0:], aqk[:, i * 2 + (4 * kv + j), c0:]).then_inc(s_qc, 1)
                with pool.Fori(0, BLOCKS) as i:
                    pool.wait_ge(s_lt, i + (BLOCKS * l + 1))
                    nc.gpsimd.tensor_tensor(l_a2[:], l_a[:], l_a[:], ALU.mult).then_inc(s_la2, 1)

        @block.scalar
        def _(act):
            chain = Chain(act, s_c_act)
            link = chain.link
            A_ = nc.scalar.activation

            def hi(b4, off):
                act.wait_ge(raw_full[off % RAW], b4 * 16 + (16 * (off // RAW) + 16))
                act.wait_ge(s_used, b4 * 4 + (off - 1))
                A_(whi[off % 2][:], wraw[off % RAW][:], ACT.Copy).then_inc(s_hi, 1)

            def pairs(l, name, evac, beside=None):
                m, last = units_of[name], (l, name) == order[-1]
                b, turns = first_unit[l, name] // 4, pairs_of[name] // 2

                def turn(i, b4, final):
                    for j in range(2):
                        for o in range(2 + m * j, m * (j + 1) + 2):
                            if not (final and o >= 2 * m):
                                hi(b4, o)
                            if beside:
                                beside(i, o - 2)
                        act.wait_ge(s_used, b4 * 4 + m * (j + 1))
                        evac(i, j)

                with act.Fori(0, turns - last) as i:
                    turn(i, i * (m // 2) + b, False)
                if last:
                    turn(turns - 1, b + (turns - 1) * (m // 2), True)

            def norm_stats(n, src, ready, c0):
                for j in range(4):
                    ready(2 * j + 2)
                    A_(sq[:, 2 * j:2 * j + 2, c0:], src[:, 2 * j:2 * j + 2, c0:], ACT.Square).then_inc(s_sq, 1)
                act.wait_ge(s_stat, n + 1)
                link(A_(rstd[:, c0:], ps[:, 6, c0:], ACT.Ln, scale=1.0 / D_MODEL, bias=eps[:]))
                A_(rstd[:, c0:], rstd[:, c0:], ACT.Exp, scale=-0.5).then_inc(s_rstd, 1)

            def make_h(l, n, shift, segs):
                for k in range(KT):
                    act.wait_ge(s_nt, KT * n + k + 1)
                    for s in segs:
                        c = slice(s * CTX, (s + 1) * CTX)
                        ins = A_(hh[:, k, c], nt[:, k, c], ACT.Identity, bias=MOD[l][:, 8 * shift + k, s:s + 1])
                    ins.then_inc(s_hhi, 1)

            for u in range(1, ADA_FIRST, 2):
                act.dma_start(ada_first[u // 4][:, u % 4], w_ada[u]).then_inc(ada_full[u // 4], 16)
            act.wait_ge(s_par, 48)
            act.wait_ge(s_ready, READY)
            A_(csil[:], cin[:], ACT.Silu).then_inc(s_csil, 1)
            act.wait_ge(s_in, 16)
            for l in range(DEPTH):
                c0, segs = c0_of(l), segs_of(c0_of(l))
                if l:
                    act.wait_ge(s_lh, BLOCKS * l + 1)
                link(A_(sp[:, 0], pcol(l, "lam"), ACT.Abs))
                link(A_(sp[:, 0], sp[:, 0], ACT.Exp, scale=-1.0))
                link(A_(sp[:, 0], sp[:, 0], ACT.Ln, bias=one[:]))
                A_(sp[:, 1], pcol(l, "lam"), ACT.Relu, scale=-1.0).then_inc(s_sp, 1)
                norm_stats(4 * l, x, (lambda k: act.wait_ge(s_x, KT * (2 * l - 1) + k)) if l else (lambda k: None), 0)
                act.wait_ge(s_mod, l + 1)
                make_h(l, 2 * l, 0, (0, 1))
                if l == 0:
                    for s in range(2):
                        act.wait_ge(raw_full[s], 16)
                        A_(whi[s][:], wraw[s][:], ACT.Copy).then_inc(s_hi, 1)

                def copy_gqk(i, j):
                    A_(gqk[:, i * 2 + j, 0, c0:], PAIR[j][:, 0, c0:], ACT.Copy)
                    A_(gqk[:, i * 2 + j, 1, :], PAIR[j][:, 1, :], ACT.Copy).then_inc(taken[j], 1)

                def copy_gv(i, j):
                    A_(gv[:, :, bass.ds(i * 512 + 256 * j, 256)], PAIR[j].rearrange("p a (b c) -> p (a b) c", c=256),
                       ACT.Copy).then_inc(taken[j], 1)

                pairs(l, "gqk", copy_gqk)
                pairs(l, "gv", copy_gv)

                act.wait_ge(s_lrw, 16 * (l + 1))
                act.wait_ge(s_lrz, 2 * (l + 1))
                A_(lrh[:, :, 0:2 * RANK], lrw[:], ACT.Copy).then_inc(s_lrh, 1)
                act.wait_ge(s_lrp, l + 1)
                A_(lr[:], ps[0:2 * RANK, 7, :], ACT.Copy).then_inc(s_lr, 1)

                def gla_prepare(h):
                    n = h + HEADS * l
                    act.wait_ge(s_gz, n + 1)
                    for d in range(2):
                        ins = A_(gl_l[:, d], ps[:, d], ACT.Abs, bias=pcol(l, "b_dec")[:, ds(h * 2 + d, 1)])
                    ins.then_inc(s_ga, 1)
                    act.wait_ge(s_ga, n + 1)
                    link(A_(gl_l[:], gl_l[:], ACT.Exp, scale=-1.0))
                    A_(gl_l[:], gl_l[:], ACT.Ln, bias=one[:]).then_inc(s_gl, 1)
                    act.wait_ge(s_gc, n + 1)
                    A_(gl_ke[:], gl_ke[:], ACT.Exp, scale=1.0 / TEMP).then_inc(s_ge, 1)
                    A_(gl_ki[:], gl_c[:], ACT.Exp, scale=-1.0 / TEMP).then_inc(s_ge, 1)
                    A_(gl_ep[:], gl_c[:], ACT.Exp, scale=1.0 / TEMP).then_inc(s_ge, 1)

                def gla_squares(h):
                    act.wait_ge(s_o, h + (HEADS * l + 1))
                    A_(go[:, :, c0:], ps[:, 4:6, c0:], ACT.Square).then_inc(s_osq, 1)

                def gla_rstd(h):
                    act.wait_ge(s_ostat, h + (HEADS * l + 1))
                    act.wait_ge(s_on, h + (HEADS * l + 1))
                    link(A_(gstat[:, 0, c0:], ps[:, 6, c0:], ACT.Ln, scale=1.0 / DV, bias=eps[:]))
                    A_(gstat[:, 0, c0:], gstat[:, 0, c0:], ACT.Exp, scale=-0.5).then_inc(s_orstd, 1)

                def gla_turn(h, prev, nxt):
                    if prev:
                        gla_squares(h - 1)
                    act.wait_ge(s_keT, h + (HEADS * l + 1))
                    A_(keT[:].rearrange("p d t k -> p d (t k)"), ps[:, 2:4], ACT.Copy).then_inc(s_keTc, 1)
                    if prev:
                        gla_rstd(h - 1)
                    if nxt:
                        gla_prepare(h + 1)

                gla_prepare(0)
                gla_turns(act, chain, 2, gla_turn)
                gla_squares(HEADS - 1)
                gla_rstd(HEADS - 1)

                def product(name, func):
                    n0 = before(PRODUCTS, l, name)

                    def evac(i, j):
                        act.wait_ge(s_evp, i * 2 + (n0 + j - 1)) if n0 + j - 1 > 0 else None
                        A_(ev[j][:, :, c0:], PAIR[j][:, :, c0:], func).then_inc(taken[j], 1)
                        act.wait_ge(s_evp, i * 2 + (n0 + j + 1))
                        A_(bh[:, bass.ds(i * 4 + 2 * j, 2), c0:], evp[j][:, :, c0:], ACT.Copy).then_inc(s_evh, 1)
                    return evac

                def gate(name):
                    def evac(i, j):
                        if j == 0:
                            act.wait_ge(taken[1], i + (first_pair[l, name] // 2 + 1))
                            A_(ev[0][:, :, c0:], PAIR[0][:, :, c0:], ACT.Tanh, scale=0.5).then_inc(taken[0], 1)
                        elif name == "br2":
                            act.wait_ge(s_evp, i + (before(PRODUCTS, l, name) + 1))
                            A_(mh[:, bass.ds(i * 2, 2), c0:], mixed[:, bass.ds(i * 2, 2), c0:], ACT.Copy, scale=0.5)\
                                .then_inc(s_evh, 1)
                    return evac

                pairs(l, "r", product("r", ACT.Silu))
                pairs(l, "br0", gate("br0"))

                def copy_aq(i, j):
                    A_(aqk[:, bass.ds(i * 4 + 2 * j, 2), c0:], PAIR[j][:, :, c0:], ACT.Copy).then_inc(taken[j], 1)

                def copy_akv(i, j):
                    if j == 0:
                        A_(aqk[:, AQ:], PAIR[0], ACT.Copy).then_inc(taken[0], 1)
                    else:
                        A_(av[:], PAIR[1].rearrange("p a (b c) -> p (a b) c", c=256), ACT.Copy).then_inc(taken[1], 1)

                pairs(l, "aq", copy_aq)
                pairs(l, "akv", copy_akv)

                wait_taken(act, l, "akv")
                t0 = (AQ + AKV) * l

                def att_stats(i, t, c):
                    for j in range(2):
                        act.wait_ge(s_asd, i * 2 + (t0 + t + j - 1)) if t0 + t + j > 1 else None
                        A_(asq[j][:, 0, c:], aqk[:, i * 2 + (t + j), c:], ACT.Square).then_inc(s_asq, 1)
                    for j in range(2):
                        act.wait_ge(s_asd, i * 2 + (t0 + t + j + 1))
                        A_(astat[:, i * 2 + (t + j), c:], ps[:, 4 + j, c:], ACT.Ln, scale=1.0 / HD, bias=eps[:])\
                            .then_inc(s_aln, 1)
                with act.Fori(0, AQ // 2) as i:
                    att_stats(i, 0, c0)
                att_stats(0, AQ, 0)
                act.wait_ge(s_aln, t0 + AQ + AKV)
                A_(astat[:, 0:AQ, c0:], astat[:, 0:AQ, c0:], ACT.Exp, scale=-0.5).then_inc(s_arstd, 1)
                A_(astat[:, AQ:], astat[:, AQ:], ACT.Exp, scale=-0.5).then_inc(s_arstd, 1)

                n0, ng = att_items(l)
                for kv in range(AKV):
                    with act.Fori(0, 2) as i:
                        def item(k):
                            return i * (2 * ng) + (n0 + 4 * ng * kv + k + 1)

                        def exps(k):
                            g, b = segs[k % ng], k % 2
                            act.wait_ge(s_nb, item(k))
                            for t in range(2):
                                ins = A_(prob[b][:, t, 0:(g + 1) * CTX], PAIR[b][:, t, 0:(g + 1) * CTX], ACT.Exp,
                                         scale=HSCALE, bias=nb[:, b, t:t + 1], accum_out=sums[:, b, t:t + 1])
                            ins.then_inc(s_ex, 1)

                        exps(0)
                        for k in range(2 * ng):
                            g, b = segs[k % ng], k % 2
                            if k + 1 < 2 * ng:
                                exps(k + 1)
                            act.wait_ge(s_pt, item(k))
                            A_(probT[b][:, 0:2 * g + 2], ps[:, 4:6].rearrange("p a (b c) -> p (a b) c", c=SEQ)[:, 0:2 * g + 2],
                               ACT.Copy).then_inc(s_ptc, 1)
                            act.wait_ge(s_av, item(k))
                            A_(bh[:, i * 2 + (4 * kv + k // ng), g * CTX:(g + 1) * CTX], ps[:, 6 + b, 0:SEQ], ACT.Copy)\
                                .then_inc(s_ahi, 1)

                def centre(name, dst, w, bias, c, tile):
                    def evac(i, j):
                        for f in range(2):
                            ins = A_(dst(i, j, f)[:, c:], PAIR[j][:, f, c:], ACT.Identity,
                                     scale=pcol(l, w)[:, bass.ds(tile(i, j, f), 1)],
                                     bias=pcol(l, bias)[:, bass.ds(tile(i, j, f), 1)] if w != "cw" else
                                     pcol(l, bias)[:, bass.ds(i * 4 + (2 * j + f), 1)])
                        ins.then_inc(s_eva, 1)
                    return evac

                pairs(l, "lx", centre("lx", lambda i, j, f: xc[:, i * 4 + (2 * j + f)], "cw", "cb", 0,
                                      lambda i, j, f: i * 4 + (2 * KT + 2 * j + f)))

                act.wait_ge(s_c4, l + 1)

                def lru(i, o):
                    j = o // 2
                    if o % 2:
                        act.wait_ge(s_lv, i * 2 + (BLOCKS * l + j + 1))
                        A_(l_tr[:], l_a2[:], ACT.Sqrt, scale=-0.25).then_inc(s_ls, 1)
                        return
                    act.wait_ge(s_lh, i * 2 + (BLOCKS * l + j + 1))
                    for d in range(2):
                        act.wait_ge(s_lz, i * 4 + (2 * BLOCKS * l + 2 * j + d + 5))
                        for g, buf in enumerate((l_tr, l_ti)):
                            ins = A_(buf[:, d], ps[:, 4 + 2 * d + g], ACT.Tanh, scale=0.5,
                                     bias=hbias[:, bass.ds(i * 8 + (4 * j + 2 * d + g), 1)])
                        ins.then_inc(s_ltz, 1)
                    act.wait_ge(s_ltz, i * 4 + (2 * BLOCKS * l + 2 * j + 4))
                    for d in range(2):
                        k4 = sp[:, 2, bass.ds(i * 4 + (2 * j + d), 1)]
                        A_(l_a[:, d], l_tr[:, d], ACT.Exp, scale=k4, bias=k4)
                        ins = A_(l_th[:, d], l_tr[:, d], ACT.Tanh, scale=k4, bias=k4)
                    ins.then_inc(s_lt, 1)

                pairs(l, "br1", gate("br1"), lru)
                act.wait_ge(s_lh, BLOCKS * (l + 1) + 1)
                wait_taken(act, l, "br1")
                pairs(l, "y", product("y", ACT.Gelu_apprx_tanh))
                pairs(l, "br2", gate("br2"))

                def copy_out(i, j):
                    A_(mixed[:, bass.ds(i * 4 + 2 * j, 2), c0:], PAIR[j][:, :, c0:], ACT.Copy).then_inc(taken[j], 1)

                pairs(l, "out", copy_out)

                def taken_tiles(name):
                    q0 = (first_pair[l, name]) // 2
                    return lambda k: act.wait_ge(taken[(k // 2 - 1) % 2], q0 + (k // 2 - 1) // 2 + 2)

                norm_stats(4 * l + 1, mixed, taken_tiles("out"), c0)
                norm_stats(4 * l + 2, x, lambda k: act.wait_ge(s_x, KT * 2 * l + k), c0)
                make_h(l, 2 * l + 1, 3, segs)

                n_p = before(PRODUCTS, l, "up")
                tap = centre("up", lambda i, j, f: fa[j][:, f], "fw", "fb", c0, None)

                def up(i, j):
                    for f in range(2):
                        t = i * 4 + (2 * j + f)
                        ins = A_(fa[j][:, f, c0:], PAIR[j][:, f, c0:], ACT.Identity,
                                 scale=pcol(l, "fw")[:, bass.ds(t + 2 * FT, 1)], bias=pcol(l, "fb")[:, bass.ds(t, 1)])
                    ins.then_inc(s_eva, 1)
                    act.wait_ge(taken[j], i + (first_pair[l, "up"] // 2 + 2))
                    A_(fs[j][:, 0, c0:], fa[j][:, 0, c0:], ACT.Silu).then_inc(s_fs, 1)
                    act.wait_ge(s_evp, i * 2 + (n_p + j + 1))
                    A_(fh[:, i * 2 + j, c0:], fa[j][:, 1, c0:], ACT.Copy).then_inc(s_evh, 1)

                pairs(l, "up", up)

                def copy_down(i, j):
                    A_(y2[:, bass.ds(i * 4 + 2 * j, 2), c0:] if not isinstance(i, int) else
                       y2[:, i * 4 + 2 * j:i * 4 + 2 * j + 2, c0:], PAIR[j][:, :, c0:], ACT.Copy).then_inc(taken[j], 1)

                pairs(l, "down", copy_down)
                norm_stats(4 * l + 3, y2, taken_tiles("down"), c0)

        @block.vector
        def _(dve):
            chain = Chain(dve, s_c_dve)
            link = chain.link
            V = nc.vector

            def lo(b4, off):
                dve.wait_ge(s_hi, b4 * 4 + (off + 1))
                V.tensor_tensor(wlo[off % 2][:], wraw[off % RAW][:], whi[off % 2][:].bitcast(F32), ALU.subtract)\
                    .then_inc(s_lo, 1)

            def pairs(l, name, evac, stride=0, beside=None):
                m, last = units_of[name], (l, name) == order[-1]
                b, turns = first_unit[l, name] // 4, pairs_of[name] // 2

                def turn(i, b4, final):
                    for j in range(2):
                        for o in range(2 + m * j, m * (j + 1) + 2):
                            if not (final and o >= 2 * m):
                                lo(b4, o)
                            if beside:
                                beside(i, o - 2)
                        if evac:
                            evac(i, j)
                    if name != "br1" and (l, name) in SIDE:
                        take_mod(l, name, i)

                with dve.Fori(0, turns - last) as i:
                    chain.enter(i, stride)
                    turn(i, i * (m // 2) + b, False)
                    chain.leave(turns - last)
                if last:
                    turn(turns - 1, b + (turns - 1) * (m // 2), True)

            def take_mod(l, name, i):
                n = len(SIDE[l, name])
                a0 = ADA_FIRST + side_before(l, name, ("ada",))
                layer, first = a0 // ADA_UNITS, a0 % ADA_UNITS // 2
                dve.wait_ge(plain_used, i * n + (a0 - ADA_FIRST // 2 + n))
                add_bias(layer, i * (n // 2) + first, n // 2)

            def add_bias(layer, a, n):
                for f in range(2):
                    ins = V.tensor_tensor(mod[:, layer, bass.ds(a, n), f, :],
                                          ps[:, 4 + f, 0:2 * n].rearrange("p (a s) -> p a s", s=2),
                                          pcol(layer, "b_ada").rearrange("p (a f) -> p a f", f=2)[:, bass.ds(a, n), f, None]
                                          .broadcast_to([P, n, 2]), ALU.add)
                ins.then_inc(s_ada, 1)

            def gains(l, norms):
                for n in norms:
                    m, plus = ((1, 1.0), (2, 0.0), (4, 1.0), (5, 0.0))[n]
                    link(V.scalar_tensor_tensor(gmod[:, n], MOD[l][:, 8 * m:8 * m + 8], plus,
                                                pcol(l, "gains")[:, 8 * n:8 * n + 8, None].broadcast_to([P, KT, 2]),
                                                ALU.add, ALU.mult))

            def split_h(l, n, gain, shift, segs):
                c0 = segs[0] * CTX
                dve.wait_ge(s_rstd, n_stat[n] + 1)
                for k0 in range(0, KT, 2):
                    for k in (k0, k0 + 1):
                        for s in segs:
                            c = slice(s * CTX, (s + 1) * CTX)
                            ins = V.scalar_tensor_tensor(nt[:, k, c], x[:, k, c], gmod[:, gain, k, s:s + 1], rstd[:, c],
                                                         ALU.mult, ALU.mult)
                        ins.then_inc(s_nt, 1)
                    for k in (k0, k0 + 1):
                        dve.wait_ge(s_hhi, KT * n + k + 1)
                        for s in segs:
                            c = slice(s * CTX, (s + 1) * CTX)
                            ins = V.scalar_tensor_tensor(hl[:, k, c], nt[:, k, c], MOD[l][:, 8 * shift + k, s:s + 1],
                                                         hh[:, k, c].bitcast(F32), ALU.add, ALU.subtract)
                        ins.then_inc(s_h, 1)

            def residual(n, src, gain, segs):
                dve.wait_ge(s_rstd, n + 1)
                for k in range(KT):
                    for s in segs:
                        c = slice(s * CTX, (s + 1) * CTX)
                        link(V.scalar_tensor_tensor(src[:, k, c], src[:, k, c], gmod[:, gain, k, s:s + 1], rstd[:, c],
                                                    ALU.mult, ALU.mult))
                    c = slice(segs[0] * CTX, TOK)
                    V.tensor_tensor(x[:, k, c], x[:, k, c], src[:, k, c], ALU.add).then_inc(s_x, 1)

            n_stat = {0: 0, 1: 2, 2: 4, 3: 6}
            V.memset(ones[:], 1.0).then_inc(s_ready, 1)
            V.memset(one[:], 1.0).then_inc(s_ready, 1)
            V.memset(eps[:], EPS).then_inc(s_ready, 1)
            link(V.memset(scanmask[:], 1.0))
            link(V.memset(scanmask[:, :, 0:1], 0.0))
            for s, k in ((taken[0], 1), (taken[1], 1), (s_ltz, 2), (s_on, 1), (s_lz, 4), (s_lh, 1), (s_alo, 4)):
                dve.sem_inc(s, k)
            dve.wait_ge(s_par, 48)
            dve.wait_ge(s_const, CONSTS)
            dve.wait_ge(s_in, 16)
            for l in range(DEPTH):
                c0, segs = c0_of(l), segs_of(c0_of(l))
                W = TOK - c0
                if l == 0:
                    dve.wait_ge(plain_used, ADA_FIRST // 2)
                    add_bias(0, 0, ADA_FIRST // 2)
                dve.wait_ge(s_ada, 1 if l == 0 else ADA_TAKES)
                gains(l, range(4) if l else (0,))
                link(V.tensor_scalar(hbias[:], pcol(l, "b_gate"), 0.5, None, ALU.mult))
                dve.wait_ge(s_sp, l + 1)
                link(V.tensor_tensor(sp[:, 0], sp[:, 0], sp[:, 1], ALU.add))
                V.tensor_scalar(sp[:, 2], sp[:, 0], -4.0, None, ALU.mult).then_inc(s_c4, 1)
                V.memset(attm[:], 0.0).then_inc(s_mod, 1)
                split_h(l, 2 * l, 0, 0, (0, 1))
                if l == 0:
                    for s in range(2):
                        dve.wait_ge(s_hi, s + 1)
                        V.tensor_tensor(wlo[s][:], wraw[s][:], whi[s][:].bitcast(F32), ALU.subtract).then_inc(s_lo, 1)
                pairs(l, "gqk", None)
                pairs(l, "gv", None)

                dve.wait_ge(s_lrw, 16 * (l + 1))
                V.memset(lrh[:].bitcast(F32), 0.0).then_inc(s_lrz, 1)
                V.memset(lrl[:].bitcast(F32), 0.0).then_inc(s_lrz, 1)
                dve.wait_ge(s_lrh, l + 1)
                V.tensor_tensor(lrl[:, :, 0:2 * RANK], lrw[:], lrh[:, :, 0:2 * RANK].bitcast(F32), ALU.subtract)\
                    .then_inc(s_lrl, 1)

                def chunks(v):
                    return v.rearrange("p (n c) -> p n c", c=CHUNK)

                def gla_prepare(h):
                    n = h + HEADS * l
                    dve.wait_ge(s_ga, n + 1)
                    for d in range(2):
                        ins = V.tensor_scalar(gl_m[:, d], ps[:, d], pcol(l, "b_dec")[:, ds(h * 2 + d, 1)], 0.0,
                                              ALU.add, ALU.min)
                    link(ins)
                    dve.wait_ge(s_gl, n + 1)
                    link(V.tensor_tensor(gl_m[:], gl_m[:], gl_l[:], ALU.subtract))
                    mask = scanmask[:].rearrange("p n c -> p (n c)")
                    V.tensor_tensor_scan(gl_c[:, 0], mask, gl_m[:, 0], 0.0, ALU.mult, ALU.add)
                    link(V.tensor_tensor_scan(gl_c[:, 1, ::-1], mask, gl_m[:, 1, ::-1], 0.0, ALU.mult, ALU.add))
                    for d, end in enumerate((CHUNK - 1, 0)):
                        v = chunks(gl_c[:, d])
                        ins = V.tensor_tensor(chunks(gl_ke[:, d]), v[:, :, end:end + 1].broadcast_to([P, NCH, CHUNK]), v,
                                              ALU.subtract)
                    ins.then_inc(s_gc, 1)
                    k = gqk[:, h, 1:2, :].broadcast_to([P, 2, TOK])
                    dve.wait_ge(s_ge, n * 3 + 1)
                    V.tensor_tensor(gl_ke[:], gl_ke[:], k, ALU.mult).then_inc(s_go, 1)
                    dve.wait_ge(s_ge, n * 3 + 2)
                    V.tensor_tensor(gl_ki[:, :, c0:], gl_ki[:, :, c0:], k[:, :, c0:], ALU.mult).then_inc(s_go, 1)

                def gla_states(h, d):
                    n = h + HEADS * l
                    for e in range(4):
                        dve.wait_ge(s_kv, n * 8 + (4 * d + e + 1))
                        for p in range(2 * e, min(2 * e + 2, NCH - 1)):
                            c = CHUNK_ORDER[d][p]
                            kv_ = ps[:, KV_BANK[e % 2] + c % 2, 0:DV]
                            if p == 0:
                                ins = V.tensor_copy(state[:, d, 1], kv_)
                            else:
                                ins = V.scalar_tensor_tensor(state[:, d, p + 1], state[:, d, p], g_end[:, d, c:c + 1],
                                                             kv_, ALU.mult, ALU.add)
                            if p % 2 or p == NCH - 2:
                                ins.then_inc(s_state, 1)
                                dve.wait_ge(s_state, n * 8 + (4 * d + e + 1))
                            else:
                                link(ins)

                def gla_norm(h):
                    dve.wait_ge(s_orstd, h + (HEADS * l + 1))
                    for t in range(2):
                        ins = V.scalar_tensor_tensor(gqk[:, h, t, c0:], ps[:, 4 + t, c0:],
                                                     pcol(l, "g_gla")[:, ds(h * 2 + t, 1)], gstat[:, 0, c0:],
                                                     ALU.mult, ALU.mult)
                    ins.then_inc(s_on, 1)

                def gla_turn(h, prev, nxt):
                    n = h + HEADS * l
                    if prev:
                        dve.wait_ge(s_o, n)
                    dve.wait_ge(s_ge, n * 3 + 3)
                    q = gqk[:, h, 0:1, c0:].broadcast_to([P, 2, W])
                    V.scalar_tensor_tensor(gl_qd[:, :, c0:], q, DK ** -0.5, gl_ep[:, :, c0:], ALU.mult, ALU.mult)\
                        .then_inc(s_go, 1)
                    dve.wait_ge(s_att, n + 1)
                    for d, end in enumerate((CHUNK - 1, 0)):
                        V.tensor_copy(g_end[:, d], chunks(gl_ep[:, d])[:, :, end])
                    for d in range(2):
                        v = slice(c0 // P, TOK // P)
                        V.copy_predicated(attm[:, d].rearrange("p (t c) -> p t c", c=P)[:, v],
                                          KEEP[:, d:d + 1].broadcast_to([P, (TOK - c0) // P, P]),
                                          ps[:, d].rearrange("p (t c) -> p t c", c=P)[:, v]).then_inc(s_attm, 1)
                    dve.wait_ge(s_attm, n * 2 + 2)
                    gla_states(h, 0)
                    if prev:
                        gla_norm(h - 1)
                    gla_states(h, 1)
                    if nxt:
                        gla_prepare(h + 1)

                gla_prepare(0)
                gla_turns(dve, chain, 9, gla_turn)
                gla_norm(HEADS - 1)

                def product(name, other):
                    n0, q0 = before(PRODUCTS, l, name), first_pair[l, name]

                    def evac(i, j):
                        dve.wait_ge(taken[j], i + (q0 // 2 + 2))
                        V.tensor_tensor(evp[j][:, :, c0:], ev[j][:, :, c0:], other(i, j), ALU.mult).then_inc(s_evp, 1)
                        dve.wait_ge(s_evh, i * 2 + (n0 + j + 1))
                        t = bass.ds(i * 4 + 2 * j, 2)
                        V.tensor_tensor(bl[:, t, c0:], evp[j][:, :, c0:], bh[:, t, c0:].bitcast(F32), ALU.subtract)\
                            .then_inc(s_b, 1)
                    return evac

                def gate(name):
                    def evac(i, j):
                        if j == 0:
                            return
                        tiles_ = bass.ds(i * 2, 2)
                        b4 = i + first_unit[l, name] // 4
                        dve.wait_ge(s_used, b4 * 4 + 4)
                        dve.wait_ge(taken[0], i + (first_pair[l, name] // 2 + 2))
                        dst = mixed[:, tiles_, c0:] if name == "br0" else evp[0][:, :, c0:]
                        V.scalar_tensor_tensor(dst, ev[0][:, :, c0:], 1.0, PAIR[1][:, :, c0:], ALU.add, ALU.mult)\
                            .then_inc(taken[1], 1)
                        if name == "br0":
                            return
                        dve.wait_ge(taken[1], i + (first_pair[l, name] // 2 + 2))
                        ins = V.tensor_tensor(mixed[:, tiles_, c0:], mixed[:, tiles_, c0:], evp[0][:, :, c0:], ALU.add)
                        if name == "br1":
                            link(ins)
                        else:
                            ins.then_inc(s_evp, 1)
                            dve.wait_ge(s_evh, i + (before(PRODUCTS, l, name) + 1))
                            V.scalar_tensor_tensor(ml[:, tiles_, c0:], mixed[:, tiles_, c0:], 0.5,
                                                   mh[:, tiles_, c0:].bitcast(F32), ALU.mult, ALU.subtract)\
                                .then_inc(s_b, 1)
                    return evac

                pairs(l, "r", product("r", lambda i, j: gqk[:, i * 2 + j, :, c0:]))
                pairs(l, "br0", gate("br0"))
                pairs(l, "aq", None)
                if l == 0:
                    dve.wait_ge(s_ada, takes_before(l, "akv"))
                    gains(l, (1, 2, 3))
                pairs(l, "akv", None)

                t0 = (AQ + AKV) * l

                def att_norm(i, t, c):
                    for j in range(2):
                        v = aqk[:, i * 2 + (t + j), c:]
                        V.scalar_tensor_tensor(v, v, pcol(l, "g_qk")[:, bass.ds(i * 2 + (t + j), 1)],
                                               astat[:, i * 2 + (t + j), c:], ALU.mult, ALU.mult).then_inc(s_anorm, 1)
                    for j in range(2):
                        v = aqk[:, i * 2 + (t + j), CTX:]
                        dve.wait_ge(s_anorm, i * 2 + (t0 + t + j + 1))
                        V.tensor_tensor(arot[j][:, 1], v, cs[:, 0], ALU.mult)
                        dve.wait_ge(s_arot, i * 2 + (t0 + t + j + 1))
                        link(V.tensor_tensor(arot[j][:, 0], ps[:, 4 + j, 0:SEQ], cs[:, 1], ALU.mult))
                        V.tensor_tensor(v, arot[j][:, 0], arot[j][:, 1], ALU.add).then_inc(s_arope, 1)
                dve.wait_ge(s_arstd, 2 * l + 2)
                with dve.Fori(0, AQ // 2) as i:
                    chain.enter(i, 2)
                    att_norm(i, 0, c0)
                    chain.leave(AQ // 2)
                att_norm(0, AQ, 0)

                n0, ng = att_items(l)
                for kv in range(AKV):
                    with dve.Fori(0, 2) as i:
                        chain.enter(i, 4 * ng)

                        def item(k):
                            return i * (2 * ng) + (n0 + 4 * ng * kv + k + 1)

                        def row_max(k):
                            g, b = segs[k % ng], k % 2
                            dve.wait_ge(s_sc, item(k))
                            link(V.tensor_reduce(mx[:, b], PAIR[b][:, :, 0:(g + 1) * CTX], AX_X, ALU.max))
                            V.tensor_scalar(nb[:, b], mx[:, b], -HSCALE, None, ALU.mult).then_inc(s_nb, 1)

                        row_max(0)
                        for k in range(2 * ng):
                            g, b = segs[k % ng], k % 2
                            if k + 1 < 2 * ng:
                                row_max(k + 1)
                            dve.wait_ge(s_ex, item(k))
                            link(V.reciprocal(rsum[:, b], sums[:, b]))
                            for t in range(2):
                                v = prob[b][:, t, 0:(g + 1) * CTX]
                                ins = V.tensor_scalar(v, v, rsum[:, b, t:t + 1], None, ALU.mult)
                            ins.then_inc(s_pn, 1)
                            dve.wait_ge(s_ahi, item(k))
                            hd, c = i * 2 + (4 * kv + k // ng), slice(g * CTX, (g + 1) * CTX)
                            V.tensor_tensor(bl[:, hd, c], ps[:, 6 + b, 0:SEQ], bh[:, hd, c].bitcast(F32), ALU.subtract)\
                                .then_inc(s_alo, 1)
                        chain.leave(2)

                def seg(v, c):
                    return v.rearrange("p (s t) -> p s t", t=CTX)[:, c // CTX:]

                def taps(name, dst, taps_, c, tile, n0, q0):
                    def evac(i, j):
                        dve.wait_ge(s_eva, i * 2 + (n0 + j + 1))
                        for n, (k, sh) in enumerate(taps_):
                            for f in range(2):
                                o, v = seg(dst(i, j, f), c), seg(PAIR[j][:, f], c)
                                a, b = (slice(-sh, None), slice(0, sh)) if sh < 0 else (slice(0, CTX - sh), slice(sh, CTX))
                                a, b = (slice(-sh, CTX), slice(0, CTX + sh)) if sh < 0 else (a, b)
                                ins = V.scalar_tensor_tensor(o[:, :, a], v[:, :, b], tile(i, j, f, k), o[:, :, a],
                                                             ALU.mult, ALU.add)
                            if n < len(taps_) - 1:
                                link(ins)
                        ins.then_inc(taken[j], 1)
                    return evac

                pairs(l, "lx", taps("lx", lambda i, j, f: xc[:, i * 4 + (2 * j + f)], ((0, -2), (1, -1), (3, 1)), 0,
                                    lambda i, j, f, k: pcol(l, "cw")[:, bass.ds(i * 4 + (KT * k + 2 * j + f), 1)],
                                    before(CENTRES, l, "lx"), first_pair[l, "lx"]), stride=4)

                wait_taken(dve, l, "lx")

                def lru(i, o):
                    j = o // 2
                    n = i * 2 + (BLOCKS * l + j + 1)
                    v = xc[:, i * 2 + j]
                    if o % 2 == 0:
                        dve.wait_ge(s_la2, n)
                        V.scalar_tensor_tensor(l_a2[:], l_a2[:], 1.0, l_th[:], ALU.add, ALU.mult).then_inc(s_lv, 1)
                        link(V.scalar_tensor_tensor(l_ti[:], l_ti[:], 1.0, xc[:, i * 2 + j, None]
                                                    .broadcast_to([P, 2, TOK]), ALU.add, ALU.mult))
                        return
                    dve.wait_ge(s_ls, n)
                    link(V.tensor_tensor(l_ti[:], l_ti[:], l_tr[:], ALU.mult))
                    V.tensor_tensor_scan(l_h[:, 0], l_a[:, 0], l_ti[:, 0], 0.0, ALU.mult, ALU.add)
                    link(V.tensor_tensor_scan(l_h[:, 1, 0:CTX][:, ::-1], l_a[:, 1, 0:CTX][:, ::-1],
                                              l_ti[:, 1, 0:CTX][:, ::-1], 0.0, ALU.mult, ALU.add))
                    link(V.tensor_tensor_scan(l_h[:, 1, CTX:][:, ::-1], l_a[:, 1, CTX:][:, ::-1],
                                              l_ti[:, 1, CTX:][:, ::-1], l_h[:, 1, 0:1], ALU.mult, ALU.add))
                    V.tensor_tensor(v[:, c0:], l_h[:, 0, c0:], l_h[:, 1, c0:], ALU.add).then_inc(s_lh, 1)

                pairs(l, "br1", gate("br1"), stride=9, beside=lru)
                dve.wait_ge(s_lh, 1 + BLOCKS * (l + 1))

                pairs(l, "y", product("y", lambda i, j: xc[:, bass.ds(i * 4 + 2 * j, 2), c0:]))
                pairs(l, "br2", gate("br2"))
                pairs(l, "out", None)
                residual(4 * l + 1, mixed, 1, segs)
                split_h(l, 2 * l + 1, 2, 3, segs)

                n_p = before(PRODUCTS, l, "up")
                up_taps = taps("up", lambda i, j, f: fa[j][:, f], ((0, -1), (2, 1)), c0,
                               lambda i, j, f, k: pcol(l, "fw")[:, bass.ds(i * 4 + (2 * FT * k + 2 * j + f), 1)],
                               before(CENTRES, l, "up"), first_pair[l, "up"])

                def up(i, j):
                    up_taps(i, j)
                    dve.wait_ge(s_fs, i * 2 + (FT * l + j + 1))
                    V.tensor_tensor(fa[j][:, 1, c0:], fs[j][:, 0, c0:], fa[j][:, 1, c0:], ALU.mult).then_inc(s_evp, 1)
                    dve.wait_ge(s_evh, i * 2 + (n_p + j + 1))
                    V.tensor_tensor(fl[:, i * 2 + j, c0:], fa[j][:, 1, c0:], fh[:, i * 2 + j, c0:].bitcast(F32),
                                    ALU.subtract).then_inc(s_b, 1)

                pairs(l, "up", up, stride=2)
                pairs(l, "down", None)
                residual(4 * l + 3, y2, 3, segs)

        @block.tensor
        def _(pe):
            mm = nc.tensor.matmul

            def ada_unit(l, name, i, k):
                n, r0 = len(SIDE[l, name]), side_before(l, name)
                if k == 0:
                    pe.wait_ge(s_ada, i + takes_before(l, name))
                pe.wait_ge(plain_full[k % 2], i * (8 * n) + (8 * r0 + 16 * (k // 2) + 16))
                for f in range(2):
                    for kt in range(UK):
                        ins = mm(ps[:, 4 + f, k // 2 * 2:k // 2 * 2 + 2], wada[k % 2][:, kt, f * P:(f + 1) * P],
                                 csil[:, UK * (k % 2) + kt, :], start=k % 2 == 0 and kt == 0,
                                 stop=k % 2 == 1 and kt == UK - 1)
                ins.then_inc(plain_used, 1)

            def lru_gates(l, i, k):
                pe.wait_ge(plain_full[k], i * 16 + (8 * side_before(l, "br1") + 16))
                for d in range(2):
                    pe.wait_ge(s_ltz, i * 4 + (2 * BLOCKS * l + 2 * k + d + 1))
                    for g in range(2):
                        ins = mm(ps[:, 4 + 2 * d + g], wgate[k][:, 2 * d + g, :], xc[:, i * 2 + k, :],
                                 start=True, stop=True)
                    ins.then_inc(s_lz, 1)

            def project(l, name, moving, feature_major=True):
                m, turns = units_of[name], pairs_of[name] // 2
                b, q2 = first_unit[l, name] // 4, first_pair[l, name] // 2
                with pe.Fori(0, turns) as i:
                    b4 = i * (m // 2) + b
                    for j in range(2):
                        pe.wait_ge(taken[j], i + (q2 + 1))
                        mh_, ml_, c = moving(i, j)
                        for h in range(m):
                            o = m * j + h
                            w_h, w_l = whi[o % 2], wlo[o % 2]
                            nk = DOWN_LAST if name == "down" and h == m - 1 else UK
                            pe.wait_ge(s_hi, b4 * 4 + (o + 1))
                            token_major = not feature_major or (name == "akv" and j == 1)
                            for part, (w, parts) in enumerate(((w_h, (mh_, ml_)), (w_l, (mh_,)))):
                                if part:
                                    pe.wait_ge(s_lo, b4 * 4 + (o + 1))
                                for r in range(4 if token_major else 2):
                                    for x_ in parts:
                                        for k in range(nk):
                                            kk = UK * h + k
                                            first = h == 0 and k == 0 and part == 0 and x_ is mh_
                                            final = h == m - 1 and k == nk - 1 and part == 1
                                            if token_major:
                                                ins = mm(PAIR[j][:, r // 2, 256 * (r % 2):256 * (r % 2 + 1)],
                                                         x_[:, kk, r * P:(r + 1) * P], w[:, k, :],
                                                         start=first and r % 2 == 0, stop=final and r % 2 == 1,
                                                         skip_group_check=True)
                                            else:
                                                c_ = c[r]
                                                ins = mm(PAIR[j][:, r, c_:], w[:, k, r * P:(r + 1) * P], x_[:, kk, c_:],
                                                         start=first, stop=final)
                            ins.then_inc(s_used, 1)
                            side = SIDE.get((l, name), ())
                            if o in side:
                                (lru_gates if name == "br1" else ada_unit)(
                                    *((l, i) if name == "br1" else (l, name, i)), side.index(o))

            def sum_squares(n, c0):
                for j in range(4):
                    pe.wait_ge(s_sq, 4 * n + j + 1)
                    for k in (2 * j, 2 * j + 1):
                        ins = mm(ps[:, 6, c0:], ones[:], sq[:, k, c0:], start=k == 0, stop=k == KT - 1)
                ins.then_inc(s_stat, 1)

            pe.wait_ge(s_ready, READY)
            pe.wait_ge(s_const, CONSTS)
            pe.wait_ge(s_csil, 1)
            for l in range(DEPTH):
                c0, segs = c0_of(l), segs_of(c0_of(l))
                if l == 0:
                    for a in range(ADA_FIRST // 2):
                        pe.wait_ge(ada_full[a // 2], 64)
                        for f in range(2):
                            for k in range(KT):
                                ins = mm(ps[:, 4 + f, 2 * a:2 * a + 2],
                                         ada_first[a // 2][:, a % 2 * 2 + k // UK, k % UK, f * P:(f + 1) * P],
                                         csil[:, k, :], start=k == 0, stop=k == KT - 1)
                        ins.then_inc(plain_used, 1)
                sum_squares(4 * l, 0)
                pe.wait_ge(s_h, KT * (2 * l + 1))
                both = (0, 0)
                project(l, "gqk", lambda i, j: (hh, hl, (c0, 0)))
                project(l, "gv", lambda i, j: (hh, hl, None), feature_major=False)

                pe.wait_ge(s_lrh, l + 1)
                for x_ in (hh, hl):
                    for k in range(KT):
                        mm(ps[:, 7, :], lrh[:, k, :], x_[:, k, :], start=k == 0 and x_ is hh, stop=False)
                pe.wait_ge(s_lrl, l + 1)
                for k in range(KT):
                    ins = mm(ps[:, 7, :], lrl[:, k, :], hh[:, k, :], start=False, stop=k == KT - 1)
                ins.then_inc(s_lrp, 1)
                pe.wait_ge(s_lr, l + 1)

                t_first = c0 // P

                def gla_decays(h):
                    pe.wait_ge(s_wdh, h + (HEADS * l + 1))
                    for d in range(2):
                        ins = mm(ps[:, d], wdh[:, d, :], lr[:], start=True, stop=True)
                    ins.then_inc(s_gz, 1)

                def gla_stat(h):
                    pe.wait_ge(s_osq, h + (HEADS * l + 1))
                    for v in range(2):
                        ins = mm(ps[:, 6, c0:], ones[:], go[:, v, c0:], start=v == 0, stop=v == 1)
                    ins.then_inc(s_ostat, 1)

                def gla_kv(h, d, prev):
                    n = h + HEADS * l
                    for e in range(4):
                        g = 4 * d + e
                        if g == 1 and prev:
                            pe.wait_ge(s_orstd, n)
                        if g >= 2:
                            pe.wait_ge(s_state, n * 8 + (g - 1))
                        for p in range(2 * e, min(2 * e + 2, NCH - 1)):
                            c = CHUNK_ORDER[d][p]
                            r = slice((c % 2) * CHUNK, (c % 2 + 1) * CHUNK)
                            ins = mm(ps[:, KV_BANK[e % 2] + c % 2, 0:DV], keT[r, d, c // 2, :],
                                     vh[r, c // 2, :], start=True, stop=True)
                        ins.then_inc(s_kv, 1)

                def gla_turn(h, prev, nxt):
                    n = h + HEADS * l
                    pe.wait_ge(s_go, n * 3 + 1)
                    for d in range(2):
                        for t in range(TOK // P):
                            ins = nc.tensor.transpose(ps[:, 2 + d, t * P:(t + 1) * P], gl_ke[:, d, t * P:(t + 1) * P],
                                                      ident[:])
                    ins.then_inc(s_keT, 1)
                    pe.wait_ge(s_go, n * 3 + 3)
                    for d in range(2):
                        for t in range(t_first, TOK // P):
                            c = slice(t * P, (t + 1) * P)
                            ins = mm(ps[:, d, c], gl_ki[:, d, c], gl_qd[:, d, c], start=True, stop=True)
                    ins.then_inc(s_att, 1)
                    if prev:
                        gla_stat(h - 1)
                    pe.wait_ge(s_vh, n + 1)
                    pe.wait_ge(s_keTc, n + 1)
                    gla_kv(h, 0, prev)
                    pe.wait_ge(s_attm, n * 2 + 2)
                    if nxt:
                        gla_decays(h + 1)
                    gla_kv(h, 1, prev)
                    pe.wait_ge(s_on, n + 1)
                    for d in range(2):
                        for t in range(t_first, TOK // P):
                            c = slice(t * P, (t + 1) * P)
                            for v in range(2):
                                mm(ps[:, 4 + v, c], vh[:, t, v * P:(v + 1) * P], attm[:, d, c],
                                   start=d == 0 and t == t_first, stop=False, skip_group_check=True)
                    for d in range(2):
                        for p in range(1, NCH):
                            c = CHUNK_ORDER[d][p]
                            if p % 2 or p == NCH - 1:
                                pe.wait_ge(s_state, n * 8 + (4 * d + (p - 1) // 2 + 1))
                            if c * CHUNK < c0:
                                continue
                            cc = slice(c * CHUNK, (c + 1) * CHUNK)
                            for v in range(2):
                                ins = mm(ps[:, 4 + v, cc], state[:, d, p, v * P:(v + 1) * P], gl_qd[:, d, cc],
                                         start=False, stop=d == 1 and p == NCH - 1, skip_group_check=True)
                    ins.then_inc(s_o, 1)

                gla_decays(0)
                gla_turns(pe, None, 0, gla_turn)
                gla_stat(HEADS - 1)

                pe.wait_ge(s_on, 1 + HEADS * (l + 1))
                project(l, "r", lambda i, j: (hh, hl, (c0, c0)))
                lat = (c0, c0)
                pe.wait_ge(s_b, before(PRODUCTS, l, "r") + R_PAIRS)
                project(l, "br0", lambda i, j: ((bh, bl, lat) if j else (hh, hl, lat)))
                project(l, "aq", lambda i, j: (hh, hl, lat))
                project(l, "akv", lambda i, j: (hh, hl, both))

                t0 = (AQ + AKV) * l
                wait_taken(pe, l, "akv")

                def att_sums(i, t, c):
                    for j in range(2):
                        n = i * 2 + (t0 + t + j + 1)
                        pe.wait_ge(s_asq, n)
                        pe.wait_ge(s_aln, n - 2) if t0 + t + j > 1 else None
                        mm(ps[:, 4 + j, c:], ones[:], asq[j][:, 0, c:], start=True, stop=True).then_inc(s_asd, 1)

                def att_swap(i, t):
                    for j in range(2):
                        n = i * 2 + (t0 + t + j + 1)
                        pe.wait_ge(s_anorm, n)
                        pe.wait_ge(s_arope, n - 2) if t0 + t + j > 1 else None
                        mm(ps[:, 4 + j, 0:SEQ], swap[:], aqk[:, i * 2 + (t + j), CTX:], start=True, stop=True)\
                            .then_inc(s_arot, 1)
                with pe.Fori(0, AQ // 2) as i:
                    att_sums(i, 0, c0)
                att_sums(0, AQ, 0)
                with pe.Fori(0, AQ // 2) as i:
                    att_swap(i, 0)
                att_swap(0, AQ)

                n0, ng = att_items(l)
                pe.wait_ge(s_arope, t0 + AQ + AKV)
                for kv in range(AKV):
                    with pe.Fori(0, 2) as i:
                        def item(k):
                            return i * (2 * ng) + (n0 + 4 * ng * kv + k + 1)

                        def scores(k):
                            g, b = segs[k % ng], k % 2
                            if k % ng == 0:
                                pe.wait_ge(s_qc, i * 2 + (AQ * l + 4 * kv + k // ng + 1))
                            for t in range(2):
                                q0 = g * CTX + t * P
                                ins = mm(PAIR[b][:, t, 0:(g + 1) * CTX], qcur[k // ng][:, 0, q0:q0 + P],
                                         aqk[:, AQ + kv, 0:(g + 1) * CTX], start=True, stop=True)
                            ins.then_inc(s_sc, 1)

                        scores(0)
                        for k in range(2 * ng):
                            g, b = segs[k % ng], k % 2
                            if k + 1 < 2 * ng:
                                scores(k + 1)
                            pe.wait_ge(s_pn, item(k))
                            for st in range(2 * g + 2):
                                for t in range(2):
                                    c = (st % 2) * SEQ + t * P
                                    ins = nc.tensor.transpose(ps[:, 4 + st // 2, c:c + P],
                                                              prob[b][:, t, st * P:(st + 1) * P], ident[:])
                            ins.then_inc(s_pt, 1)
                            pe.wait_ge(s_ptc, item(k))
                            pe.wait_ge(s_alo, item(k) + 1 + 1)
                            for st in range(2 * g + 2):
                                ins = mm(ps[:, 6 + b, 0:SEQ], av[:, st, kv * HD:(kv + 1) * HD], probT[b][:, st, :],
                                         start=st == 0, stop=st == 2 * g + 1)
                            ins.then_inc(s_av, 1)

                pe.wait_ge(s_alo, 4 + n0 + AQ * ng)
                project(l, "lx", lambda i, j: (hh, hl, both))

                wait_taken(pe, l, "lx")
                project(l, "br1", lambda i, j: ((bh, bl, lat) if j else (hh, hl, lat)))
                pe.wait_ge(s_ltz, 2 + 16 * (l + 1))
                project(l, "y", lambda i, j: (hh, hl, lat))
                pe.wait_ge(s_b, before(PRODUCTS, l, "y") + 4)
                project(l, "br2", lambda i, j: ((bh, bl, lat) if j else (hh, hl, lat)))
                pe.wait_ge(s_b, before(PRODUCTS, l, "br2") + 4)
                project(l, "out", lambda i, j: (mh, ml, lat))
                sum_squares(4 * l + 1, c0)
                sum_squares(4 * l + 2, c0)
                pe.wait_ge(s_h, KT * (2 * l + 2))
                project(l, "up", lambda i, j: (hh, hl, lat))
                pe.wait_ge(s_b, before(PRODUCTS, l, "up") + FT)
                project(l, "down", lambda i, j: (fh, fl, lat))
                sum_squares(4 * l + 3, c0)



def units(w, order):
    k_tiles = -(-w.shape[0] // (P * UK)) * UK
    if w.shape[0] < P * k_tiles:
        w = np.concatenate([w, np.zeros((P * k_tiles - w.shape[0], w.shape[1]), w.dtype)])
    got = []
    for cols in order:
        v = w[:, cols].reshape(k_tiles // UK, UK, P, UC).transpose(0, 2, 1, 3)
        got.append(v)
    return np.concatenate(got)


def lay_out(inputs):
    g = {k: np.asarray(v) for k, v in inputs.items()}
    pair = lambda base: [np.arange(base + UC * i, base + UC * (i + 1)) for i in range(1000)]
    q0, k0, v0, r0, lr0 = 0, 512, 1024, 2048, 3072
    aq0, ak0, lx0, y0, gate0 = 3104, 4128, 4640, 5664, 6688
    tile = lambda base, t: np.arange(base + P * t, base + P * (t + 1))
    weights, w_ada, w_gate, w_lr = [], [], [], []
    for l in range(DEPTH):
        w_in = g["w_in"][l]

        def branch(n):
            a = units(w_in, pair(gate0 + D_MODEL * n)[:4])
            b = units(g["w_branch"][l, n], pair(0)[:4])
            return np.stack([a.reshape(4, 2, P, UK, UC), b.reshape(4, 2, P, UK, UC)], 1).reshape(16, P, UK, UC)

        weights += [
            units(w_in, [np.concatenate([tile(q0, h), tile(k0, h)]) for h in range(HEADS)]),
            units(w_in, pair(v0)[:4]), units(w_in, pair(r0)[:4]), branch(0),
            units(w_in, pair(aq0)[:4]), units(w_in, pair(ak0)[:2]),
            units(w_in, pair(lx0)[:4]), branch(1), units(w_in, pair(y0)[:4]), branch(2), units(g["w_out"][l], pair(0)[:4]),
            units(g["ffn_w_up"][l], [np.concatenate([tile(0, t), tile(D_FF, t)]) for t in range(FT)]),
            units(g["ffn_w_down"][l], pair(0)[:4]),
        ]
        w_ada.append(units(g["w_ada"][l], pair(0)[:24]))
        w_gate.append(g["lru_w_gates"][l].reshape(4, BLOCKS, P, P).transpose(1, 2, 0, 3))
        w_lr.append(w_in[:, lr0:lr0 + 2 * RANK].reshape(KT, P, 2 * RANK).transpose(1, 0, 2))
    cols = lambda v: v.reshape(-1, P).T
    pieces = lambda v: np.concatenate([cols(r) for r in v], 1)
    params = []
    for l in range(DEPTH):
        fw = g["ffn_conv_w"][l].reshape(3, 2, FT, P).transpose(0, 2, 1, 3).reshape(-1, P).T
        fb = g["ffn_conv_b"][l].reshape(2, FT, P).transpose(1, 0, 2).reshape(-1, P).T
        params.append(np.concatenate([
            cols(g["b_ada"][l]), pieces(g["norm_gains"][l]),
            g["gla_b_decay"][l].reshape(2, HEADS, P).transpose(1, 0, 2).reshape(-1, P).T,
            cols(g["gla_norm_g"][l]),
            np.stack([g["att_q_norm_g"][l]] * AQ + [g["att_k_norm_g"][l]] * AKV, 1),
            pieces(g["lru_conv_w"][l]), cols(g["lru_conv_b"][l]),
            g["lru_b_gates"][l].reshape(2, 2, BLOCKS, P).transpose(2, 0, 1, 3).reshape(-1, P).T,
            g["lru_lambda"][l].reshape(2, BLOCKS, P).transpose(1, 0, 2).reshape(-1, P).T,
            fw, fb], 1))
    stream = np.concatenate([g["ctx"][0], g["x"][0]]).T.reshape(KT, P, TOK).transpose(1, 0, 2)
    cvec = np.stack([g["c_ctx"], g["c"][0]], 1).reshape(KT, P, 2).transpose(1, 0, 2)
    axis_dim = HD // 2
    inv_freq = (1.0 / 10000.0 ** (np.arange(0, axis_dim, 2, dtype=np.float32) / np.float32(axis_dim))).astype(np.float32)
    t = np.arange(SEQ)
    ang = np.concatenate([np.outer(inv_freq, p.astype(np.float32)) for p in (t // GRID_W, t // GRID_W, t % GRID_W,
                                                                            t % GRID_W)])
    rope = np.stack([np.cos(ang), np.sin(ang)], 1).astype(np.float32)
    return {
        "xt": stream, "cvec": cvec, "weights": np.concatenate(weights), "w_ada": np.concatenate(w_ada),
        "w_gate": np.concatenate(w_gate),
        "w_lr": np.stack(w_lr), "w_dec": g["gla_w_decay"], "params": np.stack(params, 1), "rope": rope,
    }


def kernel(**inputs):
    import concourse.bacc as _bacc
    from concourse.bass_utils import run_bass_kernel_spmd as _run

    nc = _bacc.Bacc("TRN2", target_bir_lowering=False, num_devices=1)
    arrays, args = {}, []
    for name, a in lay_out(inputs).items():
        a = np.ascontiguousarray(a)
        arrays[f"in_{name}"] = a
        args.append(nc.dram_tensor(f"in_{name}", a.shape, mybir.dt.from_np(a.dtype), kind="ExternalInput").ap())
    args.append(nc.dram_tensor("out_x", (P, KT, SEQ), F32, kind="ExternalOutput").ap())
    build(nc, *args)
    r = _run(nc, [arrays], core_ids=[0])
    got = np.asarray(r.results[0]["out_x"])
    return np.ascontiguousarray(got.transpose(2, 1, 0)).reshape(1, SEQ, D_MODEL)
```

```python
from contextlib import ExitStack

import numpy as np

import concourse.bass as bass
from concourse import mybir

F32 = mybir.dt.float32
F32R = mybir.dt.float32r
I32 = mybir.dt.int32
ALU = mybir.AluOpType
ACT = mybir.ActivationFunctionType
AX_X = mybir.AxisListType.X

P = 128
D_MODEL, SEQ, CTX, DEPTH, GRID_W = 1024, 256, 256, 2, 64
TOK = CTX + SEQ
KT = D_MODEL // P
EPS = 1e-6
HEADS, DK, DV, RANK, TEMP, CHUNK = 4, 128, 256, 16, 16.0, 64
NCH = TOK // CHUNK
AQ, AKV, HD = 8, 2, 128
BLOCKS = 8
D_FF = 2816
FT = D_FF // P
UK, UC = 4, 256
RAW = 4
ADA_RING = 2

GLA_QK_PAIRS, GLA_V_PAIRS, R_PAIRS = 4, 4, 4
ATT_Q_PAIRS = 4
DOWN_UNITS = -(-FT // UK)
DOWN_LAST = FT - UK * (DOWN_UNITS - 1)
SPLIT_UNITS = 2 * (GLA_QK_PAIRS + GLA_V_PAIRS + R_PAIRS + 8 + ATT_Q_PAIRS + 2 + 8 + 4 + 4 + 8 + 4 + FT) + 4 * DOWN_UNITS
AK, AC = 2, 512
ADA_SUM = KT // AK
ADA_UNITS = 6 * D_MODEL // AC * ADA_SUM
ADA_FIRST = 16
ADA_STAGES = [(0, "r"), (0, "br0"), (0, "aq"), (0, "lx"), (0, "y"), (0, "br2"), (0, "out"), (0, "down")]

PCOLS = {}
_at = 0
for _n, _w in (("b_ada", 48), ("gains", 32), ("b_dec", 8), ("g_gla", 8), ("g_qk", 10), ("cw", 32), ("cb", 8),
               ("b_gate", 32), ("lam", 16), ("fw", 3 * 2 * FT), ("fb", 2 * FT)):
    PCOLS[_n] = (_at, _at + _w)
    _at += _w
NPAR = _at

CONSTS, READY = 20, 3


class Chain:

    def __init__(self, eng, sem):
        self.eng, self.sem, self.base, self.k, self.i, self.stride = eng, sem, 0, 0, None, 0

    def link(self, ins):
        ins.then_inc(self.sem, 1)
        self.k += 1
        at = self.base + self.k
        self.eng.wait_ge(self.sem, at if self.i is None else self.i * self.stride + at)

    def enter(self, i, stride):
        self.base, self.k, self.i, self.stride = self.base + self.k, 0, i, stride

    def leave(self, times):
        assert self.k == self.stride, (self.k, self.stride)
        self.base, self.k, self.i = self.base + times * self.stride, 0, None


def build(nc, xt, cvec, weights, w_ada, w_gate, w_lr, w_dec, params, rope, out):
    with ExitStack() as ctx:
        def sb(name, shape, dt=F32):
            return ctx.enter_context(nc.sbuf_tensor(name, shape, dt))

        def sem(name):
            return ctx.enter_context(nc.semaphore(name))

        ident = sb("ident", [P, P])
        ones = sb("ones", [P, P])
        swap = sb("swap", [P, P])
        cs = sb("cs", [P, 2, SEQ])
        scanmask = sb("scanmask", [P, NCH, CHUNK])
        keep = sb("keep", [P, 2, P])
        par = sb("par", [P, DEPTH, NPAR])
        cin = sb("cin", [P, KT, 2])
        csil = sb("csil", [P, KT, 2])
        mod = sb("mod", [P, DEPTH, 6 * KT, 2])
        gmod = sb("gmod", [P, 4, KT, 2])
        hbias = sb("hbias", [P, 32])
        sp = sb("sp", [P, 3, 16])
        wdec = sb("wdec", [2 * RANK, 2, HEADS * DK])
        wdh = sb("wdh", [2 * RANK, 2, DK])
        rstd = sb("rstd", [P, TOK])
        g_end = sb("g_end", [P, 2, NCH])
        one, eps = sb("one", [P, 1]), sb("eps", [P, 1])
        mx = sb("mx", [P, 4, 2])
        nb = sb("nb", [P, 4, 2])
        sums = sb("sums", [P, 4, 2])
        rsum = sb("rsum", [P, 4, 2])

        SLOT = 4 * TOK
        base = -(-nc.sbuf_base // 64) * 64
        slots = (nc.sbuf_usable_end - base) // SLOT
        ctx.enter_context(nc.sbuf_tensor("arena", [P, slots * TOK], F32, align_bytes=64))

        def at(name, slot, shape, dt=F32, extra=0):
            size = 4 * int(np.prod(shape[1:]))
            assert slot * SLOT + extra + size <= slots * SLOT, (name, slot, size, slots)
            return nc.alloc_sbuf_tensor_at(name, shape, dt, offset=base + slot * SLOT + extra)

        def tiles(name, slot, n, dt=F32):
            return at(name, slot, [P, n, TOK], dt)

        X, H, WR, WS, PL = 0, 8, 24, 32, 40
        M = 44
        B = M + 8
        A = B + 16
        T = A + 16
        x = tiles("x", X, KT)
        hh, hl = tiles("hh", H, KT, F32R), tiles("hl", H + KT, KT, F32R)
        wraw = [at(f"wraw{i}", WR + 2 * i, [P, UK, UC]) for i in range(RAW)]
        whi = [at(f"whi{i}", WS + 2 * i, [P, UK, UC], F32R) for i in range(2)]
        wlo = [at(f"wlo{i}", WS + 4 + 2 * i, [P, UK, UC], F32R) for i in range(2)]
        wada = [at(f"wada{i}", PL + 2 * i, [P, AK, AC]) for i in range(ADA_RING)]
        mixed = tiles("mixed", M, KT)
        bh, bl = tiles("bh", B, KT, F32R), tiles("bl", B + KT, KT, F32R)
        ada_first = [at(f"ada_first{i}", s_, [P, ADA_SUM, AK, AC]) for i, s_ in enumerate((M, A, A + 8, T))]
        ada_sum = at("ada_sum", T + 8, [P, 2, AC])
        wgate = [at(f"wgate{i}", T + 8 + i, [P, 4, P]) for i in range(2)]
        ada_sum_first = at("ada_sum_first", B + 8, [P, 2, AC])
        sq, nt = tiles("sq", B, KT), tiles("nt", B + KT, KT)
        gqk = at("gqk", A, [P, HEADS, 2, TOK])
        gv = at("gv", A + 8, [P, TOK // P, HEADS * DV])
        go = at("go", T + 0, [P, 2, TOK])
        gl_l = tiles("gl_l", B, 2)
        gl_m = tiles("gl_m", B + 2, 2)
        gl_c = tiles("gl_c", B + 4, 2)
        gl_ep = tiles("gl_ep", B + 6, 2)
        gl_ki = tiles("gl_ki", B + 8, 2)
        gl_ke = tiles("gl_ke", B + 10, 2)
        gl_qd = tiles("gl_qd", B + 12, 2)
        lr = at("lr", B + 14, [2 * RANK, TOK])
        state = at("state", M, [P, 2, NCH, DV])
        attm = tiles("attm", T + 2, 2)
        vh = at("vh", T + 4, [P, TOK // P, DV])
        keT = at("keT", T + 6, [P, 2, TOK // P, P])
        gstat = tiles("gstat", T + 8, 1)
        lrw = at("lrw", B, [P, KT, 2 * RANK])
        lrh = at("lrh", B + 2, [P, KT, P], F32R)
        lrl = at("lrl", B + 4, [P, KT, P], F32R)
        ev = [tiles(f"ev{i}", T + 4 * i, 2) for i in range(2)]
        evp = [tiles(f"evp{i}", T + 2 + 4 * i, 2) for i in range(2)]
        aqk = tiles("aqk", A, AQ + AKV)
        av = at("av", A + AQ + AKV, [P, TOK // P, AKV * HD])
        astat = tiles("astat", B, AQ + AKV)
        asq = [tiles(f"asq{i}", T + i, 1) for i in range(2)]
        arot = [at(f"arot{i}", T + 2 + i, [P, 2, SEQ]) for i in range(2)]
        qcur = [tiles(f"qcur{i}", A + 12 + i, 1) for i in range(2)]
        prob = [tiles(f"prob{i}", T + 2 * i, 2) for i in range(2)]
        probT = [at(f"probT{i}", T + 4 + 2 * i, [P, TOK // P, SEQ]) for i in range(2)]
        xc = tiles("xc", A, BLOCKS)
        l_tr, l_ti, l_a, l_th = (tiles(n, A + 8 + 2 * i, 2) for i, n in enumerate(("l_tr", "l_ti", "l_a", "l_th")))
        l_a2 = tiles("l_a2", T + 4, 2)
        l_h = tiles("l_h", T + 6, 2)
        mh, ml = tiles("mh", A, KT, F32R), tiles("ml", A + KT, KT, F32R)
        fh, fl = tiles("fh", M, FT, F32R), tiles("fl", M + FT, FT, F32R)
        fa = [tiles(f"fa{i}", M + 2 * FT + 3 * i, 2) for i in range(2)]
        fs = [tiles(f"fs{i}", M + 2 * FT + 2 + 3 * i, 1) for i in range(2)]
        y2 = tiles("y2", H, KT)

        ps = ctx.enter_context(nc.psum_tensor("ps", [P, 8, 512], F32))
        PAIR = [ps[:, 0:2], ps[:, 2:4]]
        KEEP = keep[:].bitcast(I32)
        MOD = [mod[:, l] for l in range(DEPTH)]

        s_in, s_par = sem("x_loaded"), sem("params_loaded")
        s_const, s_ready = sem("pool_consts_made"), sem("vector_consts_made")
        raw_full = [sem(f"raw_full{i}") for i in range(RAW)]
        wada_full = [sem(f"wada_full{i}") for i in range(ADA_RING)]
        s_hi, s_lo, s_used = sem("w_hi_made"), sem("w_lo_made"), sem("w_unit_used")
        gate_full = [sem(f"gate_weights{i}_full") for i in range(2)]
        ada_full = [sem(f"ada_first_full{i}") for i in range(4)]
        wada_used = sem("ada_unit_used")
        s_asum = sem("first_ada_sums_made")
        s_red, s_ada = sem("ada_columns_done"), sem("ada_columns_taken")
        taken = [sem("pair0_taken"), sem("pair1_taken")]
        s_csil, s_mod = sem("cond_silu_made"), sem("mod_made")
        s_sq, s_stat, s_rstd = sem("squares_made"), sem("stat_done"), sem("rstd_made")
        s_nt, s_hhi, s_h = sem("scaled_made"), sem("h_hi_made"), sem("h_made")
        s_x = sem("x_updated")
        s_sp, s_c4 = sem("softplus_parts_made"), sem("softplus_made")
        s_lrw, s_wdec = sem("lr_weights_loaded"), sem("decay_weights_loaded")
        s_lrz, s_lrh, s_lrl = sem("lr_pad_zeroed"), sem("lr_hi_made"), sem("lr_lo_made")
        s_lrp, s_lr = sem("lr_done"), sem("lr_copied")
        s_wdz = sem("decay_weights_zeroed")
        s_wdh, s_vh, s_gz, s_ga, s_gl = sem("head_decay_weights_copied"), sem("head_values_copied"), sem("decay_logits_done"), sem("abs_made"), sem("ln_made")
        s_gc, s_ge, s_go = sem("cum_made"), sem("decay_exps_made"), sem("decayed_qk_made")
        s_keT, s_keTc, s_att, s_attm = sem("keT_done"), sem("keT_copied"), sem("gla_att_done"), sem("gla_att_masked")
        s_kv, s_state, s_o = sem("kv_done"), sem("states_made"), sem("gla_o_done")
        s_osq, s_ostat, s_orstd, s_on = sem("o_squares"), sem("o_stat"), sem("o_rstd"), sem("o_normed")
        s_eva, s_evp, s_evh, s_b = sem("evac_act"), sem("evac_product"), sem("evac_hi"), sem("split_pairs_made")
        s_asq, s_asd, s_aln = sem("att_squares"), sem("att_stat_done"), sem("att_ln_made")
        s_arstd, s_anorm, s_arot, s_arope = sem("att_rstd"), sem("att_normed"), sem("att_swapped"), sem("att_roped")
        s_qc, s_sc, s_nb, s_ex = sem("q_copied"), sem("scores_done"), sem("neg_max_made"), sem("probs_exped")
        s_pn, s_pt, s_ptc, s_av = sem("probs_normed"), sem("probs_transposed"), sem("probsT_copied"), sem("att_out_done")
        s_ahi, s_alo = sem("att_hi"), sem("att_lo")
        s_lz, s_ltz, s_lt, s_la2 = sem("lru_logits_done"), sem("lru_logits_taken"), sem("lru_exps_made"), sem("lru_squares")
        s_lv, s_ls, s_lh = sem("lru_v_made"), sem("lru_sqrt_made"), sem("lru_h_made")
        s_fs = sem("ffn_silu")
        s_c_act, s_c_dve = sem("act_chain"), sem("dve_chain")
        s_out = sem("out_stored")

        block = ctx.enter_context(nc.Block())

        def pcol(l, name):
            a, b = PCOLS[name]
            return par[:, l, a:b]

        def c0_of(l):
            return 0 if l < DEPTH - 1 else CTX

        def segs_of(c0):
            return [s for s in range(2) if (s + 1) * CTX > c0]

        stages = [("gqk", 4, 2), ("gv", 4, 2), ("r", 4, 2), ("br0", 8, 2), ("aq", 4, 2), ("akv", 2, 2), ("lx", 4, 2),
                  ("br1", 8, 2), ("y", 4, 2), ("br2", 8, 2), ("out", 4, 2), ("up", FT, 2), ("down", 4, DOWN_UNITS)]
        pairs_of = {n: c for n, c, _ in stages}
        units_of = {n: m for n, _, m in stages}
        order = [(l, n) for l in range(DEPTH) for n, _, _ in stages]
        first_unit, first_pair = {}, {}
        u = q = 0
        for l, name in order:
            first_unit[l, name], first_pair[l, name] = u, q
            u, q = u + pairs_of[name] * units_of[name], q + pairs_of[name]
        assert u == DEPTH * SPLIT_UNITS and all(v % 4 == 0 for v in first_unit.values())

        def ada_before(l, name):
            return sum(ADA_SUM * pairs_of[n] // 2 for k, n in order[:order.index((l, name))] if (k, n) in ADA_STAGES)

        def takes_before(l, name):
            return 1 + sum(pairs_of[n] // 2 for k, n in order[:order.index((l, name))] if (k, n) in ADA_STAGES)

        ADA_TAKES = takes_before(1, "gqk")

        def gla_turns(eng, chain, stride, turn):
            turn(0, False, True)
            with eng.Fori(0, HEADS - 2) as i:
                if chain:
                    chain.enter(i, stride)
                turn(i + 1, True, True)
                if chain:
                    chain.leave(HEADS - 2)
            turn(HEADS - 1, True, False)

        def att_turns(eng, chain, stride, turn):
            with eng.Fori(0, AQ // 2 - 1) as i:
                if chain:
                    chain.enter(i, stride)
                turn(i, False)
                if chain:
                    chain.leave(AQ // 2 - 1)
            turn(AQ // 2 - 1, True)

        def att_item(i, k, n0, ng):
            return i * (2 * ng) + (n0 + k + 1), i + (k // (2 * ng) + AQ // AKV * (k // ng % 2)), k // ng % 2

        def ds(first, n):
            return slice(first, first + n) if isinstance(first, int) else bass.ds(first, n)

        def before(group, l, name):
            n = order.index((l, name))
            return sum(pairs_of[s] // (2 if s[:2] == "br" else 1) for _, s in order[:n] if s in group)

        PRODUCTS = ("r", "y", "br2", "up")
        CENTRES = ("lx", "up")

        def wait_taken(eng, l, name):
            n = (first_pair[l, name] + pairs_of[name]) // 2
            for j in range(2):
                eng.wait_ge(taken[j], n + 1)

        CHUNK_ORDER = [list(range(NCH)), [3, 2, 1, 0, 7, 6, 5, 4]]
        KV_BANK = (2, 6)
        HSCALE = HD ** -0.5

        def att_items(l):
            return 16 * l, len(segs_of(c0_of(l)))

        @block.sync
        def _(sp_):
            def load_ada(i, r):
                sp_.wait_ge(wada_used, i * ADA_SUM + (ADA_FIRST // 2 + r - 1))
                sp_.dma_start(wada[r % 2][:], w_ada[i * ADA_SUM + (ADA_FIRST + r)]).then_inc(wada_full[r % 2], 16)

            def load_stage(l, name):
                n, last = 2 * units_of[name], (l, name) == order[-1]
                last_ada = (l, name) == ADA_STAGES[-1]
                turns, u0, a0 = pairs_of[name] // 2, first_unit[l, name], ada_before(l, name)
                if name == "br1":
                    sp_.wait_ge(s_on, 1 + HEADS * (l + 1))
                    sp_.wait_ge(s_ada, takes_before(l, name))

                def turn(i, final):
                    for o in range(n):
                        s = o % RAW
                        if not (final and last and o >= n - RAW):
                            sp_.wait_ge(s_lo, i * n + (u0 + o + 1))
                            sp_.dma_start(wraw[s][:], weights[i * n + (u0 + RAW + o)]).then_inc(raw_full[s], 16)
                        if name == "br1" and o % 2 == 0:
                            k = o // 2
                            sp_.wait_ge(s_lz, i * 4 + (2 * BLOCKS * l + 2 * k + 2))
                            sp_.dma_start(wgate[k][:], w_gate[i * 2 + (BLOCKS * l + k)]).then_inc(gate_full[k], 16)
                        if (l, name) in ADA_STAGES:
                            for u in {1: (2,), 2: (3,), 3: () if final else (4, 5)}.get(o, ()):
                                load_ada(i, a0 + u)

                peel = last or last_ada
                with sp_.Fori(0, turns - peel) as i:
                    turn(i, False)
                if peel:
                    turn(turns - 1, True)

            sp_.dma_start(x[:], xt).then_inc(s_in, 16)
            for u in range(0, ADA_FIRST, 2):
                sp_.dma_start(ada_first[u // 4][:, u % 4], w_ada[u]).then_inc(ada_full[u // 4], 16)
            for s in range(RAW):
                sp_.dma_start(wraw[s][:], weights[s]).then_inc(raw_full[s], 16)
            for r in range(2):
                sp_.dma_start(wada[r][:], w_ada[ADA_FIRST + r]).then_inc(wada_full[r], 16)
            for l, name in order:
                load_stage(l, name)
            sp_.wait_ge(s_x, KT * 2 * DEPTH)
            sp_.dma_start(out, x[:, :, CTX:TOK]).then_inc(s_out, 16)
            sp_.wait_ge(s_out, 16)

        @block.gpsimd
        def _(pool):
            pool.dma_start(par[:], params).then_inc(s_par, 16)
            pool.dma_start(cin[:], cvec).then_inc(s_par, 16)
            pool.dma_start(cs[:], rope).then_inc(s_par, 16)
            nc.gpsimd.memset(ident[:], 0.0).then_inc(s_const, 1)
            nc.gpsimd.memset(swap[:], 0.0).then_inc(s_const, 1)
            nc.gpsimd.memset(keep[:], 1.0).then_inc(s_const, 1)
            made = 3

            def select(v, op, fill, base, pattern, mult):
                nonlocal made
                pool.wait_ge(s_const, made)
                nc.gpsimd.affine_select(out=v, in_=v, compare_op=op, fill=fill, base=base, pattern=pattern,
                                        channel_multiplier=mult).then_inc(s_const, 1)
                made += 1

            select(ident[:], ALU.not_equal, 1.0, 0, [[-1, P]], 1)
            for off, fill in ((32, -1.0), (-32, 1.0)):
                for axis in range(2):
                    m0 = 64 * axis + (0 if off > 0 else 32)
                    select(swap[:, m0:m0 + 32], ALU.not_equal, fill, -(m0 + off), [[-1, 32]], 1)
            for d, sign in enumerate((1, -1)):
                for c in range(P // CHUNK):
                    v = keep[:, d, c * CHUNK:(c + 1) * CHUNK]
                    select(v, ALU.is_ge, 0.0, -c * CHUNK, [[0, CHUNK]], 1)
                    select(v, ALU.is_ge, 0.0, (c + 1) * CHUNK - 1, [[0, CHUNK]], -1)
                    select(v, ALU.is_ge, 0.0, sign * c * CHUNK, [[sign, CHUNK]], -sign)
            assert made == CONSTS
            for l in range(DEPTH):
                if l:
                    pool.wait_ge(s_wdh, HEADS * l)
                nc.gpsimd.memset(wdec[:], 0.0).then_inc(s_wdz, 1)
                pool.wait_ge(s_wdz, l + 1)
                for d in range(2):
                    pool.dma_start(wdec[d * RANK:(d + 1) * RANK, d, :], w_dec[l, d]).then_inc(s_wdec, 16)
                pool.wait_ge(s_hhi, KT * (2 * l + 1))
                pool.dma_start(lrw[:], w_lr[l]).then_inc(s_lrw, 16)
                pool.wait_ge(s_wdec, 32 * (l + 1))
                if l:
                    pool.wait_ge(s_gz, HEADS * l)
                nc.gpsimd.tensor_copy(wdh[:], wdec[:, :, 0:DK]).then_inc(s_wdh, 1)
                wait_taken(pool, l, "gv")
                nc.gpsimd.tensor_copy(vh[:], gv[:, :, 0:DV]).then_inc(s_vh, 1)
                with pool.Fori(0, HEADS - 1) as i:
                    pool.wait_ge(s_gz, i + (HEADS * l + 1))
                    nc.gpsimd.tensor_copy(wdh[:], wdec[:, :, bass.ds(i * DK + DK, DK)]).then_inc(s_wdh, 1)
                    pool.wait_ge(s_o, i + (HEADS * l + 1))
                    nc.gpsimd.tensor_copy(vh[:], gv[:, :, bass.ds(i * DV + DV, DV)]).then_inc(s_vh, 1)
                pool.wait_ge(s_arope, (l + 1) * (AQ + AKV))
                n0, ng = att_items(l)
                c0 = c0_of(l)
                for j in range(2):
                    nc.gpsimd.tensor_copy(qcur[j][:, 0, c0:], aqk[:, AQ // AKV * j, c0:]).then_inc(s_qc, 1)
                with pool.Fori(0, AQ // 2 - 1) as i:
                    for j in range(2):
                        pool.wait_ge(s_sc, i * (2 * ng) + (n0 + ng * (j + 1)))
                        nc.gpsimd.tensor_copy(qcur[j][:, 0, c0:], aqk[:, i + (1 + AQ // AKV * j), c0:]).then_inc(s_qc, 1)
                with pool.Fori(0, BLOCKS) as i:
                    pool.wait_ge(s_lt, i + (BLOCKS * l + 1))
                    nc.gpsimd.tensor_tensor(l_a2[:], l_a[:], l_a[:], ALU.mult).then_inc(s_la2, 1)

        @block.scalar
        def _(act):
            chain = Chain(act, s_c_act)
            link = chain.link
            A_ = nc.scalar.activation

            def hi(b4, off):
                act.wait_ge(raw_full[off % RAW], b4 * 16 + (16 * (off // RAW) + 16))
                act.wait_ge(s_used, b4 * 4 + (off - 1))
                A_(whi[off % 2][:], wraw[off % RAW][:], ACT.Copy).then_inc(s_hi, 1)

            def pairs(l, name, evac, beside=None):
                m, last = units_of[name], (l, name) == order[-1]
                b, turns = first_unit[l, name] // 4, pairs_of[name] // 2

                def turn(i, b4, final):
                    for j in range(2):
                        for o in range(2 + m * j, m * (j + 1) + 2):
                            if not (final and o >= 2 * m):
                                hi(b4, o)
                            if beside:
                                beside(i, o - 2)
                        act.wait_ge(s_used, b4 * 4 + m * (j + 1))
                        evac(i, j)

                with act.Fori(0, turns - last) as i:
                    turn(i, i * (m // 2) + b, False)
                if last:
                    turn(turns - 1, b + (turns - 1) * (m // 2), True)

            def norm_stats(n, src, ready, c0):
                for j in range(4):
                    ready(2 * j + 2)
                    A_(sq[:, 2 * j:2 * j + 2, c0:], src[:, 2 * j:2 * j + 2, c0:], ACT.Square).then_inc(s_sq, 1)
                act.wait_ge(s_stat, n + 1)
                link(A_(rstd[:, c0:], ps[:, 6, c0:], ACT.Ln, scale=1.0 / D_MODEL, bias=eps[:]))
                A_(rstd[:, c0:], rstd[:, c0:], ACT.Exp, scale=-0.5).then_inc(s_rstd, 1)

            def make_h(l, n, shift, segs):
                for k in range(KT):
                    act.wait_ge(s_nt, KT * n + k + 1)
                    for s in segs:
                        c = slice(s * CTX, (s + 1) * CTX)
                        ins = A_(hh[:, k, c], nt[:, k, c], ACT.Identity, bias=MOD[l][:, 8 * shift + k, s:s + 1])
                    ins.then_inc(s_hhi, 1)

            for u in range(1, ADA_FIRST, 2):
                act.dma_start(ada_first[u // 4][:, u % 4], w_ada[u]).then_inc(ada_full[u // 4], 16)
            act.wait_ge(s_par, 48)
            act.wait_ge(s_ready, READY)
            A_(csil[:], cin[:], ACT.Silu).then_inc(s_csil, 1)
            act.wait_ge(s_in, 16)
            for l in range(DEPTH):
                c0, segs = c0_of(l), segs_of(c0_of(l))
                if l:
                    act.wait_ge(s_lh, BLOCKS * l + 1)
                link(A_(sp[:, 0], pcol(l, "lam"), ACT.Abs))
                link(A_(sp[:, 0], sp[:, 0], ACT.Exp, scale=-1.0))
                link(A_(sp[:, 0], sp[:, 0], ACT.Ln, bias=one[:]))
                A_(sp[:, 1], pcol(l, "lam"), ACT.Relu, scale=-1.0).then_inc(s_sp, 1)
                norm_stats(4 * l, x, (lambda k: act.wait_ge(s_x, KT * (2 * l - 1) + k)) if l else (lambda k: None), 0)
                act.wait_ge(s_mod, l + 1)
                make_h(l, 2 * l, 0, (0, 1))
                if l == 0:
                    for s in range(2):
                        act.wait_ge(raw_full[s], 16)
                        A_(whi[s][:], wraw[s][:], ACT.Copy).then_inc(s_hi, 1)

                def copy_gqk(i, j):
                    A_(gqk[:, i * 2 + j, 0, c0:], PAIR[j][:, 0, c0:], ACT.Copy)
                    A_(gqk[:, i * 2 + j, 1, :], PAIR[j][:, 1, :], ACT.Copy).then_inc(taken[j], 1)

                def copy_gv(i, j):
                    A_(gv[:, :, bass.ds(i * 512 + 256 * j, 256)], PAIR[j].rearrange("p a (b c) -> p (a b) c", c=256),
                       ACT.Copy).then_inc(taken[j], 1)

                pairs(l, "gqk", copy_gqk)
                act.wait_ge(s_lrw, 16 * (l + 1))
                act.wait_ge(s_lrz, 2 * (l + 1))
                A_(lrh[:, :, 0:2 * RANK], lrw[:], ACT.Copy).then_inc(s_lrh, 1)
                pairs(l, "gv", copy_gv)

                act.wait_ge(s_lrp, l + 1)
                A_(lr[:], ps[0:2 * RANK, 7, :], ACT.Copy).then_inc(s_lr, 1)

                def gla_prepare(h):
                    n = h + HEADS * l
                    act.wait_ge(s_gz, n + 1)
                    for d in range(2):
                        ins = A_(gl_l[:, d], ps[:, d], ACT.Abs, bias=pcol(l, "b_dec")[:, ds(h * 2 + d, 1)])
                    ins.then_inc(s_ga, 1)
                    act.wait_ge(s_ga, n + 1)
                    link(A_(gl_l[:], gl_l[:], ACT.Exp, scale=-1.0))
                    A_(gl_l[:], gl_l[:], ACT.Ln, bias=one[:]).then_inc(s_gl, 1)
                    act.wait_ge(s_gc, n + 1)
                    A_(gl_ke[:], gl_ke[:], ACT.Exp, scale=1.0 / TEMP).then_inc(s_ge, 1)
                    A_(gl_ki[:], gl_c[:], ACT.Exp, scale=-1.0 / TEMP).then_inc(s_ge, 1)
                    A_(gl_ep[:], gl_c[:], ACT.Exp, scale=1.0 / TEMP).then_inc(s_ge, 1)

                def gla_squares(h):
                    act.wait_ge(s_o, h + (HEADS * l + 1))
                    A_(go[:, :, c0:], ps[:, 4:6, c0:], ACT.Square).then_inc(s_osq, 1)

                def gla_rstd(h):
                    act.wait_ge(s_ostat, h + (HEADS * l + 1))
                    act.wait_ge(s_on, h + (HEADS * l + 1))
                    link(A_(gstat[:, 0, c0:], ps[:, 6, c0:], ACT.Ln, scale=1.0 / DV, bias=eps[:]))
                    A_(gstat[:, 0, c0:], gstat[:, 0, c0:], ACT.Exp, scale=-0.5).then_inc(s_orstd, 1)

                def gla_turn(h, prev, nxt):
                    if prev:
                        gla_squares(h - 1)
                    act.wait_ge(s_keT, h + (HEADS * l + 1))
                    A_(keT[:].rearrange("p d t k -> p d (t k)"), ps[:, 2:4], ACT.Copy).then_inc(s_keTc, 1)
                    if prev:
                        gla_rstd(h - 1)
                    if nxt:
                        gla_prepare(h + 1)

                gla_prepare(0)
                gla_turns(act, chain, 2, gla_turn)
                gla_squares(HEADS - 1)
                gla_rstd(HEADS - 1)

                def product(name, func):
                    n0 = before(PRODUCTS, l, name)

                    def evac(i, j):
                        act.wait_ge(s_evp, i * 2 + (n0 + j - 1)) if n0 + j - 1 > 0 else None
                        A_(ev[j][:, :, c0:], PAIR[j][:, :, c0:], func).then_inc(taken[j], 1)
                        act.wait_ge(s_evp, i * 2 + (n0 + j + 1))
                        A_(bh[:, bass.ds(i * 4 + 2 * j, 2), c0:], evp[j][:, :, c0:], ACT.Copy).then_inc(s_evh, 1)
                    return evac

                def gate(name):
                    def evac(i, j):
                        if j == 0:
                            act.wait_ge(taken[1], i + (first_pair[l, name] // 2 + 1))
                            A_(ev[0][:, :, c0:], PAIR[0][:, :, c0:], ACT.Tanh, scale=0.5).then_inc(taken[0], 1)
                        elif name == "br2":
                            act.wait_ge(s_evp, i + (before(PRODUCTS, l, name) + 1))
                            A_(mh[:, bass.ds(i * 2, 2), c0:], mixed[:, bass.ds(i * 2, 2), c0:], ACT.Copy, scale=0.5)\
                                .then_inc(s_evh, 1)
                    return evac

                pairs(l, "r", product("r", ACT.Silu))
                pairs(l, "br0", gate("br0"))

                def copy_aq(i, j):
                    A_(aqk[:, bass.ds(i * 4 + 2 * j, 2), c0:], PAIR[j][:, :, c0:], ACT.Copy).then_inc(taken[j], 1)

                def copy_akv(i, j):
                    if j == 0:
                        A_(aqk[:, AQ:], PAIR[0], ACT.Copy).then_inc(taken[0], 1)
                    else:
                        A_(av[:], PAIR[1].rearrange("p a (b c) -> p (a b) c", c=256), ACT.Copy).then_inc(taken[1], 1)

                pairs(l, "aq", copy_aq)
                pairs(l, "akv", copy_akv)

                wait_taken(act, l, "akv")
                t0 = (AQ + AKV) * l

                def att_squares(i, t, c):
                    for j in range(2):
                        act.wait_ge(s_asd, i * 2 + (t0 + t + j + 1))
                        A_(asq[j][:, 0, c:], aqk[:, i * 2 + (t + j), c:], ACT.Square).then_inc(s_asq, 1)
                with act.Fori(0, AQ // 2) as i:
                    att_squares(i, 0, c0)
                att_squares(0, AQ, 0)
                act.wait_ge(s_asd, 2 + t0 + AQ)
                A_(astat[:, 0:AQ, c0:], ps[:, :, c0:], ACT.Ln, scale=1.0 / HD, bias=eps[:]).then_inc(s_aln, 1)
                act.wait_ge(s_asd, 2 + t0 + AQ + AKV)
                A_(astat[:, AQ:], PAIR[0], ACT.Ln, scale=1.0 / HD, bias=eps[:]).then_inc(s_aln, 1)
                act.wait_ge(s_aln, 2 * l + 2)
                for v in (astat[:, 0:AQ // 2, c0:], astat[:, AQ // 2:AQ, c0:], astat[:, AQ:]):
                    A_(v, v, ACT.Exp, scale=-0.5).then_inc(s_arstd, 1)

                n0, ng = att_items(l)

                def exps(i, k):
                    g, b, (n, _, _) = segs[k % ng], k % 2, att_item(i, k, n0, ng)
                    act.wait_ge(s_nb, n)
                    for t in range(2):
                        ins = A_(prob[b][:, t, 0:(g + 1) * CTX], PAIR[b][:, t, 0:(g + 1) * CTX], ACT.Exp,
                                 scale=HSCALE, bias=nb[:, b, t:t + 1], accum_out=sums[:, b, t:t + 1])
                    ins.then_inc(s_ex, 1)

                def att_turn(i, last):
                    for k in range(2 * ng):
                        g, b, (n, head, _) = segs[k % ng], k % 2, att_item(i, k, n0, ng)
                        act.wait_ge(s_pt, n)
                        A_(probT[b][:, 0:2 * g + 2], ps[:, 4:6].rearrange("p a (b c) -> p (a b) c", c=SEQ)[:, 0:2 * g + 2],
                           ACT.Copy).then_inc(s_ptc, 1)
                        if not (last and k + 2 >= 2 * ng):
                            exps(i, k + 2)
                        act.wait_ge(s_av, n)
                        A_(bh[:, head, g * CTX:(g + 1) * CTX], ps[:, 6 + b, 0:SEQ], ACT.Copy).then_inc(s_ahi, 1)

                exps(0, 0)
                exps(0, 1)
                att_turns(act, None, 0, att_turn)

                def centre(name, dst, w, bias, c, tile):
                    def evac(i, j):
                        for f in range(2):
                            ins = A_(dst(i, j, f)[:, c:], PAIR[j][:, f, c:], ACT.Identity,
                                     scale=pcol(l, w)[:, bass.ds(tile(i, j, f), 1)],
                                     bias=pcol(l, bias)[:, bass.ds(tile(i, j, f), 1)] if w != "cw" else
                                     pcol(l, bias)[:, bass.ds(i * 4 + (2 * j + f), 1)])
                        ins.then_inc(s_eva, 1)
                    return evac

                pairs(l, "lx", centre("lx", lambda i, j, f: xc[:, i * 4 + (2 * j + f)], "cw", "cb", 0,
                                      lambda i, j, f: i * 4 + (2 * KT + 2 * j + f)))

                act.wait_ge(s_c4, l + 1)

                def lru(i, o):
                    j = o // 2
                    if o % 2:
                        act.wait_ge(s_lv, i * 2 + (BLOCKS * l + j + 1))
                        A_(l_tr[:], l_a2[:], ACT.Sqrt, scale=-0.25).then_inc(s_ls, 1)
                        return
                    act.wait_ge(s_lh, i * 2 + (BLOCKS * l + j + 1))
                    for d in range(2):
                        act.wait_ge(s_lz, i * 4 + (2 * BLOCKS * l + 2 * j + d + 5))
                        for g, buf in enumerate((l_tr, l_ti)):
                            ins = A_(buf[:, d], ps[:, 4 + 2 * d + g], ACT.Tanh, scale=0.5,
                                     bias=hbias[:, bass.ds(i * 8 + (4 * j + 2 * d + g), 1)])
                        ins.then_inc(s_ltz, 1)
                    act.wait_ge(s_ltz, i * 4 + (2 * BLOCKS * l + 2 * j + 4))
                    for d in range(2):
                        k4 = sp[:, 2, bass.ds(i * 4 + (2 * j + d), 1)]
                        A_(l_a[:, d], l_tr[:, d], ACT.Exp, scale=k4, bias=k4)
                        ins = A_(l_th[:, d], l_tr[:, d], ACT.Tanh, scale=k4, bias=k4)
                    ins.then_inc(s_lt, 1)

                pairs(l, "br1", gate("br1"), lru)
                act.wait_ge(s_lh, BLOCKS * (l + 1) + 1)
                wait_taken(act, l, "br1")
                pairs(l, "y", product("y", ACT.Gelu_apprx_tanh))
                pairs(l, "br2", gate("br2"))

                def copy_out(i, j):
                    A_(mixed[:, bass.ds(i * 4 + 2 * j, 2), c0:], PAIR[j][:, :, c0:], ACT.Copy).then_inc(taken[j], 1)

                pairs(l, "out", copy_out)

                def taken_tiles(name):
                    q0 = (first_pair[l, name]) // 2
                    return lambda k: act.wait_ge(taken[(k // 2 - 1) % 2], q0 + (k // 2 - 1) // 2 + 2)

                norm_stats(4 * l + 1, mixed, taken_tiles("out"), c0)
                norm_stats(4 * l + 2, x, lambda k: act.wait_ge(s_x, KT * 2 * l + k), c0)
                make_h(l, 2 * l + 1, 3, segs)

                n_p = before(PRODUCTS, l, "up")

                def up(i, j):
                    for f in range(2):
                        t = i * 4 + (2 * j + f)
                        ins = A_(fa[j][:, f, c0:], PAIR[j][:, f, c0:], ACT.Identity,
                                 scale=pcol(l, "fw")[:, bass.ds(t + 2 * FT, 1)], bias=pcol(l, "fb")[:, bass.ds(t, 1)])
                    ins.then_inc(s_eva, 1)
                    act.wait_ge(taken[j], i + (first_pair[l, "up"] // 2 + 2))
                    A_(fs[j][:, 0, c0:], fa[j][:, 0, c0:], ACT.Silu).then_inc(s_fs, 1)
                    act.wait_ge(s_evp, i * 2 + (n_p + j + 1))
                    A_(fh[:, i * 2 + j, c0:], fa[j][:, 1, c0:], ACT.Copy).then_inc(s_evh, 1)

                pairs(l, "up", up)

                def copy_down(i, j):
                    A_(y2[:, bass.ds(i * 4 + 2 * j, 2), c0:] if not isinstance(i, int) else
                       y2[:, i * 4 + 2 * j:i * 4 + 2 * j + 2, c0:], PAIR[j][:, :, c0:], ACT.Copy).then_inc(taken[j], 1)

                pairs(l, "down", copy_down)
                norm_stats(4 * l + 3, y2, taken_tiles("down"), c0)

        @block.vector
        def _(dve):
            chain = Chain(dve, s_c_dve)
            link = chain.link
            V = nc.vector

            def lo(b4, off):
                dve.wait_ge(s_hi, b4 * 4 + (off + 1))
                V.tensor_tensor(wlo[off % 2][:], wraw[off % RAW][:], whi[off % 2][:].bitcast(F32), ALU.subtract)\
                    .then_inc(s_lo, 1)

            def pairs(l, name, evac, stride=0, beside=None):
                m, last = units_of[name], (l, name) == order[-1]
                b, turns = first_unit[l, name] // 4, pairs_of[name] // 2
                stride += ADA_SUM if (l, name) in ADA_STAGES else 0

                def turn(i, b4, final):
                    for j in range(2):
                        for o in range(2 + m * j, m * (j + 1) + 2):
                            if (l, name) in ADA_STAGES:
                                for u in {2: (0,), 3: (1,), 4: (2, 3)}.get(o, ()):
                                    ada_unit(l, name, i, u)
                            if not (final and o >= 2 * m):
                                lo(b4, o)
                            if beside:
                                beside(i, o - 2)
                        if j and (l, name) in ADA_STAGES:
                            take_mod(l, name, i)
                        if evac:
                            evac(i, j)

                with dve.Fori(0, turns - last) as i:
                    chain.enter(i, stride)
                    turn(i, i * (m // 2) + b, False)
                    chain.leave(turns - last)
                if last:
                    turn(turns - 1, b + (turns - 1) * (m // 2), True)

            def ada_products(dst, w, u):
                for kt in range(AK):
                    for c in range(2):
                        v, k = dst[:, c], csil[:, AK * u + kt, c:c + 1]
                        ins = (V.tensor_scalar(v, w[:, kt], k, None, ALU.mult) if u == kt == 0 else
                               V.scalar_tensor_tensor(v, w[:, kt], k, v, ALU.mult, ALU.add))
                    if kt < AK - 1:
                        link(ins)
                return ins

            def ada_unit(l, name, i, u):
                a0 = ada_before(l, name)
                dve.wait_ge(wada_full[u % 2], i * (8 * ADA_SUM) + (8 * a0 + 16 * (u // 2) + 16))
                ada_products(ada_sum, wada[u % 2], u).then_inc(wada_used, 1)
                dve.wait_ge(wada_used, i * ADA_SUM + (ADA_FIRST // 2 + a0 + u + 1))

            def take_mod(l, name, i):
                a0 = (ADA_FIRST + ada_before(l, name)) // ADA_SUM
                layer, first = a0 // (ADA_UNITS // ADA_SUM), a0 % (ADA_UNITS // ADA_SUM)
                dve.wait_ge(s_red, i + (takes_before(l, name) + 2))
                add_bias(layer, i * 4 + 4 * first, 4, 4).then_inc(s_ada, 1)

            def add_bias(layer, t, n, bank):
                return V.tensor_tensor(mod[:, layer, ds(t, n), :], ps[:, bank, 0:2 * n].rearrange("p (t s) -> p t s", s=2),
                                       pcol(layer, "b_ada")[:, ds(t, n), None].broadcast_to([P, n, 2]), ALU.add)

            def gains(l, norms):
                for n in norms:
                    m, plus = ((1, 1.0), (2, 0.0), (4, 1.0), (5, 0.0))[n]
                    link(V.scalar_tensor_tensor(gmod[:, n], MOD[l][:, 8 * m:8 * m + 8], plus,
                                                pcol(l, "gains")[:, 8 * n:8 * n + 8, None].broadcast_to([P, KT, 2]),
                                                ALU.add, ALU.mult))

            def split_h(l, n, gain, shift, segs):
                c0 = segs[0] * CTX
                dve.wait_ge(s_rstd, n_stat[n] + 1)
                for k0 in range(0, KT, 2):
                    for k in (k0, k0 + 1):
                        for s in segs:
                            c = slice(s * CTX, (s + 1) * CTX)
                            ins = V.scalar_tensor_tensor(nt[:, k, c], x[:, k, c], gmod[:, gain, k, s:s + 1], rstd[:, c],
                                                         ALU.mult, ALU.mult)
                        ins.then_inc(s_nt, 1)
                    for k in (k0, k0 + 1):
                        dve.wait_ge(s_hhi, KT * n + k + 1)
                        for s in segs:
                            c = slice(s * CTX, (s + 1) * CTX)
                            ins = V.scalar_tensor_tensor(hl[:, k, c], nt[:, k, c], MOD[l][:, 8 * shift + k, s:s + 1],
                                                         hh[:, k, c].bitcast(F32), ALU.add, ALU.subtract)
                        ins.then_inc(s_h, 1)

            def residual(n, src, gain, segs):
                dve.wait_ge(s_rstd, n + 1)
                for k in range(KT):
                    for s in segs:
                        c = slice(s * CTX, (s + 1) * CTX)
                        link(V.scalar_tensor_tensor(src[:, k, c], src[:, k, c], gmod[:, gain, k, s:s + 1], rstd[:, c],
                                                    ALU.mult, ALU.mult))
                    c = slice(segs[0] * CTX, TOK)
                    V.tensor_tensor(x[:, k, c], x[:, k, c], src[:, k, c], ALU.add).then_inc(s_x, 1)

            n_stat = {0: 0, 1: 2, 2: 4, 3: 6}
            V.memset(ones[:], 1.0).then_inc(s_ready, 1)
            V.memset(one[:], 1.0).then_inc(s_ready, 1)
            V.memset(eps[:], EPS).then_inc(s_ready, 1)
            link(V.memset(scanmask[:], 1.0))
            link(V.memset(scanmask[:, :, 0:1], 0.0))
            for s, k in ((taken[0], 1), (taken[1], 1), (s_ltz, 2), (s_on, 1), (s_lz, 4), (wada_used, ADA_FIRST // 2), (s_asd, 2), (s_lh, 1), (s_alo, 4)):
                dve.sem_inc(s, k)
            dve.wait_ge(s_par, 48)
            dve.wait_ge(s_const, CONSTS)
            dve.wait_ge(s_in, 16)
            for l in range(DEPTH):
                c0, segs = c0_of(l), segs_of(c0_of(l))
                W = TOK - c0
                if l == 0:
                    dve.wait_ge(s_csil, 1)
                    for g, dst in ((2, ada_sum), (3, ada_sum_first)):
                        dve.wait_ge(ada_full[g], 64)
                        for u in range(ADA_SUM):
                            link(ada_products(dst, ada_first[g][:, u], u))
                        dve.sem_inc(s_asum, 1)
                    dve.wait_ge(s_red, 2)
                    add_bias(0, 0, 8, 4)
                    add_bias(0, 8, 8, 5).then_inc(s_ada, 1)
                dve.wait_ge(s_ada, 1 if l == 0 else ADA_TAKES)
                gains(l, range(4) if l else (0,))
                link(V.tensor_scalar(hbias[:], pcol(l, "b_gate"), 0.5, None, ALU.mult))
                dve.wait_ge(s_sp, l + 1)
                link(V.tensor_tensor(sp[:, 0], sp[:, 0], sp[:, 1], ALU.add))
                V.tensor_scalar(sp[:, 2], sp[:, 0], -4.0, None, ALU.mult).then_inc(s_c4, 1)
                V.memset(attm[:], 0.0).then_inc(s_mod, 1)
                split_h(l, 2 * l, 0, 0, (0, 1))
                if l == 0:
                    for s in range(2):
                        dve.wait_ge(s_hi, s + 1)
                        V.tensor_tensor(wlo[s][:], wraw[s][:], whi[s][:].bitcast(F32), ALU.subtract).then_inc(s_lo, 1)
                pairs(l, "gqk", None)
                dve.wait_ge(s_lrw, 16 * (l + 1))
                V.memset(lrh[:].bitcast(F32), 0.0).then_inc(s_lrz, 1)
                V.memset(lrl[:].bitcast(F32), 0.0).then_inc(s_lrz, 1)
                dve.wait_ge(s_lrh, l + 1)
                V.tensor_tensor(lrl[:, :, 0:2 * RANK], lrw[:], lrh[:, :, 0:2 * RANK].bitcast(F32), ALU.subtract)\
                    .then_inc(s_lrl, 1)
                pairs(l, "gv", None)

                def chunks(v):
                    return v.rearrange("p (n c) -> p n c", c=CHUNK)

                def gla_prepare(h):
                    n = h + HEADS * l
                    dve.wait_ge(s_ga, n + 1)
                    for d in range(2):
                        ins = V.tensor_scalar(gl_m[:, d], ps[:, d], pcol(l, "b_dec")[:, ds(h * 2 + d, 1)], 0.0,
                                              ALU.add, ALU.min)
                    link(ins)
                    dve.wait_ge(s_gl, n + 1)
                    link(V.tensor_tensor(gl_m[:], gl_m[:], gl_l[:], ALU.subtract))
                    mask = scanmask[:].rearrange("p n c -> p (n c)")
                    V.tensor_tensor_scan(gl_c[:, 0], mask, gl_m[:, 0], 0.0, ALU.mult, ALU.add)
                    link(V.tensor_tensor_scan(gl_c[:, 1, ::-1], mask, gl_m[:, 1, ::-1], 0.0, ALU.mult, ALU.add))
                    for d, end in enumerate((CHUNK - 1, 0)):
                        v = chunks(gl_c[:, d])
                        ins = V.tensor_tensor(chunks(gl_ke[:, d]), v[:, :, end:end + 1].broadcast_to([P, NCH, CHUNK]), v,
                                              ALU.subtract)
                    ins.then_inc(s_gc, 1)
                    k = gqk[:, h, 1:2, :].broadcast_to([P, 2, TOK])
                    dve.wait_ge(s_ge, n * 3 + 1)
                    V.tensor_tensor(gl_ke[:], gl_ke[:], k, ALU.mult).then_inc(s_go, 1)
                    dve.wait_ge(s_ge, n * 3 + 2)
                    V.tensor_tensor(gl_ki[:, :, c0:], gl_ki[:, :, c0:], k[:, :, c0:], ALU.mult).then_inc(s_go, 1)

                def gla_states(h, d):
                    n = h + HEADS * l
                    for e in range(4):
                        dve.wait_ge(s_kv, n * 8 + (4 * d + e + 1))
                        for p in range(2 * e, min(2 * e + 2, NCH - 1)):
                            c = CHUNK_ORDER[d][p]
                            kv_ = ps[:, KV_BANK[e % 2] + c % 2, 0:DV]
                            if p == 0:
                                ins = V.tensor_copy(state[:, d, 1], kv_)
                            else:
                                ins = V.scalar_tensor_tensor(state[:, d, p + 1], state[:, d, p], g_end[:, d, c:c + 1],
                                                             kv_, ALU.mult, ALU.add)
                            if p % 2 or p == NCH - 2:
                                ins.then_inc(s_state, 1)
                                dve.wait_ge(s_state, n * 8 + (4 * d + e + 1))
                            else:
                                link(ins)

                def gla_norm(h):
                    dve.wait_ge(s_orstd, h + (HEADS * l + 1))
                    for t in range(2):
                        ins = V.scalar_tensor_tensor(gqk[:, h, t, c0:], ps[:, 4 + t, c0:],
                                                     pcol(l, "g_gla")[:, ds(h * 2 + t, 1)], gstat[:, 0, c0:],
                                                     ALU.mult, ALU.mult)
                    ins.then_inc(s_on, 1)

                def gla_turn(h, prev, nxt):
                    n = h + HEADS * l
                    if prev:
                        dve.wait_ge(s_o, n)
                    dve.wait_ge(s_ge, n * 3 + 3)
                    q = gqk[:, h, 0:1, c0:].broadcast_to([P, 2, W])
                    V.scalar_tensor_tensor(gl_qd[:, :, c0:], q, DK ** -0.5, gl_ep[:, :, c0:], ALU.mult, ALU.mult)\
                        .then_inc(s_go, 1)
                    dve.wait_ge(s_att, n + 1)
                    for d, end in enumerate((CHUNK - 1, 0)):
                        V.tensor_copy(g_end[:, d], chunks(gl_ep[:, d])[:, :, end])
                    for d in range(2):
                        v = slice(c0 // P, TOK // P)
                        V.copy_predicated(attm[:, d].rearrange("p (t c) -> p t c", c=P)[:, v],
                                          KEEP[:, d:d + 1].broadcast_to([P, (TOK - c0) // P, P]),
                                          ps[:, d].rearrange("p (t c) -> p t c", c=P)[:, v]).then_inc(s_attm, 1)
                    dve.wait_ge(s_attm, n * 2 + 2)
                    gla_states(h, 0)
                    if prev:
                        gla_norm(h - 1)
                    gla_states(h, 1)
                    if nxt:
                        gla_prepare(h + 1)

                gla_prepare(0)
                gla_turns(dve, chain, 9, gla_turn)
                gla_norm(HEADS - 1)
                dve.wait_ge(s_on, 1 + HEADS * (l + 1))

                def product(name, other):
                    n0, q0 = before(PRODUCTS, l, name), first_pair[l, name]

                    def evac(i, j):
                        dve.wait_ge(taken[j], i + (q0 // 2 + 2))
                        V.tensor_tensor(evp[j][:, :, c0:], ev[j][:, :, c0:], other(i, j), ALU.mult).then_inc(s_evp, 1)
                        dve.wait_ge(s_evh, i * 2 + (n0 + j + 1))
                        t = bass.ds(i * 4 + 2 * j, 2)
                        V.tensor_tensor(bl[:, t, c0:], evp[j][:, :, c0:], bh[:, t, c0:].bitcast(F32), ALU.subtract)\
                            .then_inc(s_b, 1)
                    return evac

                def gate(name):
                    def evac(i, j):
                        if j == 0:
                            return
                        tiles_ = bass.ds(i * 2, 2)
                        b4 = i + first_unit[l, name] // 4
                        dve.wait_ge(s_used, b4 * 4 + 4)
                        dve.wait_ge(taken[0], i + (first_pair[l, name] // 2 + 2))
                        dst = mixed[:, tiles_, c0:] if name == "br0" else evp[0][:, :, c0:]
                        V.scalar_tensor_tensor(dst, ev[0][:, :, c0:], 1.0, PAIR[1][:, :, c0:], ALU.add, ALU.mult)\
                            .then_inc(taken[1], 1)
                        if name == "br0":
                            return
                        dve.wait_ge(taken[1], i + (first_pair[l, name] // 2 + 2))
                        ins = V.tensor_tensor(mixed[:, tiles_, c0:], mixed[:, tiles_, c0:], evp[0][:, :, c0:], ALU.add)
                        if name == "br1":
                            link(ins)
                        else:
                            ins.then_inc(s_evp, 1)
                            dve.wait_ge(s_evh, i + (before(PRODUCTS, l, name) + 1))
                            V.scalar_tensor_tensor(ml[:, tiles_, c0:], mixed[:, tiles_, c0:], 0.5,
                                                   mh[:, tiles_, c0:].bitcast(F32), ALU.mult, ALU.subtract)\
                                .then_inc(s_b, 1)
                    return evac

                pairs(l, "r", product("r", lambda i, j: gqk[:, i * 2 + j, :, c0:]))
                pairs(l, "br0", gate("br0"))
                pairs(l, "aq", None)
                if l == 0:
                    dve.wait_ge(s_ada, takes_before(l, "akv"))
                    gains(l, (1, 2, 3))
                pairs(l, "akv", None)

                t0 = (AQ + AKV) * l

                def att_norm(i, t, c):
                    for j in range(2):
                        v = aqk[:, i * 2 + (t + j), c:]
                        V.scalar_tensor_tensor(v, v, pcol(l, "g_qk")[:, bass.ds(i * 2 + (t + j), 1)],
                                               astat[:, i * 2 + (t + j), c:], ALU.mult, ALU.mult).then_inc(s_anorm, 1)
                    for j in range(2):
                        v = aqk[:, i * 2 + (t + j), CTX:]
                        dve.wait_ge(s_anorm, i * 2 + (t0 + t + j + 1))
                        V.tensor_tensor(arot[j][:, 1], v, cs[:, 0], ALU.mult)
                        dve.wait_ge(s_arot, i * 2 + (t0 + t + j + 1))
                        link(V.tensor_tensor(arot[j][:, 0], ps[:, 4 + j, 0:SEQ], cs[:, 1], ALU.mult))
                        V.tensor_tensor(v, arot[j][:, 0], arot[j][:, 1], ALU.add).then_inc(s_arope, 1)
                for half in range(2):
                    dve.wait_ge(s_arstd, 3 * l + half + 1)
                    with dve.Fori(0, AQ // 4) as i:
                        chain.enter(i, 2)
                        att_norm(i, AQ // 2 * half, c0)
                        chain.leave(AQ // 4)
                dve.wait_ge(s_arstd, 3 * l + 3)
                att_norm(0, AQ, 0)

                n0, ng = att_items(l)

                def row_max(i, k):
                    g, b, (n, _, _) = segs[k % ng], k % 2, att_item(i, k, n0, ng)
                    dve.wait_ge(s_sc, n)
                    link(V.tensor_reduce(mx[:, b], PAIR[b][:, :, 0:(g + 1) * CTX], AX_X, ALU.max))
                    V.tensor_scalar(nb[:, b], mx[:, b], -HSCALE, None, ALU.mult).then_inc(s_nb, 1)

                def normalise(i, k):
                    g, b, (n, _, _) = segs[k % ng], k % 2, att_item(i, k, n0, ng)
                    dve.wait_ge(s_ex, n)
                    link(V.reciprocal(rsum[:, b], sums[:, b]))
                    for t in range(2):
                        v = prob[b][:, t, 0:(g + 1) * CTX]
                        ins = V.tensor_scalar(v, v, rsum[:, b, t:t + 1], None, ALU.mult)
                    ins.then_inc(s_pn, 1)

                def att_turn(i, last):
                    for k in range(2 * ng):
                        g, b, (n, head, _) = segs[k % ng], k % 2, att_item(i, k, n0, ng)
                        if not (last and k + 2 >= 2 * ng):
                            row_max(i, k + 2)
                        if not (last and k + 1 >= 2 * ng):
                            normalise(i, k + 1)
                        dve.wait_ge(s_ahi, n)
                        c = slice(g * CTX, (g + 1) * CTX)
                        V.tensor_tensor(bl[:, head, c], ps[:, 6 + b, 0:SEQ], bh[:, head, c].bitcast(F32), ALU.subtract)\
                            .then_inc(s_alo, 1)

                row_max(0, 0)
                row_max(0, 1)
                normalise(0, 0)
                att_turns(dve, chain, 4 * ng, att_turn)

                def seg(v, c):
                    return v.rearrange("p (s t) -> p s t", t=CTX)[:, c // CTX:]

                def taps(name, dst, taps_, c, tile, n0, q0):
                    def evac(i, j):
                        dve.wait_ge(s_eva, i * 2 + (n0 + j + 1))
                        for n, (k, sh) in enumerate(taps_):
                            for f in range(2):
                                o, v = seg(dst(i, j, f), c), seg(PAIR[j][:, f], c)
                                a, b = (slice(-sh, None), slice(0, sh)) if sh < 0 else (slice(0, CTX - sh), slice(sh, CTX))
                                a, b = (slice(-sh, CTX), slice(0, CTX + sh)) if sh < 0 else (a, b)
                                ins = V.scalar_tensor_tensor(o[:, :, a], v[:, :, b], tile(i, j, f, k), o[:, :, a],
                                                             ALU.mult, ALU.add)
                            if n < len(taps_) - 1:
                                link(ins)
                        ins.then_inc(taken[j], 1)
                    return evac

                pairs(l, "lx", taps("lx", lambda i, j, f: xc[:, i * 4 + (2 * j + f)], ((0, -2), (1, -1), (3, 1)), 0,
                                    lambda i, j, f, k: pcol(l, "cw")[:, bass.ds(i * 4 + (KT * k + 2 * j + f), 1)],
                                    before(CENTRES, l, "lx"), first_pair[l, "lx"]), stride=4)

                wait_taken(dve, l, "lx")

                def lru(i, o):
                    j = o // 2
                    n = i * 2 + (BLOCKS * l + j + 1)
                    v = xc[:, i * 2 + j]
                    if o % 2 == 0:
                        dve.wait_ge(s_la2, n)
                        V.scalar_tensor_tensor(l_a2[:], l_a2[:], 1.0, l_th[:], ALU.add, ALU.mult).then_inc(s_lv, 1)
                        link(V.scalar_tensor_tensor(l_ti[:], l_ti[:], 1.0, xc[:, i * 2 + j, None]
                                                    .broadcast_to([P, 2, TOK]), ALU.add, ALU.mult))
                        return
                    dve.wait_ge(s_ls, n)
                    link(V.tensor_tensor(l_ti[:], l_ti[:], l_tr[:], ALU.mult))
                    V.tensor_tensor_scan(l_h[:, 0], l_a[:, 0], l_ti[:, 0], 0.0, ALU.mult, ALU.add)
                    link(V.tensor_tensor_scan(l_h[:, 1, 0:CTX][:, ::-1], l_a[:, 1, 0:CTX][:, ::-1],
                                              l_ti[:, 1, 0:CTX][:, ::-1], 0.0, ALU.mult, ALU.add))
                    link(V.tensor_tensor_scan(l_h[:, 1, CTX:][:, ::-1], l_a[:, 1, CTX:][:, ::-1],
                                              l_ti[:, 1, CTX:][:, ::-1], l_h[:, 1, 0:1], ALU.mult, ALU.add))
                    V.tensor_tensor(v[:, c0:], l_h[:, 0, c0:], l_h[:, 1, c0:], ALU.add).then_inc(s_lh, 1)

                pairs(l, "br1", gate("br1"), stride=9, beside=lru)
                dve.wait_ge(s_lh, 1 + BLOCKS * (l + 1))

                pairs(l, "y", product("y", lambda i, j: xc[:, bass.ds(i * 4 + 2 * j, 2), c0:]))
                pairs(l, "br2", gate("br2"))
                pairs(l, "out", None)
                residual(4 * l + 1, mixed, 1, segs)
                split_h(l, 2 * l + 1, 2, 3, segs)

                n_p = before(PRODUCTS, l, "up")
                up_taps = taps("up", lambda i, j, f: fa[j][:, f], ((0, -1), (2, 1)), c0,
                               lambda i, j, f, k: pcol(l, "fw")[:, bass.ds(i * 4 + (2 * FT * k + 2 * j + f), 1)],
                               before(CENTRES, l, "up"), first_pair[l, "up"])

                def up(i, j):
                    up_taps(i, j)
                    dve.wait_ge(s_fs, i * 2 + (FT * l + j + 1))
                    V.tensor_tensor(fa[j][:, 1, c0:], fs[j][:, 0, c0:], fa[j][:, 1, c0:], ALU.mult).then_inc(s_evp, 1)
                    dve.wait_ge(s_evh, i * 2 + (n_p + j + 1))
                    V.tensor_tensor(fl[:, i * 2 + j, c0:], fa[j][:, 1, c0:], fh[:, i * 2 + j, c0:].bitcast(F32),
                                    ALU.subtract).then_inc(s_b, 1)

                pairs(l, "up", up, stride=2)
                dve.wait_ge(s_b, before(PRODUCTS, l, "up") + FT)
                pairs(l, "down", None)
                residual(4 * l + 3, y2, 3, segs)

        @block.tensor
        def _(pe):
            mm = nc.tensor.matmul

            def ada_reduce(src, bank, at_):
                for f in range(AC // P):
                    for c in range(2):
                        ins = mm(ps[:, bank, at_ + 2 * f + c:at_ + 2 * f + c + 1], src[:, c, f * P:(f + 1) * P],
                                 ones[:, 0:1], start=True, stop=True)
                ins.then_inc(s_red, 1)

            def ada_turn(l, name, i):
                pe.wait_ge(wada_used, i * ADA_SUM + (ADA_FIRST // 2 + ada_before(l, name) + ADA_SUM))
                pe.wait_ge(s_ada, i + takes_before(l, name))
                ada_reduce(ada_sum, 4, 0)

            def lru_gates(l, i, k):
                if k == 0:
                    wait_taken(pe, l, "lx")
                pe.wait_ge(gate_full[k], i * 16 + (8 * BLOCKS * l + 16))
                for d in range(2):
                    pe.wait_ge(s_ltz, i * 4 + (2 * BLOCKS * l + 2 * k + d + 1))
                    for g in range(2):
                        ins = mm(ps[:, 4 + 2 * d + g], wgate[k][:, 2 * d + g, :], xc[:, i * 2 + k, :],
                                 start=True, stop=True)
                    ins.then_inc(s_lz, 1)

            def project(l, name, moving, feature_major=True, ready=None, ready_pair=0):
                m, turns = units_of[name], pairs_of[name] // 2
                b, q2 = first_unit[l, name] // 4, first_pair[l, name] // 2
                with pe.Fori(0, turns) as i:
                    b4 = i * (m // 2) + b
                    for j in range(2):
                        pe.wait_ge(taken[j], i + (q2 + 1))
                        mh_, ml_, c = moving(i, j)
                        for h in range(m):
                            o = m * j + h
                            w_h, w_l = whi[o % 2], wlo[o % 2]
                            nk = DOWN_LAST if name == "down" and h == m - 1 else UK
                            pe.wait_ge(s_hi, b4 * 4 + (o + 1))
                            if ready and j == ready_pair:
                                ready(h)
                            token_major = not feature_major or (name == "akv" and j == 1)
                            for part, (w, parts) in enumerate(((w_h, (mh_, ml_)), (w_l, (mh_,)))):
                                if part:
                                    pe.wait_ge(s_lo, b4 * 4 + (o + 1))
                                for r in range(4 if token_major else 2):
                                    for x_ in parts:
                                        for k in range(nk):
                                            kk = UK * h + k
                                            first = h == 0 and k == 0 and part == 0 and x_ is mh_
                                            final = h == m - 1 and k == nk - 1 and part == 1
                                            if token_major:
                                                ins = mm(PAIR[j][:, r // 2, 256 * (r % 2):256 * (r % 2 + 1)],
                                                         x_[:, kk, r * P:(r + 1) * P], w[:, k, :],
                                                         start=first and r % 2 == 0, stop=final and r % 2 == 1,
                                                         skip_group_check=True)
                                            else:
                                                c_ = c[r]
                                                ins = mm(PAIR[j][:, r, c_:], w[:, k, r * P:(r + 1) * P], x_[:, kk, c_:],
                                                         start=first, stop=final)
                            ins.then_inc(s_used, 1)
                            if name == "br1" and o % 2 == 0:
                                lru_gates(l, i, o // 2)
                            if (l, name) in ADA_STAGES and o == 3:
                                ada_turn(l, name, i)

            def sum_squares(n, c0):
                for j in range(4):
                    pe.wait_ge(s_sq, 4 * n + j + 1)
                    for k in (2 * j, 2 * j + 1):
                        ins = mm(ps[:, 6, c0:], ones[:], sq[:, k, c0:], start=k == 0, stop=k == KT - 1)
                ins.then_inc(s_stat, 1)

            def normed(n):
                return lambda h: pe.wait_ge(s_h, KT * n + UK * (h + 1))

            def split(l, name, each):
                n, most = before(PRODUCTS, l, name), pairs_of[name] // (2 if name[:2] == "br" else 1)
                return lambda h: pe.wait_ge(s_b, n + min(UK * (h + 1) // each, most))

            pe.wait_ge(s_ready, READY)
            pe.wait_ge(s_const, CONSTS)
            pe.wait_ge(s_csil, 1)
            for l in range(DEPTH):
                c0, segs = c0_of(l), segs_of(c0_of(l))
                if l == 0:
                    for g in range(2):
                        pe.wait_ge(ada_full[g], 64)
                        for f in range(AC // P):
                            t = 4 * g + f
                            for k in range(KT):
                                mm(ps[:, 4, 2 * t:2 * t + 2], ada_first[g][:, k // AK, k % AK, f * P:(f + 1) * P],
                                   csil[:, k, :], start=k == 0, stop=k == KT - 1)
                    for g, src in ((2, ada_sum), (3, ada_sum_first)):
                        pe.wait_ge(s_asum, g - 1)
                        ada_reduce(src, 5, 8 * (g - 2))
                sum_squares(4 * l, 0)
                both = (0, 0)
                project(l, "gqk", lambda i, j: (hh, hl, (c0, 0)), ready=normed(2 * l))
                project(l, "gv", lambda i, j: (hh, hl, None), feature_major=False)

                pe.wait_ge(s_lrh, l + 1)
                for x_ in (hh, hl):
                    for k in range(KT):
                        mm(ps[:, 7, :], lrh[:, k, :], x_[:, k, :], start=k == 0 and x_ is hh, stop=False)
                pe.wait_ge(s_lrl, l + 1)
                for k in range(KT):
                    ins = mm(ps[:, 7, :], lrl[:, k, :], hh[:, k, :], start=False, stop=k == KT - 1)
                ins.then_inc(s_lrp, 1)
                pe.wait_ge(s_lr, l + 1)

                t_first = c0 // P

                def gla_decays(h):
                    pe.wait_ge(s_wdh, h + (HEADS * l + 1))
                    for d in range(2):
                        ins = mm(ps[:, d], wdh[:, d, :], lr[:], start=True, stop=True)
                    ins.then_inc(s_gz, 1)

                def gla_stat(h):
                    pe.wait_ge(s_osq, h + (HEADS * l + 1))
                    for v in range(2):
                        ins = mm(ps[:, 6, c0:], ones[:], go[:, v, c0:], start=v == 0, stop=v == 1)
                    ins.then_inc(s_ostat, 1)

                def gla_kv(h, d, prev):
                    n = h + HEADS * l
                    for e in range(4):
                        g = 4 * d + e
                        if g == 1 and prev:
                            pe.wait_ge(s_orstd, n)
                        if g >= 2:
                            pe.wait_ge(s_state, n * 8 + (g - 1))
                        for p in range(2 * e, min(2 * e + 2, NCH - 1)):
                            c = CHUNK_ORDER[d][p]
                            r = slice((c % 2) * CHUNK, (c % 2 + 1) * CHUNK)
                            ins = mm(ps[:, KV_BANK[e % 2] + c % 2, 0:DV], keT[r, d, c // 2, :],
                                     vh[r, c // 2, :], start=True, stop=True)
                        ins.then_inc(s_kv, 1)

                def gla_turn(h, prev, nxt):
                    n = h + HEADS * l
                    pe.wait_ge(s_go, n * 3 + 1)
                    for d in range(2):
                        for t in range(TOK // P):
                            ins = nc.tensor.transpose(ps[:, 2 + d, t * P:(t + 1) * P], gl_ke[:, d, t * P:(t + 1) * P],
                                                      ident[:])
                    ins.then_inc(s_keT, 1)
                    pe.wait_ge(s_go, n * 3 + 3)
                    for d in range(2):
                        for t in range(t_first, TOK // P):
                            c = slice(t * P, (t + 1) * P)
                            ins = mm(ps[:, d, c], gl_ki[:, d, c], gl_qd[:, d, c], start=True, stop=True)
                    ins.then_inc(s_att, 1)
                    if prev:
                        gla_stat(h - 1)
                    pe.wait_ge(s_vh, n + 1)
                    pe.wait_ge(s_keTc, n + 1)
                    gla_kv(h, 0, prev)
                    pe.wait_ge(s_attm, n * 2 + 2)
                    if nxt:
                        gla_decays(h + 1)
                    gla_kv(h, 1, prev)
                    pe.wait_ge(s_on, n + 1)
                    for d in range(2):
                        for t in range(t_first, TOK // P):
                            c = slice(t * P, (t + 1) * P)
                            for v in range(2):
                                mm(ps[:, 4 + v, c], vh[:, t, v * P:(v + 1) * P], attm[:, d, c],
                                   start=d == 0 and t == t_first, stop=False, skip_group_check=True)
                    for d in range(2):
                        for p in range(1, NCH):
                            c = CHUNK_ORDER[d][p]
                            if p % 2 or p == NCH - 1:
                                pe.wait_ge(s_state, n * 8 + (4 * d + (p - 1) // 2 + 1))
                            if c * CHUNK < c0:
                                continue
                            cc = slice(c * CHUNK, (c + 1) * CHUNK)
                            for v in range(2):
                                ins = mm(ps[:, 4 + v, cc], state[:, d, p, v * P:(v + 1) * P], gl_qd[:, d, cc],
                                         start=False, stop=d == 1 and p == NCH - 1, skip_group_check=True)
                    ins.then_inc(s_o, 1)

                gla_decays(0)
                gla_turns(pe, None, 0, gla_turn)
                gla_stat(HEADS - 1)

                pe.wait_ge(s_on, 1 + HEADS * (l + 1))
                project(l, "r", lambda i, j: (hh, hl, (c0, c0)))
                lat = (c0, c0)
                project(l, "br0", lambda i, j: ((bh, bl, lat) if j else (hh, hl, lat)), ready=split(l, "r", 2),
                        ready_pair=1)
                project(l, "aq", lambda i, j: (hh, hl, lat))
                project(l, "akv", lambda i, j: (hh, hl, both))

                t0 = (AQ + AKV) * l
                wait_taken(pe, l, "akv")
                pe.wait_ge(s_ada, takes_before(l, "akv"))

                def att_sums(i, t, c):
                    for j in range(2):
                        n = i * 2 + (t0 + t + j + 1)
                        pe.wait_ge(s_asq, n)
                        mm(ps[:, i * 2 + j, c:], ones[:], asq[j][:, 0, c:], start=True, stop=True).then_inc(s_asd, 1)

                def att_swap(i, t):
                    for j in range(2):
                        n = i * 2 + (t0 + t + j + 1)
                        pe.wait_ge(s_anorm, n)
                        pe.wait_ge(s_arope, n - 2) if t0 + t + j > 1 else None
                        mm(ps[:, 4 + j, 0:SEQ], swap[:], aqk[:, i * 2 + (t + j), CTX:], start=True, stop=True)\
                            .then_inc(s_arot, 1)
                with pe.Fori(0, AQ // 2) as i:
                    att_sums(i, 0, c0)
                pe.wait_ge(s_aln, 2 * l + 1)
                att_sums(0, AQ, 0)
                with pe.Fori(0, AQ // 2) as i:
                    att_swap(i, 0)
                att_swap(0, AQ)

                n0, ng = att_items(l)
                pe.wait_ge(s_arope, t0 + AQ + AKV)

                def scores(i, k):
                    g, b, (n, _, kv) = segs[k % ng], k % 2, att_item(i, k, n0, ng)
                    if k % ng == 0:
                        pe.wait_ge(s_qc, i * 2 + (AQ * l + k // ng + 1))
                    for t in range(2):
                        q0 = g * CTX + t * P
                        ins = mm(PAIR[b][:, t, 0:(g + 1) * CTX], qcur[kv][:, 0, q0:q0 + P],
                                 aqk[:, AQ + kv, 0:(g + 1) * CTX], start=True, stop=True)
                    ins.then_inc(s_sc, 1)

                def att_turn(i, last):
                    for k in range(2 * ng):
                        g, b, (n, _, kv) = segs[k % ng], k % 2, att_item(i, k, n0, ng)
                        pe.wait_ge(s_pn, n)
                        for st in range(2 * g + 2):
                            for t in range(2):
                                c = (st % 2) * SEQ + t * P
                                ins = nc.tensor.transpose(ps[:, 4 + st // 2, c:c + P],
                                                          prob[b][:, t, st * P:(st + 1) * P], ident[:])
                        ins.then_inc(s_pt, 1)
                        if not (last and k + 2 >= 2 * ng):
                            scores(i, k + 2)
                        pe.wait_ge(s_ptc, n)
                        pe.wait_ge(s_alo, n + 1 + 1)
                        for st in range(2 * g + 2):
                            ins = mm(ps[:, 6 + b, 0:SEQ], av[:, st, kv * HD:(kv + 1) * HD], probT[b][:, st, :],
                                     start=st == 0, stop=st == 2 * g + 1)
                        ins.then_inc(s_av, 1)

                scores(0, 0)
                scores(0, 1)
                att_turns(pe, None, 0, att_turn)

                pe.wait_ge(s_alo, 4 + n0 + AQ * ng)
                project(l, "lx", lambda i, j: (hh, hl, both))

                project(l, "br1", lambda i, j: ((bh, bl, lat) if j else (hh, hl, lat)))
                pe.wait_ge(s_ltz, 2 + 16 * (l + 1))
                project(l, "y", lambda i, j: (hh, hl, lat))
                project(l, "br2", lambda i, j: ((bh, bl, lat) if j else (hh, hl, lat)), ready=split(l, "y", 2),
                        ready_pair=1)
                project(l, "out", lambda i, j: (mh, ml, lat), ready=split(l, "br2", 2))
                sum_squares(4 * l + 1, c0)
                sum_squares(4 * l + 2, c0)
                project(l, "up", lambda i, j: (hh, hl, lat), ready=normed(2 * l + 1))
                project(l, "down", lambda i, j: (fh, fl, lat), ready=split(l, "up", 1))
                sum_squares(4 * l + 3, c0)



def units(w, order):
    k_tiles = -(-w.shape[0] // (P * UK)) * UK
    if w.shape[0] < P * k_tiles:
        w = np.concatenate([w, np.zeros((P * k_tiles - w.shape[0], w.shape[1]), w.dtype)])
    got = []
    for cols in order:
        v = w[:, cols].reshape(k_tiles // UK, UK, P, UC).transpose(0, 2, 1, 3)
        got.append(v)
    return np.concatenate(got)


def lay_out(inputs):
    g = {k: np.asarray(v) for k, v in inputs.items()}
    pair = lambda base: [np.arange(base + UC * i, base + UC * (i + 1)) for i in range(1000)]
    q0, k0, v0, r0, lr0 = 0, 512, 1024, 2048, 3072
    aq0, ak0, lx0, y0, gate0 = 3104, 4128, 4640, 5664, 6688
    tile = lambda base, t: np.arange(base + P * t, base + P * (t + 1))
    weights, w_ada, w_gate, w_lr = [], [], [], []
    for l in range(DEPTH):
        w_in = g["w_in"][l]

        def branch(n):
            a = units(w_in, pair(gate0 + D_MODEL * n)[:4])
            b = units(g["w_branch"][l, n], pair(0)[:4])
            return np.stack([a.reshape(4, 2, P, UK, UC), b.reshape(4, 2, P, UK, UC)], 1).reshape(16, P, UK, UC)

        weights += [
            units(w_in, [np.concatenate([tile(q0, h), tile(k0, h)]) for h in range(HEADS)]),
            units(w_in, pair(v0)[:4]), units(w_in, pair(r0)[:4]), branch(0),
            units(w_in, pair(aq0)[:4]), units(w_in, pair(ak0)[:2]),
            units(w_in, pair(lx0)[:4]), branch(1), units(w_in, pair(y0)[:4]), branch(2), units(g["w_out"][l], pair(0)[:4]),
            units(g["ffn_w_up"][l], [np.concatenate([tile(0, t), tile(D_FF, t)]) for t in range(FT)]),
            units(g["ffn_w_down"][l], pair(0)[:4]),
        ]
        w_ada.append(g["w_ada"][l].reshape(ADA_SUM, AK, P, 6 * D_MODEL // AC, AC).transpose(3, 0, 2, 1, 4)
                     .reshape(ADA_UNITS, P, AK, AC))
        w_gate.append(g["lru_w_gates"][l].reshape(4, BLOCKS, P, P).transpose(1, 2, 0, 3))
        w_lr.append(w_in[:, lr0:lr0 + 2 * RANK].reshape(KT, P, 2 * RANK).transpose(1, 0, 2))
    cols = lambda v: v.reshape(-1, P).T
    pieces = lambda v: np.concatenate([cols(r) for r in v], 1)
    params = []
    for l in range(DEPTH):
        fw = g["ffn_conv_w"][l].reshape(3, 2, FT, P).transpose(0, 2, 1, 3).reshape(-1, P).T
        fb = g["ffn_conv_b"][l].reshape(2, FT, P).transpose(1, 0, 2).reshape(-1, P).T
        params.append(np.concatenate([
            cols(g["b_ada"][l]), pieces(g["norm_gains"][l]),
            g["gla_b_decay"][l].reshape(2, HEADS, P).transpose(1, 0, 2).reshape(-1, P).T,
            cols(g["gla_norm_g"][l]),
            np.stack([g["att_q_norm_g"][l]] * AQ + [g["att_k_norm_g"][l]] * AKV, 1),
            pieces(g["lru_conv_w"][l]), cols(g["lru_conv_b"][l]),
            g["lru_b_gates"][l].reshape(2, 2, BLOCKS, P).transpose(2, 0, 1, 3).reshape(-1, P).T,
            g["lru_lambda"][l].reshape(2, BLOCKS, P).transpose(1, 0, 2).reshape(-1, P).T,
            fw, fb], 1))
    stream = np.concatenate([g["ctx"][0], g["x"][0]]).T.reshape(KT, P, TOK).transpose(1, 0, 2)
    cvec = np.stack([g["c_ctx"], g["c"][0]], 1).reshape(KT, P, 2).transpose(1, 0, 2)
    axis_dim = HD // 2
    inv_freq = (1.0 / 10000.0 ** (np.arange(0, axis_dim, 2, dtype=np.float32) / np.float32(axis_dim))).astype(np.float32)
    t = np.arange(SEQ)
    ang = np.concatenate([np.outer(inv_freq, p.astype(np.float32)) for p in (t // GRID_W, t // GRID_W, t % GRID_W,
                                                                            t % GRID_W)])
    rope = np.stack([np.cos(ang), np.sin(ang)], 1).astype(np.float32)
    return {
        "xt": stream, "cvec": cvec, "weights": np.concatenate(weights), "w_ada": np.concatenate(w_ada),
        "w_gate": np.concatenate(w_gate),
        "w_lr": np.stack(w_lr), "w_dec": g["gla_w_decay"], "params": np.stack(params, 1), "rope": rope,
    }


def kernel(**inputs):
    import concourse.bacc as _bacc
    from concourse.bass_utils import run_bass_kernel_spmd as _run

    nc = _bacc.Bacc("TRN2", target_bir_lowering=False, num_devices=1)
    arrays, args = {}, []
    for name, a in lay_out(inputs).items():
        a = np.ascontiguousarray(a)
        arrays[f"in_{name}"] = a
        args.append(nc.dram_tensor(f"in_{name}", a.shape, mybir.dt.from_np(a.dtype), kind="ExternalInput").ap())
    args.append(nc.dram_tensor("out_x", (P, KT, SEQ), F32, kind="ExternalOutput").ap())
    build(nc, *args)
    r = _run(nc, [arrays], core_ids=[0])
    got = np.asarray(r.results[0]["out_x"])
    return np.ascontiguousarray(got.transpose(2, 1, 0)).reshape(1, SEQ, D_MODEL)
```
